# Optimizing a Trainium2 kernel written in Bass

```python
import math
import jax, jax.numpy as jnp
from jax import lax
import numpy as np

"""One inference step (DEPTH layers) of a hybrid chunk-causal streaming encoder.

Layer (post-norm with DeepNorm residual scaling):
  x <- LN1(ALPHA*x + W_out(g_ssm * S5(x) + g_attn * DSA(x)))   (parallel gated token mixers)
  x <- LN2(ALPHA*x + MoE(x))                                     (fine-grained sigmoid-routed MoE)

Inputs:
  x_prompt     (BATCH, SEQ, D_MODEL)          first SEQ frames of new streams, positions 0..SEQ-1
  x_sample     (DEC_BATCH, DEC_SEQ, D_MODEL)  next frames of running streams, positions PAST_LEN..PAST_LEN+DEC_SEQ-1
  cache_k      (DEPTH, DEC_BATCH, PAST_LEN, N_KV_HEADS, HEAD_DIM)  rotated attention keys
  cache_v      (DEPTH, DEC_BATCH, PAST_LEN, N_KV_HEADS, HEAD_DIM)  attention values
  cache_idx_k  (DEPTH, DEC_BATCH, PAST_LEN, IDX_DIM)               rotated indexer keys
  state_ssm_re (DEPTH, DEC_BATCH, N_GROUPS, N_STATE)  real part of S5 state
  state_ssm_im (DEPTH, DEC_BATCH, N_GROUPS, N_STATE)  imaginary part of S5 state
  followed by the layer weights (leading DEPTH axis).

Returns the tuple
  (y_prompt (BATCH, SEQ, D_MODEL), y_sample (DEC_BATCH, DEC_SEQ, D_MODEL),
   k_prompt (DEPTH, BATCH, SEQ, N_KV_HEADS, HEAD_DIM), v_prompt (same),
   idx_k_prompt (DEPTH, BATCH, SEQ, IDX_DIM),
   ssm_re_prompt (DEPTH, BATCH, N_GROUPS, N_STATE), ssm_im_prompt (same),
   k_sample (DEPTH, DEC_BATCH, DEC_SEQ, N_KV_HEADS, HEAD_DIM), v_sample (same),
   idx_k_sample (DEPTH, DEC_BATCH, DEC_SEQ, IDX_DIM),
   ssm_re_sample (DEPTH, DEC_BATCH, N_GROUPS, N_STATE), ssm_im_sample (same))
"""

D_MODEL = 1024
BATCH = 1
SEQ = 1024
DEPTH = 1
DEC_BATCH = 1
DEC_SEQ = 64
PAST_LEN = 2048

CHUNK = 64
D_SSM = 512
SSM_GROUP = 16
N_GROUPS = D_SSM // SSM_GROUP
N_STATE = 64
N_HEADS = 8
N_KV_HEADS = 2
HEAD_DIM = 64
D_ATTN = N_HEADS * HEAD_DIM
KV_GROUP = N_HEADS // N_KV_HEADS
ROPE_DIM = HEAD_DIM // 4
ROPE_THETA = 500000.0
IDX_HEADS = 8
IDX_DIM = 64
TOPK_KEYS = 256
Q_BLOCK = 64
N_EXPERTS = 64
MOE_TOPK = 6
D_EXPERT = 256
D_SHARED = 256
ROUTED_SCALE = 2.5
MOE_BLOCK = 128
LN_EPS = 1e-5
ALPHA = (2 * DEPTH) ** 0.25
BETA = (8 * DEPTH) ** -0.25
IN_WIDTHS = (D_SSM, D_ATTN, N_KV_HEADS * HEAD_DIM, N_KV_HEADS * HEAD_DIM,
             IDX_HEADS * IDX_DIM, IDX_DIM, IDX_HEADS, 2 * D_MODEL)
IN_SPLITS = tuple(int(s) for s in np.cumsum(IN_WIDTHS)[:-1])
D_IN = sum(IN_WIDTHS)

kernel_name = "hybrid_s5_dsa_moe_stream_step"

def layer_norm(x, g, b):
    xf = x.astype(jnp.float32)
    mu = xf.mean(-1, keepdims=True)
    var = jnp.square(xf - mu).mean(-1, keepdims=True)
    return ((xf - mu) * lax.rsqrt(var + LN_EPS) * g.astype(jnp.float32) + b.astype(jnp.float32)).astype(x.dtype)

def rope(x, pos):
    half = ROPE_DIM // 2
    inv_freq = ROPE_THETA ** (-jnp.arange(half, dtype=jnp.float32) * 2.0 / ROPE_DIM)
    ang = pos.astype(jnp.float32)[:, None] * inv_freq
    cos = jnp.cos(ang)[:, None, :]
    sin = jnp.sin(ang)[:, None, :]
    xr = x[..., :ROPE_DIM].astype(jnp.float32)
    x1, x2 = xr[..., :half], xr[..., half:]
    rot = jnp.concatenate([x1 * cos - x2 * sin, x1 * sin + x2 * cos], axis=-1).astype(x.dtype)
    return jnp.concatenate([rot, x[..., ROPE_DIM:]], axis=-1)

def s5_branch(u, h0, a_re, a_im, log_dt, b_re, b_im, c_re, c_im, d_skip, w_glu):
    B, L, _ = u.shape
    f32 = jnp.float32
    uf = u.astype(f32).reshape(B, L, N_GROUPS, SSM_GROUP)
    ar, ai = a_re.astype(f32), a_im.astype(f32)
    dt = jnp.exp(log_dt.astype(f32))[:, None]
    mag = jnp.exp(dt * ar)
    abar_re, abar_im = mag * jnp.cos(dt * ai), mag * jnp.sin(dt * ai)
    den = ar * ar + ai * ai
    num_re, num_im = abar_re - 1.0, abar_im
    coef_re = (num_re * ar + num_im * ai) / den
    coef_im = (num_im * ar - num_re * ai) / den
    br, bi = b_re.astype(f32), b_im.astype(f32)
    bbar_re = coef_re[..., None] * br - coef_im[..., None] * bi
    bbar_im = coef_re[..., None] * bi + coef_im[..., None] * br
    bu_re = jnp.einsum("blgc,gnc->blgn", uf, bbar_re)
    bu_im = jnp.einsum("blgc,gnc->blgn", uf, bbar_im)
    if h0 is not None:
        hr0, hi0 = h0[0].astype(f32), h0[1].astype(f32)
        bu_re = bu_re.at[:, 0].add(abar_re * hr0 - abar_im * hi0)
        bu_im = bu_im.at[:, 0].add(abar_re * hi0 + abar_im * hr0)
    a_seq_re = jnp.broadcast_to(abar_re, (1, L, N_GROUPS, N_STATE))
    a_seq_im = jnp.broadcast_to(abar_im, (1, L, N_GROUPS, N_STATE))

    def combine(e1, e2):
        a1r, a1i, b1r, b1i = e1
        a2r, a2i, b2r, b2i = e2
        return (a2r * a1r - a2i * a1i, a2r * a1i + a2i * a1r,
                a2r * b1r - a2i * b1i + b2r, a2r * b1i + a2i * b1r + b2i)

    _, _, h_re, h_im = lax.associative_scan(combine, (a_seq_re, a_seq_im, bu_re, bu_im), axis=1)
    y = (jnp.einsum("blgn,gcn->blgc", h_re, c_re.astype(f32))
         - jnp.einsum("blgn,gcn->blgc", h_im, c_im.astype(f32))
         + d_skip.astype(f32).reshape(N_GROUPS, SSM_GROUP) * uf)
    y = jax.nn.gelu(y.reshape(B, L, D_SSM)).astype(u.dtype)
    val, gate = jnp.split(jnp.einsum("ble,ed->bld", y, w_glu), 2, axis=-1)
    out = val * jax.nn.sigmoid(gate)
    return out, h_re[:, -1].astype(u.dtype), h_im[:, -1].astype(u.dtype)

def dsa_attention(q, iq, iw, k, v, ik, q_pos, k_pos):
    B, Lq = q.shape[:2]
    Lk = k.shape[1]
    n_sel = min(TOPK_KEYS, Lk // 4)
    qb = min(Q_BLOCK, Lq)
    nb = Lq // qb
    f32 = jnp.float32

    def to_blocks(a):
        return jnp.moveaxis(a.reshape(B, nb, qb, *a.shape[2:]), 1, 0)

    ikf = ik.astype(f32)
    k_chunk = k_pos // CHUNK

    def block(args):
        qblk, iqblk, iwblk, pblk = args
        q_chunk = pblk // CHUNK
        rel = jax.nn.relu(jnp.einsum("bqhd,bkd->bqhk", iqblk.astype(f32), ikf) * IDX_DIM ** -0.5)
        score = jnp.einsum("bqhk,bqh->bqk", rel, iwblk.astype(f32) * IDX_HEADS ** -0.5)
        visible = k_chunk[None, :] <= q_chunk[:, None]
        score = jnp.where(visible[None], score, -jnp.inf)
        _, sel = lax.top_k(score, n_sel)
        kg = jax.vmap(lambda kk, ii: kk[ii])(k, sel)
        vg = jax.vmap(lambda vv, ii: vv[ii])(v, sel)
        ok = k_chunk[sel] <= q_chunk[None, :, None]
        qg = qblk.reshape(B, qb, N_KV_HEADS, KV_GROUP, HEAD_DIM)
        logits = jnp.einsum("bqgrd,bqngd->bqgrn", qg, kg).astype(f32) * HEAD_DIM ** -0.5
        logits = jnp.where(ok[:, :, None, None, :], logits, -jnp.inf)
        prob = jax.nn.softmax(logits, axis=-1).astype(v.dtype)
        o = jnp.einsum("bqgrn,bqngd->bqgrd", prob, vg)
        return o.reshape(B, qb, D_ATTN)

    out = lax.map(block, (to_blocks(q), to_blocks(iq), to_blocks(iw), q_pos.reshape(nb, qb)))
    return jnp.moveaxis(out, 0, 1).reshape(B, Lq, D_ATTN)

def swiglu(x, w_gu, w_down):
    a, b = jnp.split(jnp.einsum("...d,df->...f", x, w_gu), 2, axis=-1)
    return jnp.einsum("...f,fd->...d", jax.nn.silu(a) * b, w_down)

def routed_experts(xt, idx, gate, w_exp_gu, w_exp_down):
    T, D = xt.shape
    S = T * MOE_TOPK
    n_blocks = -(-S // MOE_BLOCK) + N_EXPERTS
    R = n_blocks * MOE_BLOCK
    e_flat = idx.reshape(S)
    tok_flat = jnp.repeat(jnp.arange(T, dtype=jnp.int32), MOE_TOPK)
    g_flat = gate.reshape(S)
    order = jnp.argsort(e_flat)
    e_sorted = e_flat[order]
    counts = jnp.zeros((N_EXPERTS,), jnp.int32).at[e_flat].add(1)
    padded = (counts + MOE_BLOCK - 1) // MOE_BLOCK * MOE_BLOCK
    start = jnp.cumsum(counts) - counts
    pend = jnp.cumsum(padded)
    pstart = pend - padded
    dest = pstart[e_sorted] + (jnp.arange(S, dtype=jnp.int32) - start[e_sorted])
    row_tok = jnp.full((R,), T, jnp.int32).at[dest].set(tok_flat[order])
    row_gate = jnp.zeros((R,), gate.dtype).at[dest].set(g_flat[order])
    block_start = jnp.arange(n_blocks, dtype=jnp.int32) * MOE_BLOCK
    block_expert = jnp.minimum(jnp.searchsorted(pend, block_start, side="right"), N_EXPERTS - 1)
    x_pad = jnp.concatenate([xt, jnp.zeros((1, D), xt.dtype)], axis=0)

    def run_block(args):
        tok, g, e = args
        return swiglu(x_pad[tok], w_exp_gu[e], w_exp_down[e]) * g[:, None]

    out = lax.map(run_block, (row_tok.reshape(n_blocks, MOE_BLOCK),
                              row_gate.reshape(n_blocks, MOE_BLOCK), block_expert))
    return jnp.zeros((T + 1, D), xt.dtype).at[row_tok].add(out.reshape(R, D))[:T]

def moe(x, w_router, router_bias, w_exp_gu, w_exp_down, w_sh_gu, w_sh_down):
    B, L, D = x.shape
    xt = x.reshape(B * L, D)
    scores = jax.nn.sigmoid(jnp.einsum("td,de->te", xt.astype(jnp.float32), w_router.astype(jnp.float32)))
    _, idx = lax.top_k(scores + router_bias.astype(jnp.float32), MOE_TOPK)
    gate = jnp.take_along_axis(scores, idx, axis=-1)
    gate = gate / gate.sum(-1, keepdims=True) * ROUTED_SCALE
    routed = routed_experts(xt, idx, gate.astype(x.dtype), w_exp_gu, w_exp_down)
    shared = swiglu(xt, w_sh_gu, w_sh_down)
    return (routed + shared).reshape(B, L, D)

def layer(x, pos, past, p):
    (w_in, ssm_a_re, ssm_a_im, ssm_log_dt, ssm_b_re, ssm_b_im, ssm_c_re, ssm_c_im, ssm_d,
     w_glu, w_attn_proj, w_out, ln1_g, ln1_b, w_router, router_bias,
     w_exp_gu, w_exp_down, w_sh_gu, w_sh_down, ln2_g, ln2_b) = p
    B, L, _ = x.shape
    z = jnp.einsum("bld,de->ble", x, w_in)
    u, q, k, v, iq, ik, iw, gates = jnp.split(z, IN_SPLITS, axis=-1)
    q = rope(q.reshape(B, L, N_HEADS, HEAD_DIM), pos)
    k = rope(k.reshape(B, L, N_KV_HEADS, HEAD_DIM), pos)
    v = v.reshape(B, L, N_KV_HEADS, HEAD_DIM)
    iq = rope(iq.reshape(B, L, IDX_HEADS, IDX_DIM), pos)
    ik = rope(ik[:, :, None, :], pos)[:, :, 0, :]
    g_ssm, g_attn = jnp.split(jax.nn.sigmoid(gates), 2, axis=-1)
    if past is None:
        k_all, v_all, ik_all, h0 = k, v, ik, None
    else:
        ck, cv, cik, h_re0, h_im0 = past
        k_all = jnp.concatenate([ck, k], axis=1)
        v_all = jnp.concatenate([cv, v], axis=1)
        ik_all = jnp.concatenate([cik, ik], axis=1)
        h0 = (h_re0, h_im0)
    k_pos = jnp.arange(k_all.shape[1], dtype=jnp.int32)
    ssm_out, h_re, h_im = s5_branch(u, h0, ssm_a_re, ssm_a_im, ssm_log_dt, ssm_b_re, ssm_b_im,
                                    ssm_c_re, ssm_c_im, ssm_d, w_glu)
    attn = dsa_attention(q, iq, iw, k_all, v_all, ik_all, pos, k_pos)
    attn_out = jnp.einsum("ble,ed->bld", attn, w_attn_proj)
    mixed = jnp.einsum("ble,ed->bld", g_ssm * ssm_out + g_attn * attn_out, w_out)
    x = layer_norm(ALPHA * x + mixed, ln1_g, ln1_b)
    x = layer_norm(ALPHA * x + moe(x, w_router, router_bias, w_exp_gu, w_exp_down, w_sh_gu, w_sh_down),
                   ln2_g, ln2_b)
    return x, (k, v, ik, h_re, h_im)

def setup_inputs(seed: int = 0) -> dict:
    key = jax.random.key(seed)
    ks = iter(jax.random.split(key, 40))
    f32 = jnp.float32

    def nrm(shape, scale):
        return jax.random.normal(next(ks), shape, f32) * scale

    Dd = DEPTH
    return {
        "x_prompt": nrm((BATCH, SEQ, D_MODEL), 1.0),
        "x_sample": nrm((DEC_BATCH, DEC_SEQ, D_MODEL), 1.0),
        "cache_k": nrm((Dd, DEC_BATCH, PAST_LEN, N_KV_HEADS, HEAD_DIM), 1.0),
        "cache_v": nrm((Dd, DEC_BATCH, PAST_LEN, N_KV_HEADS, HEAD_DIM), 1.0),
        "cache_idx_k": nrm((Dd, DEC_BATCH, PAST_LEN, IDX_DIM), 1.0),
        "state_ssm_re": nrm((Dd, DEC_BATCH, N_GROUPS, N_STATE), 0.1),
        "state_ssm_im": nrm((Dd, DEC_BATCH, N_GROUPS, N_STATE), 0.1),
        "w_in": nrm((Dd, D_MODEL, D_IN), D_MODEL ** -0.5),
        "ssm_a_re": -0.5 + nrm((Dd, N_GROUPS, N_STATE), 0.01),
        "ssm_a_im": jnp.pi * jnp.arange(N_STATE, dtype=f32) + nrm((Dd, N_GROUPS, N_STATE), 0.01),
        "ssm_log_dt": jax.random.uniform(next(ks), (Dd, N_GROUPS), f32,
                                         minval=math.log(1e-3), maxval=math.log(1e-1)),
        "ssm_b_re": nrm((Dd, N_GROUPS, N_STATE, SSM_GROUP), (2 * SSM_GROUP) ** -0.5),
        "ssm_b_im": nrm((Dd, N_GROUPS, N_STATE, SSM_GROUP), (2 * SSM_GROUP) ** -0.5),
        "ssm_c_re": nrm((Dd, N_GROUPS, SSM_GROUP, N_STATE), N_STATE ** -0.5),
        "ssm_c_im": nrm((Dd, N_GROUPS, SSM_GROUP, N_STATE), N_STATE ** -0.5),
        "ssm_d": nrm((Dd, D_SSM), 1.0),
        "w_glu": nrm((Dd, D_SSM, 2 * D_MODEL), D_SSM ** -0.5),
        "w_attn_proj": nrm((Dd, D_ATTN, D_MODEL), D_ATTN ** -0.5),
        "w_out": nrm((Dd, D_MODEL, D_MODEL), BETA * D_MODEL ** -0.5),
        "ln1_g": 1.0 + nrm((Dd, D_MODEL), 0.02),
        "ln1_b": nrm((Dd, D_MODEL), 0.02),
        "w_router": nrm((Dd, D_MODEL, N_EXPERTS), D_MODEL ** -0.5),
        "router_bias": nrm((Dd, N_EXPERTS), 0.01),
        "w_exp_gu": nrm((Dd, N_EXPERTS, D_MODEL, 2 * D_EXPERT), D_MODEL ** -0.5),
        "w_exp_down": nrm((Dd, N_EXPERTS, D_EXPERT, D_MODEL), BETA * D_EXPERT ** -0.5),
        "w_sh_gu": nrm((Dd, D_MODEL, 2 * D_SHARED), D_MODEL ** -0.5),
        "w_sh_down": nrm((Dd, D_SHARED, D_MODEL), BETA * D_SHARED ** -0.5),
        "ln2_g": 1.0 + nrm((Dd, D_MODEL), 0.02),
        "ln2_b": nrm((Dd, D_MODEL), 0.02),
    }

def reference(x_prompt, x_sample, cache_k, cache_v, cache_idx_k, state_ssm_re, state_ssm_im,
              w_in, ssm_a_re, ssm_a_im, ssm_log_dt, ssm_b_re, ssm_b_im, ssm_c_re, ssm_c_im, ssm_d,
              w_glu, w_attn_proj, w_out, ln1_g, ln1_b, w_router, router_bias,
              w_exp_gu, w_exp_down, w_sh_gu, w_sh_down, ln2_g, ln2_b):
    weights = (w_in, ssm_a_re, ssm_a_im, ssm_log_dt, ssm_b_re, ssm_b_im, ssm_c_re, ssm_c_im, ssm_d,
               w_glu, w_attn_proj, w_out, ln1_g, ln1_b, w_router, router_bias,
               w_exp_gu, w_exp_down, w_sh_gu, w_sh_down, ln2_g, ln2_b)
    past_len = cache_k.shape[2]
    pos_prompt = jnp.arange(x_prompt.shape[1], dtype=jnp.int32)
    pos_sample = past_len + jnp.arange(x_sample.shape[1], dtype=jnp.int32)
    y_p, y_s = x_prompt, x_sample
    new_p, new_s = [], []
    for l in range(DEPTH):
        p_l = tuple(w[l] for w in weights)
        y_p, st_p = layer(y_p, pos_prompt, None, p_l)
        y_s, st_s = layer(y_s, pos_sample,
                          (cache_k[l], cache_v[l], cache_idx_k[l], state_ssm_re[l], state_ssm_im[l]), p_l)
        new_p.append(st_p)
        new_s.append(st_s)
    k_p, v_p, ik_p, hre_p, him_p = [jnp.stack(a) for a in zip(*new_p)]
    k_s, v_s, ik_s, hre_s, him_s = [jnp.stack(a) for a in zip(*new_s)]
    return (y_p, y_s, k_p, v_p, ik_p, hre_p, him_p, k_s, v_s, ik_s, hre_s, him_s)


_drawn_inputs = setup_inputs


def setup_inputs(seed=0):
    import zlib

    import numpy as np

    out = dict(_drawn_inputs(seed))
    spreads = {}
    factors = {'ssm_a_re': 49.281, 'ln2_g': 29.928, 'ln2_b': 26.406, 'ssm_c_re': 2.751, 'ssm_c_im': 3.075}
    for name, (base, spread) in spreads.items():
        noise = np.random.default_rng([zlib.crc32(name.encode()), seed]).standard_normal(out[name].shape)
        drawn = base * np.exp(spread * noise) if base else spread * noise
        out[name] = __import__('jax').numpy.asarray(drawn.astype(out[name].dtype))
    for name, factor in factors.items():
        out[name] = (out[name] * factor).astype(out[name].dtype)
    return out
```

```python
from contextlib import ExitStack

import numpy as np

import concourse.bass as bass
from concourse import mybir

F32, I32, U32 = mybir.dt.float32, mybir.dt.int32, mybir.dt.uint32
ALU, ACT, AX = mybir.AluOpType, mybir.ActivationFunctionType, mybir.AxisListType

P = 128
DM = 1024
SEQ, DEC, PAST = 1024, 64, 2048
T = SEQ + DEC
NT = 9
DK = DM // P
HD, NH, NKV = 64, 8, 2
DS, GC, NG, NS = 512, 16, 32, 64
GP = NG // 2
BL = 8
NJ, NJS = SEQ // BL, DEC // BL
UC = NJ + 1 + NJS
HC = UC + 1
TOPK = 256
NE, MK, DE = 64, 6, 256
EPS = 1e-5
ALPHA = 2.0 ** 0.25
ROUTED_SCALE = 2.5
HID = -1e30
TAKEN = -3e38
KEYS = SEQ + PAST + DEC
NB_MAX = (T * MK) // P + NE
NBP = NB_MAX + 2
TWO_PI = 6.283185307179586
ROUND = 12582912.0


def rows(i):
    return P if i < NT - 1 else DEC


def tok(i):
    return slice(i * P, i * P + rows(i))


def keys(i):
    return (0, P * (i + 1)) if i < NT - 1 else (SEQ, PAST + DEC)


def split(n, m):
    return [(a, min(m, n - a)) for a in range(0, n, m)]


MASK_AT = [sum(keys(j)[1] for j in range(i)) for i in range(NT)]
MASK_W = sum(keys(j)[1] for j in range(NT))
TOK_CHUNKS = [(0, 384), (384, 384), (768, 320)]
CHOOSING = list(range(2, NT))


class Banks:

    def __init__(self):
        self.fills, self.turn, self.at, self.counts, self.reader = [0] * 8, {}, {}, {}, [None] * 8

    def take(self, key, reader, pool, n, value, signals):
        t = (self.turn.get(pool, 0) + n - 1) // n * n % len(pool)
        self.turn[pool] = t + n
        first = pool[t]
        before = [self.reader[b] for b in range(first, first + n)]
        self.at[key] = (first, self.fills[first:first + n])
        if value is None:
            value = self.counts[reader] = self.counts.get(reader, 0) + 1
        for b in range(first, first + n):
            self.reader[b] = (reader, value)
            self.fills[b] += signals
        return first, before


def layer_program(nc, a, out):
    banks = Banks()
    with ExitStack() as ctx:
        def sb(name, shape, dt=F32):
            return ctx.enter_context(nc.sbuf_tensor(name, shape, dt))

        def sem(name):
            return ctx.enter_context(nc.semaphore(name))

        def dram(name, shape, dt=F32):
            return nc.dram_tensor(name, shape, dt, kind="Internal").ap()

        kpad_d = dram("kpad_d", (NG, GC, 15 * GC))
        x1_d = dram("x1_d", (T, DM))
        base_d = dram("base_d", (T, DM))
        slots_d = dram("slots_d", (NBP * P, DM))
        blk_d = dram("blk_d", (P, 1), I32)

        psum = ctx.enter_context(nc.psum_tensor("psum", [P, 8, 512], F32))

        arena = sb("arena", [P, 49792])

        def at(off, *shape):
            n = int(np.prod(shape))
            v = arena[:, off:off + n]
            if len(shape) == 1:
                return v
            names = "abcde"[:len(shape)]
            return v.rearrange(f"p ({' '.join(names)}) -> p {' '.join(names)}",
                               **{c: s for c, s in zip(names[1:], shape[1:])})

        xT = at(0, DK, T)
        x1T = xT
        mk = at(8704, MASK_W)
        t1, t2 = at(8704, 2304), at(8704 + 2304, 2304)
        braw, bbar, craw = at(8704 + 4608, 2, GP, GC), at(8704 + 5120, 2, GP, GC), at(8704 + 5632, 2, GP, GC)
        g1 = at(15424, DK, T)
        w_u = at(15424, DK, DS)
        m_op = at(15424, NG, P)
        ca = at(15424 + 4096, 2, GP, 9, GC)
        R = 24128
        uT = at(R, NG, UC)
        hp = at(R + 4384, HC, 2, GP)
        u2 = at(32928, NG, BL, GC)
        u2s = at(37024, NG, BL, GC)
        ba = at(41120, 2, GP, BL, GC)
        bopT = at(45216, 2, GP, P)
        xin = at(45216, 2, DM)
        kpad = at(41120, NG, 15, GC)[0:GC]
        cst = at(14848, 2, 2, P)
        u64 = at(32000, DS)
        w_i = at(32928, DK, 584)
        iqT = at(37600, 4, T - 2 * P)
        ikT = at(40928, KEYS)
        zi = at(44064, 2, 640)
        rel = at(45344, 4, 512)
        cikd = at(47392, 16, P)
        rtmp = at(49440, 4, 10, 8)
        y2 = at(32928, BL, DS)
        y2s = at(37024, BL, DS)
        yT = at(41120, 4, T)
        y64 = at(45472, DS)
        wgs = at(R, 2, 16, P)
        sg = at(R + 4096, 4, 384)
        w_q = at(34816, DK, 768)
        qT = at(41088, 4, T)
        zq = at(45440, 2, 768)
        kT = at(R, NKV, KEYS)
        v_tm = at(30400, 25, P)
        kdup = at(33600, 2, 256)
        ckd = at(46976, 4, 256)
        pr = at(34816, 2, PAST + DEC)
        pT = at(39040, 2, 512)
        diag = at(40064, 2, P)
        zeros = at(40320, 512)
        aT = at(45440, 4, T)
        wap = at(8704, 2, 12, P)
        sga = at(8704 + 3072, 4, 384)
        w_o = at(R, DK, DM)
        xre = at(47104, 2, DM)
        ln1 = at(40960, 2, DM)
        x1b = at(43008, 3, DM)
        w_sg = at(8704, DK, 2 * DE)
        w_sd = at(32320, 2, DM)
        w_r = at(12800, DK, NE)
        hsh = at(13312, 2, DE)
        hst = at(48000, 4, P)
        gcol = sb("gcol", [P, 2])
        sb64 = sb("sb64", [P, NE])
        gsum = sb("gsum", [P, 2])
        hshT = at(13824, 2, DE)
        rk = at(14336, NT, NE)
        cnt = at(14912, 4, NE)
        oh = at(49152, MK, NE)
        oh2 = at(34368, MK, NE)
        ewg = [at(34816, DK, 2 * DE), at(40960, DK, 2 * DE)]
        ewd = [at(34816 + 4096, 2, DM), at(40960 + 4096, 2, DM)]
        xg = [at(0, DM), at(1024, DM)]
        xgT = [at(2048, DK, P), at(3072, DK, P)]
        yb = [at(4096, DM), at(5120, DM)]
        eh = at(6144, 4, DE)
        ehT = [at(7168, 2, P), at(7424, 2, P)]
        onehot = at(15424, 2, 2 * P + 2 * P)
        part = at(15424, 8, DM)
        bas = at(8704, 2, DM)
        ln2 = at(10752, 2, DM)

        ident = sb("ident", [P, P])
        tri = sb("tri", [P, P])
        ones = sb("ones", [P, P])
        iota64 = sb("iota64", [P, P])
        rope = sb("rope", [P, NT, 2, 8])
        pst = sb("pst", [P, P])
        ldt = sb("ldt", [P, 2])
        carry = sb("carry", [1, 1])
        par = sb("par", [P, 5, GP])
        sm = sb("sm", [P, 16, GP])
        pw = sb("pw", [P, 2, 9, GP])
        a8 = sb("a8", [P, 2, 2, GP])
        sct = sb("sct", [P, 2, 2, GP])
        dsk = sb("dsk", [GC, NG])
        iws = sb("iws", [P, NT, 8])
        best = sb("best", [P, 8])
        mx = sb("mx", [P, 2, 4])
        nbias = sb("nbias", [P, 2])
        rsum = sb("rsum", [P, 2])
        rinv = sb("rinv", [P, 2])
        stats = sb("stats", [P, 2, 6])
        mv = sb("mv", [P, 2])
        lst = sb("lst", [P, 4])
        rsc = sb("rsc", [P, 2, NE])
        rbias = sb("rbias", [P, NE])
        v8 = sb("v8", [P, 8])
        i8 = sb("i8", [P, 8], U32)
        idx = sb("idx", [P, NT, 8])
        gate = sb("gate", [P, NT, 8])
        sel = sb("sel", [P, 2, NE])
        cum = sb("cum", [P, NE])
        slot = sb("slot", [P, NT, 8])
        slot_i = sb("slot_i", [P, NT, 8], I32)
        sblk = sb("sblk", [P, NT, 8])
        sin_ = sb("sin_", [P, NT, 8])
        tokid = sb("tokid", [P, NT])
        tab = sb("tab", [P, 2, NBP])
        tid = [sb(f"tid{u}", [P, 1], I32) for u in range(2)]
        bexp = sb("bexp", [P, 4])
        bexp_i = sb("bexp_i", [P, 1], I32)
        brow = sb("brow", [1, P], I32)
        npair = sb("npair", [1, 8])
        npair_i = sb("npair_i", [1, 8], I32)

        full = [sem(f"bank_full{b}") for b in range(8)]
        dve_step = sem("dve_step")
        pool_step = sem("pool_step")
        S = {}

        def s(name):
            if name not in S:
                S[name] = sem(name)
            return S[name]

        def bank(key, j=0):
            f, c = banks.at[key]
            return psum[:, f + j, :]

        def await_bank(eng, key, j=0):
            f, c = banks.at[key]
            eng.wait_ge(full[f + j], c[j] + 1)

        block = ctx.enter_context(nc.Block())
        score_keys = lambda i: [(i, a0, n0) for a0, n0 in split(keys(i)[1], 512)]
        ATT = [(i, h) for i in range(NT) for h in range(NH)]
        key_tiles = lambda i: split(keys(i)[1], P)
        key_groups = lambda i: split(len(key_tiles(i)), 4)
        group_no = {}
        for n, (i, h) in enumerate(ATT):
            for q in range(len(key_groups(i))):
                group_no[n, q] = len(group_no)
        MASKINGS = sum(len(split(keys(i)[1], 1024)) for i, h in ATT)
        score_no = {}
        for i in CHOOSING:
            for _, c0, w in score_keys(i):
                for h in range(NH):
                    score_no[i, c0, h] = len(score_no)

        @block.tensor
        def _(pe):
            def claim(key, reader, value=None, pool=tuple(range(8)), n=1, signals=1):
                first, before = banks.take(key, reader, pool, n, value, signals)
                for name, v in {b for b in before if b}:
                    pe.wait_ge(s(name), v)
                return first

            def filled(ins, key, j=0):
                ins.then_inc(full[banks.at[key][0] + j], 1)

            mm, tr = pe.matmul, pe.transpose

            pe.wait_ge(s("constants"), 8)
            for i in range(NT):
                r = rows(i)
                pe.wait_ge(s(f"x_loaded{i % 2}"), 16 * (i // 2 + 1))
                for half in range(2):
                    b = claim(("x", i, half), "xT_ready")
                    for q in range(4):
                        k = 4 * half + q
                        last = tr(psum[:, b, q * P:q * P + r], xin[0:r, i % 2, k::DK], ident[0:r, 0:r])
                    filled(last, ("x", i, half))
            pe.wait_ge(s("param_rows"), 1)
            b = claim("par", "par_ready")
            filled(tr(psum[:, b, 0:80], pst[0:80, :], ident[0:80, 0:80]), "par")
            pe.wait_ge(s("xT_ready"), 2 * NT)
            pe.wait_ge(s("w_u_loaded"), 16)
            for t in range(BL):
                b = claim(("u", t), "u2_ready")
                for k in range(DK):
                    last = mm(psum[:, b, :], xT[:, k, t:SEQ:BL], w_u[:, k, :], start=k == 0, stop=k == DK - 1)
                filled(last, ("u", t))
            b = claim("u_s", "u64_ready")
            for k in range(DK):
                last = mm(psum[0:DEC, b, :], xT[:, k, SEQ:T], w_u[:, k, :], start=k == 0, stop=k == DK - 1)
            filled(last, "u_s")
            pe.wait_ge(s("c_loaded"), 16 * 8)
            b = claim("c", "c_turned")
            for part_ in range(2):
                for e in range(2):
                    last = tr(psum[:, b, (2 * part_ + e) * P:(2 * part_ + e + 1) * P], cst[:, part_, e, :], ident[:])
            filled(last, "c")
            pe.wait_ge(s("u2_ready"), BL)
            for q4 in range(8):
                b = claim(("ut", q4), "uT_ready")
                for q in range(4):
                    g = 4 * q4 + q
                    last = tr(psum[:, b, q * P:(q + 1) * P], u2[:, g, :, :].rearrange("p t c -> p (t c)"), ident[:])
                filled(last, ("ut", q4))
            pe.wait_ge(s("u2s_ready"), 16 * NJS)
            b = claim("uts", "uT_ready")
            for g in range(NG):
                last = tr(psum[:, b, g * NJS:(g + 1) * NJS],
                          u2s[0:NJS, g, :, :].rearrange("p t c -> p (t c)"), ident[0:NJS, 0:NJS])
            filled(last, "uts")
            pe.wait_ge(s("s5_operators"), 2)
            for q4 in range(8):
                b = claim(("bt", q4), "bopT_ready")
                for q in range(4):
                    n = 4 * q4 + q
                    last = tr(psum[:, b, q * P:(q + 1) * P],
                              ba[:, n // GP, n % GP, :, :].rearrange("p t c -> p (t c)"), ident[:])
                filled(last, ("bt", q4))
            pe.wait_ge(s("uT_ready"), 9)
            pe.wait_ge(s("bopT_ready"), 8)
            for gp in range(GP):
                b = claim(("b", gp), "b_ready")
                for part_ in range(2):
                    for e in range(2):
                        last = mm(psum[e * 64:(e + 1) * 64, b, part_ * UC:(part_ + 1) * UC],
                                  bopT[:, part_, gp, e * 64:(e + 1) * 64], uT[:, 2 * gp + e, :],
                                  start=True, stop=True)
                filled(last, ("b", gp))
            pe.wait_ge(s("s5_operators"), 3)
            for q4 in range(4):
                for e in range(2):
                    claim(("k", q4, e), "k_ready")
                for q in range(4):
                    for e in range(2):
                        b, _ = banks.at["k", q4, e]
                        for part_ in range(2):
                            last = mm(psum[0:GC, b, q * P:(q + 1) * P], bbar[e * 64:(e + 1) * 64, part_, 4 * q4 + q, :],
                                      ca[e * 64:(e + 1) * 64, part_, 4 * q4 + q, 0:BL, :].rearrange("p t c -> p (t c)"),
                                      start=part_ == 0, stop=part_ == 1)
                        if q == 3:
                            filled(last, ("k", q4, e))

            def z_index(i):
                r = rows(i)
                if i == 0:
                    pe.wait_ge(s("w_i_loaded"), 16)
                for key, c0, n in (("iq", 0, 512), ("ik", 512, 72)):
                    b = claim((key, i), "zi_ready", i + 1)
                    for k in range(DK):
                        last = mm(psum[0:r, b, 0:n], xT[:, k, tok(i)], w_i[:, k, c0:c0 + n],
                                  start=k == 0, stop=k == DK - 1)
                    filled(last, (key, i))

            def turn_index(i):
                r = rows(i)
                pe.wait_ge(s("zi_roped"), i + 1)
                b = claim(("ikT", i), "ikT_ready")
                filled(tr(psum[:, b, 0:r], zi[0:r, i % 2, 512:640], ident[0:r, 0:r]), ("ikT", i))
                if i in CHOOSING:
                    b = claim(("iqT", i), "iqT_ready")
                    for q in range(4):
                        last = tr(psum[:, b, q * P:q * P + r], zi[0:r, i % 2, q * P:(q + 1) * P], ident[0:r, 0:r])
                    filled(last, ("iqT", i))

            def scores(i):
                r = rows(i)
                pe.wait_ge(s("ikT_ready"), i + 1)
                if i == NT - 1:
                    pe.wait_ge(s("cik_ready"), 4)
                pe.wait_ge(s("iqT_ready"), i - 1)
                for _, c0, n in score_keys(i):
                    for h in range(NH):
                        b = claim(("s", i, c0, h), "rel_ready")
                        e = h % 2
                        filled(mm(psum[0:r, b, 0:n],
                                  iqT[e * 64:(e + 1) * 64, h // 2, (i - 2) * P:(i - 2) * P + r],
                                  ikT[e * 64:(e + 1) * 64, keys(i)[0] + c0:keys(i)[0] + c0 + n],
                                  start=True, stop=True), ("s", i, c0, h))

            for i in range(NT):
                z_index(i)
                if i > 0:
                    turn_index(i - 1)
                    if i - 1 in CHOOSING:
                        scores(i - 1)
                if i == 7:
                    pe.wait_ge(s("cik_loaded"), 32)
                    for q4 in range(4):
                        b = claim(("cik", q4), "cik_ready")
                        for q in range(4):
                            last = tr(psum[:, b, q * P:(q + 1) * P], cikd[:, 4 * q4 + q, :], ident[:])
                        filled(last, ("cik", q4))
            turn_index(NT - 1)
            scores(NT - 1)

            pe.wait_ge(s("m_loaded"), 16 * BL)
            pe.wait_ge(s("state_ready"), 1)
            for sample in range(2):
                r, j0 = (NJS, NJ + 1) if sample else (NJ, 0)
                for q4 in range(4):
                    for e in range(2):
                        claim(("y", sample, q4, e), "y2s_ready" if sample else "y_ready")
                    for q in range(4):
                        gp = 4 * q4 + q
                        o = [psum[0:r, banks.at["y", sample, q4, e][0], q * P:(q + 1) * P] for e in range(2)]
                        for e in range(2):
                            mm(o[e], uT[:, 2 * gp + e, j0:j0 + r], m_op[:, 2 * gp + e, :], start=True, stop=False)
                        for part_ in range(2):
                            for e in range(2):
                                last = mm(o[e], hp[e * 64:(e + 1) * 64, j0:j0 + r, part_, gp],
                                          ca[e * 64:(e + 1) * 64, part_, gp, 1:9, :].rearrange("p t c -> p (t c)"),
                                          start=False, stop=part_ == 1)
                                if q == 3 and part_ == 1:
                                    filled(last, ("y", sample, q4, e))
            pe.wait_ge(s("y_ready"), 8)
            b = claim("hst", "states_ready")
            for q in range(4):
                last = tr(psum[0:GP, b, q * P:(q + 1) * P], hp[:, (NJ, HC - 1)[q // 2], q % 2, :], ident[:])
            filled(last, "hst")
            for t in range(BL):
                b = claim(("yt", t), "yT_ready")
                for q in range(4):
                    last = tr(psum[:, b, q * P:(q + 1) * P], y2[:, t, q * P:(q + 1) * P], ident[:])
                filled(last, ("yt", t))
            pe.wait_ge(s("y64_ready"), 16 * NJS)
            b = claim("yts", "yT_ready")
            for q in range(4):
                last = tr(psum[:, b, q * DEC:(q + 1) * DEC], y64[0:DEC, q * P:(q + 1) * P], ident[0:DEC, 0:DEC])
            filled(last, "yts")

            pe.wait_ge(s("yT_ready"), 9)
            for d in range(DK):
                pe.wait_ge(s(f"wgs_loaded{d % 2}"), 48 * (d // 2 + 1))
                for c, (t0, n) in enumerate(TOK_CHUNKS):
                    for key, w0, src, nk in (("val", 8, yT, 4), ("glu", 12, yT, 4), ("gs", 0, xT, DK)):
                        b = claim((key, d, c), "val_used" if key == "val" else "sg_ready")
                        for k in range(nk):
                            last = mm(psum[:, b, 0:n], wgs[:, d % 2, w0 + k, :], src[:, k, t0:t0 + n],
                                      start=k == 0, stop=k == nk - 1)
                        filled(last, (key, d, c))

            def z_qkv(i):
                r = rows(i)
                if i == 0:
                    pe.wait_ge(s("w_q_loaded"), 16)
                for key, c0, n in (("q", 0, 512), ("kv", 512, 256)):
                    b = claim((key, i), "zq_ready", i + 1)
                    for k in range(DK):
                        last = mm(psum[0:r, b, 0:n], xT[:, k, tok(i)], w_q[:, k, c0:c0 + n],
                                  start=k == 0, stop=k == DK - 1)
                    filled(last, (key, i))

            def turn_qkv(i):
                r = rows(i)
                pe.wait_ge(s("zq_roped"), i + 1)
                b = claim(("qT", i), "qT_ready")
                for q in range(4):
                    last = tr(psum[:, b, q * P:q * P + r], zq[0:r, i % 2, q * P:(q + 1) * P], ident[0:r, 0:r])
                filled(last, ("qT", i))
                b = claim(("kT", i), "qT_ready")
                for q in range(2):
                    last = tr(psum[:, b, q * P:q * P + r], kdup[0:r, i % 2, q * P:(q + 1) * P], ident[0:r, 0:r])
                filled(last, ("kT", i))

            for i in range(NT):
                z_qkv(i)
                if i > 0:
                    turn_qkv(i - 1)
            turn_qkv(NT - 1)
            for j in range(16):
                pe.wait_ge(s(f"ck_loaded{j % 4}"), 32 * (j // 4 + 1))
                b = claim(("ck", j), "ckT_ready")
                for q in range(2):
                    last = tr(psum[:, b, q * P:(q + 1) * P], ckd[:, j % 4, q * P:(q + 1) * P], ident[:])
                filled(last, ("ck", j))

            LOGITS, TURNED, OUTS = (0, 1, 2, 3), (4, 5), (6, 7)

            def logits(n):
                i, h = ATT[n]
                r, e = rows(i), h % 2
                if n == 0:
                    pe.wait_ge(s("qT_ready"), 2 * NT)
                    pe.wait_ge(s("ckT_ready"), 16)
                    pe.wait_ge(s("cv_loaded"), 16)
                for c0, w in split(keys(i)[1], 1024):
                    claim(("l", n, c0), "masked", pool=LOGITS, n=len(split(w, 512)))
                    for j, (a0, m) in enumerate(split(w, 512)):
                        b = banks.at[("l", n, c0)][0] + j
                        k0 = keys(i)[0] + c0 + a0
                        filled(mm(psum[0:r, b, 0:m], qT[e * 64:(e + 1) * 64, h // 2, tok(i)],
                                  kT[e * 64:(e + 1) * 64, h // 4, k0:k0 + m], start=True, stop=True), ("l", n, c0), j)

            def attend(n):
                i, h = ATT[n]
                r, e, nk = rows(i), h % 2, keys(i)[1]
                tiles = split(nk, P)
                groups = split(len(tiles), 4)
                if h == 0:
                    claim(("o", i), "aT_ready", pool=OUTS, signals=0)
                o = psum[e * 64:(e + 1) * 64, banks.at[("o", i)][0], (h // 2) * P:(h // 2) * P + r]
                pe.wait_ge(s("diag_ready"), n + 1)

                def values(q):
                    gq = group_no[n, q]
                    pe.wait_ge(s("pT_ready"), gq + 1)
                    for c in range(groups[q][1]):
                        k0, w = tiles[groups[q][0] + c]
                        v0 = k0 // P + (8 if i == NT - 1 else 0)
                        last = mm(o, v_tm[0:w, v0, (h // 4) * HD:(h // 4 + 1) * HD],
                                  pT[0:w, gq % 2, c * P:c * P + r], start=k0 == 0, stop=k0 + w == nk)
                    last.then_inc(s("pT_used"), 1)

                for q, (g0, gn) in enumerate(groups):
                    b = claim(("p", n, q), "pT_ready", pool=TURNED)
                    for c in range(gn):
                        k0, w = tiles[g0 + c]
                        last = mm(psum[0:w, b, c * P:c * P + r], pr[0:r, n % 2, k0:k0 + w], diag[0:r, n % 2, 0:r],
                                  start=True, stop=True)
                    filled(last, ("p", n, q))
                    if q > 0:
                        values(q - 1)
                values(len(groups) - 1)

            logits(0)
            for n in range(len(ATT)):
                if n + 1 < len(ATT):
                    logits(n + 1)
                attend(n)

            pe.wait_ge(s("aT_ready"), NT)
            for d in range(DK):
                pe.wait_ge(s(f"wap_loaded{d % 2}"), 32 * (d // 2 + 1))
                for c, (t0, n) in enumerate(TOK_CHUNKS):
                    for key, w0, src, nk in (("ga", 0, xT, DK), ("ao", 8, aT, 4)):
                        b = claim((key, d, c), "sga_ready" if key == "ga" else "ao_used")
                        for k in range(nk):
                            last = mm(psum[:, b, 0:n], wap[:, d % 2, w0 + k, :], src[:, k, t0:t0 + n],
                                      start=k == 0, stop=k == nk - 1)
                        filled(last, (key, d, c))

            def project(i):
                r = rows(i)
                claim(("wo", i), "res_ready", n=2)
                for j in range(2):
                    for k in range(DK):
                        last = mm(psum[0:r, banks.at[("wo", i)][0] + j, :], g1[:, k, tok(i)],
                                  w_o[:, k, j * 512:(j + 1) * 512], start=k == 0, stop=k == DK - 1)
                    filled(last, ("wo", i), j)

            def turn_x1(i):
                r = rows(i)
                pe.wait_ge(s("x1_ready"), i + 1)
                for half in range(2):
                    b = claim(("x1", i, half), "x1T_ready")
                    for q in range(4):
                        last = tr(psum[:, b, q * P:q * P + r], x1b[0:r, i % 3, 4 * half + q::DK], ident[0:r, 0:r])
                    filled(last, ("x1", i, half))

            def route_and_share(i):
                r = rows(i)
                pe.wait_ge(s("x1T_ready"), 2 * (i + 1))
                if i == 0:
                    pe.wait_ge(s("w_s_loaded"), 64)
                for key, w, n in (("r", w_r, NE), ("sg", w_sg, 2 * DE)):
                    b = claim((key, i), "rsc_ready" if key == "r" else "hsh_ready")
                    for k in range(DK):
                        last = mm(psum[0:r, b, 0:n], x1T[:, k, tok(i)], w[:, k, :], start=k == 0, stop=k == DK - 1)
                    filled(last, (key, i))

            def rank_and_share(i):
                r = rows(i)
                pe.wait_ge(s("hsh_ready"), i + 1)
                b = claim(("ht", i), "hshT_ready")
                for k in range(2):
                    last = tr(psum[:, b, k * P:k * P + r], hsh[0:r, i % 2, k::2], ident[0:r, 0:r])
                filled(last, ("ht", i))
                pe.wait_ge(s("sel_ready"), i + 1)
                b = claim(("rk", i), "rk_ready")
                if i > 0:
                    pe.wait_ge(s("cum_ready"), i)
                    mm(psum[0:r, b, 0:NE], ones[:, 0:r], cum[:], start=True, stop=False)
                filled(mm(psum[0:r, b, 0:NE], tri[0:r, 0:r], sel[0:r, i % 2, :], start=i == 0, stop=True), ("rk", i))
                pe.wait_ge(s("hshT_ready"), i + 1)
                claim(("sd", i), "base_ready", n=2)
                for j in range(2):
                    for k in range(2):
                        last = mm(psum[0:r, banks.at[("sd", i)][0] + j, :], hshT[:, i % 2, k * P:k * P + r],
                                  w_sd[:, k, j * 512:(j + 1) * 512], start=k == 0, stop=k == 1)
                    filled(last, ("sd", i), j)

            pe.wait_ge(s("mixed_ready"), DK * 3)
            pe.wait_ge(s("w_o_loaded"), 16)
            for i in range(NT + 2):
                if i < NT:
                    project(i)
                if 0 <= i - 1 < NT:
                    turn_x1(i - 1)
                    route_and_share(i - 1)
                if 0 <= i - 2 < NT:
                    rank_and_share(i - 2)
            pe.wait_ge(s("cum_ready"), NT)
            b = claim("cnt", "blocks_planned", 1)
            filled(mm(psum[:, b, 0:NE], ones[:], cum[:], start=True, stop=True), "cnt")
            b = claim("tab", "tab_ready")
            n_oh = 0
            for i in range(NT):
                r = rows(i)
                for k in range(MK):
                    pe.wait_ge(s("onehot_ready"), n_oh + 1)
                    last = mm(psum[:, b, 0:2 * NBP], onehot[0:r, n_oh % 2, 0:P],
                              onehot[0:r, n_oh % 2, P:P + 2 * NBP], start=n_oh == 0, stop=n_oh == NT * MK - 1)
                    n_oh += 1
                    if n_oh < NT * MK:
                        last.then_inc(s("onehot_used"), 1)
            filled(last, "tab")

            pe.wait_ge(s("blocks_planned"), 2)
            n_pairs = pe.value_load(npair_i[0:1, 0:1], min_val=NE // 2, max_val=NBP // 2)

            def turn_xg(u, need_x, need_T):
                pe.wait_ge(s(f"xg_loaded{u}"), need_x)
                if need_T is not None:
                    pe.wait_ge(s(f"xgT_read{u}"), need_T)
                for half in range(2):
                    for q in range(4):
                        last = tr(psum[:, half, q * P:(q + 1) * P], xg[u][:, 4 * half + q::DK], ident[:])
                    last.then_inc(s(f"xg_turned{half}"), 1)

            turn_xg(0, 16, None)
            with pe.Fori(0, n_pairs) as ip:
                for u in range(2):
                    n = ip * 2 + u
                    pe.wait_ge(s("xgT_ready"), (n + 1) * 2)
                    pe.wait_ge(s(f"ewg_loaded{u}"), ip * 16 + 16)
                    for k in range(DK):
                        last = mm(psum[:, 2, :], xgT[u][:, k, :], ewg[u][:, k, :], start=k == 0, stop=k == DK - 1)
                    last.then_inc(s("egu_full"), 1)
                    pe.wait_ge(s(f"xg_loaded{1 - u}"), ip * 16 + 16 + 16 * u)
                    for half in range(2):
                        for q in range(4):
                            last = tr(psum[:, half, q * P:(q + 1) * P], xg[1 - u][:, 4 * half + q::DK], ident[:])
                        last.then_inc(s(f"xg_turned{half}"), 1)
                    pe.wait_ge(s("eh_ready"), n + 1)
                    for k in range(2):
                        last = tr(psum[:, 3, k * P:(k + 1) * P], eh[:, 2 + u, k::2], ident[:])
                    last.then_inc(s("eh_turned"), 1)
                    pe.wait_ge(s("ehT_ready"), n + 1)
                    pe.wait_ge(s(f"ewd_loaded{u}"), ip * 16 + 16)
                    for j in range(2):
                        for k in range(2):
                            last = mm(psum[:, 4 + 2 * u + j, :], ehT[u][:, k, :], ewd[u][:, k, j * 512:(j + 1) * 512],
                                      start=k == 0, stop=k == 1)
                        last.then_inc(s(f"edn_full{j}"), 1)

        @block.sync
        def _(sp):
            def ld(dst, src, name, small=False):
                sp.dma_start(dst, src, allow_slow_non_contiguous=small).then_inc(s(name), 16)

            def load_x(i):
                if i >= 2:
                    await_bank(sp, ("x", i - 2, 1))
                r = rows(i)
                src = a["x_prompt"][0, tok(i), :] if i < NT - 1 else a["x_sample"][0]
                ld(xin[0:r, i % 2, :], src, f"x_loaded{i % 2}")

            w_in = a["w_in"][0]
            w_glu = a["w_glu"][0]
            by_chunk = lambda w: w.rearrange("(p k) f -> p k f", k=DK)
            load_x(0)
            load_x(1)
            flat = lambda ap: ap.rearrange("(q e) n -> q (e n)", e=2)
            for q, name in enumerate(("ssm_a_re", "ssm_a_im")):
                ld(pst[q * GP:(q + 1) * GP, :], flat(a[name][0]), "params_loaded")
            for q, name in enumerate(("state_ssm_re", "state_ssm_im")):
                ld(pst[(q + 2) * GP:(q + 3) * GP, :], flat(a[name][0, 0]), "params_loaded")
            ld(ldt[64:80, :], a["ssm_log_dt"][0].rearrange("(q e) -> q e", e=2), "params_loaded")
            ld(w_u, by_chunk(w_in[:, 0:DS]), "w_u_loaded")
            for q, name in enumerate(("ssm_b_re", "ssm_b_im")):
                ld(braw[:, q, :, :], a[name][0].rearrange("(q e) n c -> (e n) q c", e=2), "b_loaded")
            for q, name in enumerate(("ssm_c_re", "ssm_c_im")):
                for half in range(2):
                    for g8 in range(8):
                        g = 16 * half + 2 * g8
                        ld(cst[g8 * GC:(g8 + 1) * GC, q, half, :].rearrange("c (e n) -> c e n", e=2),
                           a[name][0, g:g + 2].rearrange("e c n -> c e n"), "c_loaded")
            ld(dsk[:], a["ssm_d"][0].rearrange("(g c) -> c g", c=GC), "d_loaded", small=True)
            ld(rope[:], a["rope_table"].rearrange("(t p) a f -> p t a f", p=P), "rope_loaded")
            for i in range(2, NT):
                load_x(i)
            sp.wait_ge(s("u64_ready"), 1)
            for t in range(BL):
                ld(u2s[0:NJS, :, t, :], u64[t:DEC:BL, :].rearrange("p (g c) -> p g c", c=GC), "u2s_ready")
            sp.wait_ge(s("uT_ready"), 9)
            ld(w_i, by_chunk(w_in[:, 1280:1864]), "w_i_loaded")
            sp.wait_ge(s("s5_operators"), 4)
            ld(kpad_d.rearrange("g c (l o) -> c g l o", o=GC), kpad, "kpad_stored")
            sp.wait_ge(s("kpad_stored"), 16)
            for t in range(BL):
                ld(m_op[t * GC:(t + 1) * GC, :, :],
                   kpad_d.rearrange("g c l -> c g l")[:, :, (7 - t) * GC:(7 - t) * GC + P], "m_loaded")
            for rep in range(2):
                ld(cikd[:, :, rep * HD:(rep + 1) * HD], a["cache_idx_k"][0, 0].rearrange("(j p) d -> p j d", p=P),
                   "cik_loaded")
            for i in range(NT):
                sp.wait_ge(s("zi_roped"), i + 1)
                dst = out["ik_p"][0, 0, tok(i), :] if i < NT - 1 else out["ik_s"][0, 0]
                ld(dst, zi[0:rows(i), i % 2, 512:576], f"ik_stored{i % 2}")
            sp.wait_ge(s("y2s_ready"), 8)
            sp.wait_ge(s("rel_used"), len(score_no))
            for t in range(BL):
                ld(y64[t:DEC:BL, :], y2s[0:NJS, t, :], "y64_ready")
            sp.wait_ge(s("states_ready"), 1)
            for q, key in enumerate(("hre_p", "him_p")):
                ld(out[key][0, 0].rearrange("(q e) n -> q (e n)", e=2), hst[0:16, q, :], "h_stored")
            for q, key in enumerate(("hre_s", "him_s")):
                ld(out[key][0, 0].rearrange("(q e) n -> q (e n)", e=2), hst[0:16, 2 + q, :], "h_stored")

            def load_wgs(d):
                if d >= 2:
                    await_bank(sp, ("gs", d - 2, 2))
                u, c = d % 2, slice(d * P, (d + 1) * P)
                ld(wgs[:, u, 0:8, :], by_chunk(w_in[:, 1864 + d * P:1864 + (d + 1) * P]), f"wgs_loaded{u}")
                ld(wgs[:, u, 8:12, :], w_glu[:, c].rearrange("(k p) f -> p k f", p=P), f"wgs_loaded{u}")
                ld(wgs[:, u, 12:16, :], w_glu[:, DM + d * P:DM + (d + 1) * P].rearrange("(k p) f -> p k f", p=P),
                   f"wgs_loaded{u}")

            load_wgs(0)
            load_wgs(1)
            sp.wait_ge(s("yT_ready"), 9)
            ld(w_q, by_chunk(w_in[:, 512:1280]), "w_q_loaded")
            ld(v_tm[:, 8:24, :], a["cache_v"][0, 0].rearrange("(j p) h d -> p j (h d)", p=P), "cv_loaded")
            for d in range(2, DK):
                load_wgs(d)
            for i in range(NT):
                r = rows(i)
                sp.wait_ge(s("zq_roped"), i + 1)
                kd, vd = (out["k_p"][0, 0, tok(i)], out["v_p"][0, 0, tok(i)]) if i < NT - 1 else \
                    (out["k_s"][0, 0], out["v_s"][0, 0])
                ld(kd.rearrange("t h d -> t (h d)"), zq[0:r, i % 2, 512:640], f"k_stored{i % 2}")
                ld(vd.rearrange("t h d -> t (h d)"), v_tm[0:r, i if i < NT - 1 else 24, :], "v_stored")
            ck = a["cache_k"][0, 0].rearrange("(j p) h d -> j p h d", p=P)
            for j in range(16):
                if j >= 4:
                    await_bank(sp, ("ck", j - 4))
                for rep in range(2):
                    ld(ckd[:, j % 4, :].rearrange("p (h r d) -> p h r d", h=2, r=2)[:, :, rep, :], ck[j],
                       f"ck_loaded{j % 4}")

            sp.wait_ge(s("zeros_ready"), 1)
            for j in range(2):
                ld(slots_d[NE * P:, j * 512:(j + 1) * 512].rearrange("(b p) f -> p b f", p=P),
                   zeros.unsqueeze(1).broadcast_to([P, NBP - NE, 512]), "slots_cleared")
            w_ap = a["w_attn_proj"][0]

            def load_wap(d):
                if d >= 2:
                    await_bank(sp, ("ao", d - 2, 2))
                u = d % 2
                ld(wap[:, u, 0:8, :], by_chunk(w_in[:, 2888 + d * P:2888 + (d + 1) * P]), f"wap_loaded{u}")
                ld(wap[:, u, 8:12, :], w_ap[:, d * P:(d + 1) * P].rearrange("(k p) f -> p k f", p=P),
                   f"wap_loaded{u}")

            sp.wait_ge(s("masked"), MASKINGS)
            load_wap(0)
            load_wap(1)
            sp.wait_ge(s("aT_ready"), NT)
            ld(w_o, a["w_out"][0].rearrange("(k p) f -> p k f", p=P), "w_o_loaded")
            ld(w_sd, a["w_sh_down"][0].rearrange("(p k) f -> p k f", k=2), "w_s_loaded")
            for q, name in enumerate(("ln1_g", "ln1_b")):
                ld(ln1[:, q, :], a[name].broadcast_to([P, DM]), "ln1_loaded")
            for d in range(2, DK):
                load_wap(d)

            def load_xre(i):
                if i >= 2:
                    sp.wait_ge(s("normed"), i - 1)
                src = a["x_prompt"][0, tok(i), :] if i < NT - 1 else a["x_sample"][0]
                ld(xre[0:rows(i), i % 2, :], src, f"xre_loaded{i % 2}")

            sp.wait_ge(s("mixed_ready"), 3 * DK)
            load_xre(0)
            load_xre(1)
            ld(w_sg, by_chunk(a["w_sh_gu"][0]), "w_s_loaded")
            ld(w_r, by_chunk(a["w_router"][0]), "w_s_loaded")
            ld(rbias[:], a["router_bias"].broadcast_to([P, NE]), "w_s_loaded")
            for i in range(NT + 2):
                if 2 <= i < NT:
                    load_xre(i)
                if i < NT:
                    sp.wait_ge(s("x1_ready"), i + 1)
                    ld(x1_d[tok(i), :], x1b[0:rows(i), i % 3, :], f"x1_stored{i % 3}")
                if i >= 2:
                    sp.wait_ge(s("base_ready"), i - 1)
                    ld(base_d[tok(i - 2), :], x1b[0:rows(i - 2), (i - 2) % 3, :], f"base_stored{(i - 2) % 3}")

            sp.wait_ge(s("blocks_planned"), 3)
            ld(blk_d, bexp_i[:], "blk_stored")
            sp.wait_ge(s("blk_stored"), 16)
            ld(brow[:], blk_d.rearrange("p a -> a p"), "blk_stored")
            sp.wait_ge(s("blk_stored"), 32)
            sp.wait_ge(s("blocks_planned"), 2)
            last_pair = sp.value_load(npair_i[0:1, 1:2], min_val=NE // 2 - 1, max_val=NBP // 2 - 1)

            def expert(n):
                return sp.value_load(brow[0:1, bass.ds(n, 1)], min_val=0, max_val=NE - 1)

            def load_gu(e, u):
                ld(ewg[u], a["w_exp_gu"][0, bass.ds(e, 1)].rearrange("a (p k) f -> (a p) k f", k=DK), f"ewg_loaded{u}")

            def load_dn(e, u):
                ld(ewd[u], a["w_exp_down"][0, bass.ds(e, 1)].rearrange("a (p k) f -> (a p) k f", k=2),
                   f"ewd_loaded{u}")

            def store_y(n, u):
                sp.wait_ge(s("y_slot_ready"), (n + 1) * 2)
                ld(slots_d[bass.ds(n * P, P), :], yb[u], f"y_stored{u}")

            sp.wait_ge(s("tab_ready"), 1)
            sp.wait_ge(s("slots_cleared"), 32)
            for u in range(2):
                ld(slots_d[(NBP - 1) * P:NBP * P, u * P:(u + 1) * P], ident[:], f"y_stored{u}")
                e = expert(u)
                load_gu(e, u)
                load_dn(e, u)
            with sp.Fori(0, last_pair) as ip:
                for u in range(2):
                    n = ip * 2 + u
                    e = expert(n + 2)
                    sp.wait_ge(s("egu_full"), n + 1)
                    load_gu(e, u)
                    sp.wait_ge(s("edn_full1"), n + 1)
                    load_dn(e, u)
                    store_y(n, u)
            for u in range(2):
                store_y(last_pair * 2 + u, u)
            for u in range(2):
                sp.wait_ge(s(f"y_stored{u}"), last_pair * 16 + 32)
            sp.nop().then_inc(s("slots_done"), 1)

            for q, name in enumerate(("ln2_g", "ln2_b")):
                ld(ln2[:, q, :], a[name].broadcast_to([P, DM]), "ln2_loaded")
            for i in range(NT + 1):
                if i < NT:
                    if i >= 2:
                        sp.wait_ge(s(f"out_stored{i % 2}"), 16 * (i // 2))
                    ld(bas[0:rows(i), i % 2, :], base_d[tok(i), :], f"bas_loaded{i % 2}")
                if i >= 1:
                    sp.wait_ge(s("out_ready"), i)
                    dst = out["y_p"][0, tok(i - 1), :] if i - 1 < NT - 1 else out["y_s"][0]
                    ld(dst, bas[0:rows(i - 1), (i - 1) % 2, :], f"out_stored{(i - 1) % 2}")
            sp.wait_ge(s("out_stored0"), 16 * 5)
            sp.wait_ge(s("out_stored1"), 16 * 4)
            sp.wait_ge(s("v_stored"), 16 * NT)
            sp.wait_ge(s("k_stored0"), 16 * 5)
            sp.wait_ge(s("k_stored1"), 16 * 4)
            sp.wait_ge(s("ik_stored0"), 16 * 5)
            sp.wait_ge(s("ik_stored1"), 16 * 4)
            sp.wait_ge(s("h_stored"), 64)

        @block.gpsimd
        def _(pool):
            steps = [0]

            def step(ins):
                steps[0] += 1
                ins.then_inc(pool_step, 1)
                pool.wait_ge(pool_step, steps[0])

            tt = pool.tensor_tensor
            step(pool.memset(ident[:], 0.0))
            pool.affine_select(out=ident[:], in_=ident[:], compare_op=ALU.not_equal, fill=1.0, base=0,
                               pattern=[[-1, P]], channel_multiplier=1).then_inc(s("constants"), 1)
            step(pool.memset(tri[:], 0.0))
            pool.affine_select(out=tri[:], in_=tri[:], compare_op=ALU.is_ge, fill=1.0, base=0,
                               pattern=[[-1, P]], channel_multiplier=1).then_inc(s("constants"), 1)
            pool.memset(ones[:], 1.0).then_inc(s("constants"), 1)
            pool.iota(iota64[:], [[1, P]], base=0, channel_multiplier=0,
                      allow_small_or_imprecise_dtypes=True).then_inc(s("constants"), 1)
            pool.iota(tokid[:], [[P, NT]], base=0, channel_multiplier=1,
                      allow_small_or_imprecise_dtypes=True).then_inc(s("constants"), 1)
            pool.memset(uT[:, :, NJ], 0.0).then_inc(s("constants"), 1)
            pool.memset(hp[:, 0, :, :], 0.0).then_inc(s("constants"), 1)
            pool.iota(bexp[:, 0:1], [[0, 1]], base=0, channel_multiplier=1,
                      allow_small_or_imprecise_dtypes=True).then_inc(s("constants"), 1)

            pool.wait_ge(s("b_ready"), GP)
            pool.wait_ge(s("s5_operators"), 1)
            step(pool.tensor_copy(hp[:, NJ + 1, :, :], par[:, 2:4, :]))
            for j in list(range(NJ)) + list(range(NJ + 1, HC - 1)):
                h, hn = hp[:, j, :, :], hp[:, j + 1, :, :]
                tt(sct[:, 0, :, :], a8[:, 0, :, :], h, ALU.mult).then_inc(pool_step, 1)
                steps[0] += 1
                step(tt(sct[:, 1, :, :], a8[:, 1, :, :], h, ALU.mult))
                step(tt(hn, hn, sct[:, 0, :, :], ALU.add))
                tt(hp[:, j + 1, 0, :], hp[:, j + 1, 0, :], sct[:, 1, 1, :], ALU.add).then_inc(pool_step, 1)
                steps[0] += 1
                step(tt(hp[:, j + 1, 1, :], hp[:, j + 1, 1, :], sct[:, 1, 0, :], ALU.add))
            pool.memset(sct[:], 0.0).then_inc(s("state_ready"), 1)

            def rotate(z, r, i, h0, nh):
                v = z.rearrange("p (h d) -> p h d", d=HD)[:, h0:h0 + nh, :]
                lo, hi = v[:, :, 0:8], v[:, :, 8:16]
                cos = rope[0:r, i, 0, :].unsqueeze(1).broadcast_to([r, nh, 8])
                sin = rope[0:r, i, 1, :].unsqueeze(1).broadcast_to([r, nh, 8])
                tmp = [rtmp[0:r, q, 0:nh, :] for q in range(4)]
                for q, (x, w) in enumerate(((lo, cos), (hi, sin), (lo, sin), (hi, cos))):
                    steps[0] += 1
                    tt(tmp[q], x, w, ALU.mult).then_inc(pool_step, 1)
                pool.wait_ge(pool_step, steps[0])
                steps[0] += 1
                tt(lo, tmp[0], tmp[1], ALU.subtract).then_inc(pool_step, 1)
                step(tt(hi, tmp[2], tmp[3], ALU.add))

            pool.wait_ge(s("rope_loaded"), 16)
            for i in range(NT):
                r = rows(i)
                pool.wait_ge(s("zi_ready"), i + 1)
                rotate(zi[0:r, i % 2, 0:576], r, i, 0, 9)
                pool.tensor_copy(zi[0:r, i % 2, 576:640], zi[0:r, i % 2, 512:576]).then_inc(s("zi_roped"), 1)
            m = 0
            for d in range(DK):
                for c, (t0, n) in enumerate(TOK_CHUNKS):
                    pool.wait_ge(s("val_used"), m + 1)
                    tt(g1[:, d, t0:t0 + n], sg[:, 2 * (m % 2), 0:n], sg[:, 2 * (m % 2) + 1, 0:n],
                       ALU.mult).then_inc(s("sg_used"), 1)
                    m += 1
            for i in range(NT):
                r = rows(i)
                pool.wait_ge(s("zq_ready"), i + 1)
                if i >= 2:
                    await_bank(pool, ("kT", i - 2))
                rotate(zq[0:r, i % 2, 0:640], r, i, 0, 10)
                dup = kdup[0:r, i % 2, :].rearrange("p (h e d) -> p h e d", h=2, e=2)
                k2 = zq[0:r, i % 2, 512:640].rearrange("p (h d) -> p h d", h=2)
                step(pool.tensor_copy(dup[:, :, 0, :], k2))
                pool.tensor_copy(dup[:, :, 1, :], k2).then_inc(s("zq_roped"), 1)

            m = 0
            for d in range(DK):
                for c, (t0, n) in enumerate(TOK_CHUNKS):
                    pool.wait_ge(s("ao_used"), m + 1)
                    tt(g1[:, d, t0:t0 + n], g1[:, d, t0:t0 + n], sga[:, m % 4, 0:n],
                       ALU.add).then_inc(s("mixed_ready"), 1)
                    m += 1

            pool.wait_ge(s("ln1_loaded"), 32)
            for i in range(NT):
                r = rows(i)
                x1 = x1b[0:r, i % 3, :]
                pool.wait_ge(s("normed"), i + 1)
                step(tt(x1, x1, ln1[0:r, 0, :], ALU.mult))
                tt(x1, x1, ln1[0:r, 1, :], ALU.add).then_inc(s("x1_ready"), 1)

            pool.wait_ge(s("blocks_planned"), 2)
            pool.wait_ge(s("tab_ready"), 1)
            for u in range(3):
                pool.wait_ge(s(f"x1_stored{u}"), 16 * 3)
            n_pairs = pool.value_load(npair_i[0:1, 0:1], min_val=NE // 2, max_val=NBP // 2)

            def gather(u):
                pool.indirect_dma_start(xg[u], None, x1_d,
                                        bass.IndirectOffsetOnAxis(ap=tid[u][:, 0:1], axis=0)
                                        ).then_inc(s(f"xg_loaded{u}"), 16)

            def carry_wait():
                tt(carry[:], ones[0:1, 0:1], ones[0:1, 0:1], ALU.mult).then_inc(s("carried"), 1)

            pool.wait_ge(s("tid_ready"), 1)
            carry_wait()
            gather(0)
            with pool.Fori(0, n_pairs) as ip:
                for u in range(2):
                    n = ip * 2 + u
                    pool.wait_ge(s("carried"), n + 1)
                    pool.wait_ge(s("tid_ready"), n + 2)
                    carry_wait()
                    gather(1 - u)

            pool.wait_ge(s("slots_done"), 1)
            pool.wait_ge(s("ln2_loaded"), 32)
            for i in range(NT + 1):
                for k in range(MK if i < NT else 0):
                    m = i * MK + k
                    if m >= 8:
                        pool.wait_ge(s("part_used"), m - 7)
                    pool.indirect_dma_start(part[0:rows(i), m % 8, :], None, slots_d,
                                            bass.IndirectOffsetOnAxis(ap=slot_i[0:rows(i), i, k:k + 1], axis=0)
                                            ).then_inc(s(f"part_loaded{m % 8}"), 16)
                if i >= 1:
                    r, y = rows(i - 1), bas[0:rows(i - 1), (i - 1) % 2, :]
                    pool.wait_ge(s("normed"), NT + i)
                    step(tt(y, y, ln2[0:r, 0, :], ALU.mult))
                    tt(y, y, ln2[0:r, 1, :], ALU.add).then_inc(s("out_ready"), 1)

        @block.scalar
        def _(act):
            def f(dst, src, fn=ACT.Copy, **kw):
                return act.activation(dst, src, fn, **kw)

            def take(key, dst, src, name, fn=ACT.Copy, **kw):
                await_bank(act, key)
                f(dst, src, fn, **kw).then_inc(s(name), 1)

            quad = lambda key, n=P: bank(key)[:, 0:4 * P].rearrange("p (q n) -> p q n", q=4)[:, :, 0:n]

            for i in range(NT):
                for half in range(2):
                    take(("x", i, half), xT[:, 4 * half:4 * half + 4, tok(i)], quad(("x", i, half), rows(i)), "xT_ready")
            take("par", par[:].rearrange("p a b -> p (a b)"), bank("par")[:, 0:80], "par_ready")
            act.wait_ge(s("par_ready"), 1)
            f(sm[:, 0, :], par[:, 4, :], ACT.Exp).then_inc(s("trig_ready"), 1)
            act.wait_ge(s("angle_ready"), 1)
            f(sm[:, 3, :], sm[:, 1, :], ACT.Exp)
            f(sm[:, 4, :], sm[:, 2, :], ACT.Sin)
            f(sm[:, 5, :], sm[:, 2, :], ACT.Sin, scale=0.5).then_inc(s("trig_ready"), 1)
            for t in range(BL):
                take(("u", t), u2[:, :, t, :], bank(("u", t)).rearrange("p (g c) -> p g c", c=GC), "u2_ready")
            take("u_s", u64[0:DEC, :], bank("u_s")[0:DEC, :], "u64_ready")
            take("c", craw.rearrange("p a b c -> p (a b c)"), bank("c"), "c_turned")
            for q4 in range(8):
                take(("ut", q4), uT[:, 4 * q4:4 * q4 + 4, 0:NJ], quad(("ut", q4)), "uT_ready")
            take("uts", uT[:, :, NJ + 1:UC], bank("uts")[:, 0:NG * NJS].rearrange("p (g j) -> p g j", j=NJS),
                 "uT_ready")
            bopT_flat = bopT.rearrange("p a b n -> p (a b) n")
            for q4 in range(8):
                take(("bt", q4), bopT_flat[:, 4 * q4:4 * q4 + 4, :], quad(("bt", q4)), "bopT_ready")
            act.wait_ge(s("constants"), 8)
            for gp in range(GP):
                take(("b", gp), hp[:, 1:1 + UC, :, gp].rearrange("p j a -> p a j"),
                     bank(("b", gp))[:, 0:2 * UC].rearrange("p (a j) -> p a j", a=2), "b_ready")
            for q4 in range(4):
                for e in range(2):
                    b = ("k", q4, e)
                    take(b, kpad[:, 8 * q4 + e:8 * q4 + e + 7:2, 7:15, :].rearrange("p g l o -> p g (l o)"),
                         quad(b)[0:GC], "k_ready")

            def take_zi(i):
                r, z = rows(i), zi[0:rows(i), i % 2, :]
                if i == 0:
                    act.wait_ge(s("kpad_stored"), 16)
                if i >= 2:
                    await_bank(act, ("iqT", i - 2) if i - 2 in CHOOSING else ("ikT", i - 2))
                    act.wait_ge(s(f"ik_stored{i % 2}"), 16 * (i // 2))
                await_bank(act, ("iq", i))
                f(z[:, 0:512], bank(("iq", i))[0:r, :])
                await_bank(act, ("ik", i))
                f(z[:, 512:576], bank(("ik", i))[0:r, 0:64])
                f(iws[0:r, i, :], bank(("ik", i))[0:r, 64:72], scale=8 ** -0.5).then_inc(s("zi_ready"), 1)

            def take_turned(i):
                r = rows(i)
                k0 = i * P if i < NT - 1 else SEQ + PAST
                take(("ikT", i), ikT[:, k0:k0 + r], bank(("ikT", i))[:, 0:r], "ikT_ready")
                if i in CHOOSING:
                    take(("iqT", i), iqT[:, :, (i - 2) * P:(i - 2) * P + r], quad(("iqT", i), r), "iqT_ready")

            def take_scores(i):
                r = rows(i)
                for _, c0, n in score_keys(i):
                    for h in range(NH):
                        m = score_no[i, c0, h]
                        if m >= 4:
                            act.wait_ge(s("rel_used"), m - 3)
                        take(("s", i, c0, h), rel[0:r, m % 4, 0:n], bank(("s", i, c0, h))[0:r, 0:n], "rel_ready",
                             ACT.Relu, scale=HD ** -0.5)

            for i in range(NT):
                take_zi(i)
                if i > 0:
                    take_turned(i - 1)
                    if i - 1 in CHOOSING:
                        take_scores(i - 1)
                if i == 7:
                    for q4 in range(4):
                        take(("cik", q4), ikT[:, SEQ + q4 * 512:SEQ + (q4 + 1) * 512], bank(("cik", q4)), "cik_ready")
            take_turned(NT - 1)
            take_scores(NT - 1)

            for sample in range(2):
                r, y = (NJS, y2s) if sample else (NJ, y2)
                for key in [("y", sample, q4, e) for q4 in range(4) for e in range(2)]:
                    take(key, y[0:r].rearrange("p t (q g e c) -> p q e g t c", q=4, g=4, e=2)[:, key[2], key[3]],
                         bank(key)[0:r].rearrange("p (g t c) -> p g t c", g=4, t=BL),
                         "y2s_ready" if sample else "y_ready", ACT.Gelu_apprx_tanh)
            act.wait_ge(s("rel_used"), len(score_no))
            for u in range(2):
                act.wait_ge(s(f"ik_stored{u}"), 16 * (5 - u))
            take("hst", hst[0:16].rearrange("p a n -> p (a n)"), bank("hst")[0:16, :], "states_ready")
            for t in range(BL):
                take(("yt", t), yT[:, :, t:SEQ:BL], quad(("yt", t)), "yT_ready")
            take("yts", yT[:, :, SEQ:T], bank("yts")[:, 0:4 * DEC].rearrange("p (q n) -> p q n", q=4), "yT_ready")

            m = 0
            for d in range(DK):
                for c, (t0, n) in enumerate(TOK_CHUNKS):
                    if m >= 2:
                        act.wait_ge(s("sg_used"), m - 1)
                    for q, key in enumerate(("glu", "gs")):
                        take((key, d, c), sg[:, 2 * (m % 2) + q, 0:n], bank((key, d, c))[:, 0:n], "sg_ready",
                             ACT.Sigmoid)
                    m += 1

            def take_qkv(i):
                r, z = rows(i), zq[0:rows(i), i % 2, :]
                if i >= 2:
                    await_bank(act, ("qT", i - 2))
                    act.wait_ge(s(f"k_stored{i % 2}"), 16 * (i // 2))
                if i == 0:
                    act.wait_ge(s("sg_used"), 3 * DK)
                await_bank(act, ("q", i))
                f(z[:, 0:512], bank(("q", i))[0:r, :])
                await_bank(act, ("kv", i))
                f(z[:, 512:640], bank(("kv", i))[0:r, 0:128])
                f(v_tm[0:r, i if i < NT - 1 else 24, :], bank(("kv", i))[0:r, 128:256]).then_inc(s("zq_ready"), 1)

            def take_qk_turned(i):
                r = rows(i)
                k0 = i * P if i < NT - 1 else SEQ + PAST
                take(("qT", i), qT[:, :, tok(i)], quad(("qT", i), r), "qT_ready")
                take(("kT", i), kT[:, :, k0:k0 + r], quad(("kT", i), r)[:, 0:2, :], "qT_ready")

            for i in range(NT):
                take_qkv(i)
                if i > 0:
                    take_qk_turned(i - 1)
            take_qk_turned(NT - 1)
            for j in range(16):
                take(("ck", j), kT[:, :, SEQ + j * P:SEQ + (j + 1) * P], quad(("ck", j))[:, 0:2, :], "ckT_ready")

            def soften(n):
                i, h = ATT[n]
                r, nk = rows(i), keys(i)[1]
                act.wait_ge(s("nbias_ready"), n + 1)
                p = pr[0:r, n % 2, 0:nk]
                f(p, p, ACT.Exp, bias=nbias[0:r, n % 2:n % 2 + 1], scale=HD ** -0.5,
                  accum_out=rsum[0:r, n % 2:n % 2 + 1]).then_inc(s("probs"), 1)

            def take_pT(n, q):
                i, _ = ATT[n]
                r, gq = rows(i), group_no[n, q]
                g0, gn = key_groups(i)[q]
                if gq >= 2:
                    act.wait_ge(s("pT_used"), gq - 1)
                w = key_tiles(i)[g0][1]
                take(("p", n, q), pT[0:w, gq % 2, :].rearrange("p (c n) -> p c n", c=4)[:, 0:gn, 0:r],
                     quad(("p", n, q), r)[0:w, 0:gn, :], "pT_ready")

            soften(0)
            for n, (i, h) in enumerate(ATT):
                take_pT(n, 0)
                if n + 1 < len(ATT):
                    soften(n + 1)
                for q in range(1, len(key_groups(i))):
                    take_pT(n, q)
                if h == NH - 1:
                    if i == 0:
                        act.wait_ge(s("h_stored"), 64)
                        act.wait_ge(s("k_stored0"), 16 * 5)
                        act.wait_ge(s("k_stored1"), 16 * 4)
                    act.wait_ge(s("pT_used"), group_no[n, len(key_groups(i)) - 1] + 1)
                    f(aT[:, :, tok(i)], quad(("o", i), rows(i))).then_inc(s("aT_ready"), 1)

            m = 0
            for d in range(DK):
                for c, (t0, n) in enumerate(TOK_CHUNKS):
                    if m >= 4:
                        act.wait_ge(s("mixed_ready"), m - 3)
                    if m == 0:
                        act.wait_ge(s("masked"), MASKINGS)
                    take(("ga", d, c), sga[:, m % 4, 0:n], bank(("ga", d, c))[:, 0:n], "sga_ready", ACT.Sigmoid)
                    m += 1

            def norm(i):
                r = rows(i)
                act.wait_ge(s("var_ready"), i + 1)
                f(lst[0:r, 1:2], lst[0:r, 0:1], ACT.Sqrt).then_inc(s("std_ready"), 1)
                act.wait_ge(s("rstd_ready"), i + 1)
                if i >= 3:
                    act.wait_ge(s(f"base_stored{i % 3}"), 16 * (i // 3))
                f(x1b[0:r, i % 3, :], xre[0:r, i % 2, :], ACT.Identity, bias=lst[0:r, 3:4],
                  scale=lst[0:r, 2:3]).then_inc(s("normed"), 1)

            def after_norm(i):
                r = rows(i)
                for half in range(2):
                    take(("x1", i, half), x1T[:, 4 * half:4 * half + 4, tok(i)], quad(("x1", i, half), r), "x1T_ready")
                if i >= 2:
                    act.wait_ge(s("sel_ready"), i - 1)
                take(("r", i), rsc[0:r, i % 2, :], bank(("r", i))[0:r, 0:NE], "rsc_ready", ACT.Sigmoid)
                await_bank(act, ("sg", i))
                if i >= 2:
                    await_bank(act, ("ht", i - 2))
                f(hsh[0:r, i % 2, :], bank(("sg", i))[0:r, 0:DE], ACT.Silu).then_inc(s("silu_ready"), 1)

            for i in range(NT + 2):
                if i < NT:
                    norm(i)
                if 0 <= i - 1 < NT:
                    after_norm(i - 1)
                if 0 <= i - 2 < NT:
                    r = rows(i - 2)
                    take(("ht", i - 2), hshT[:, i % 2, :].rearrange("p (k n) -> p k n", k=2)[:, :, 0:r],
                         quad(("ht", i - 2), r)[:, 0:2, :], "hshT_ready")

            act.wait_ge(s("blocks_planned"), 2)
            n_pairs = act.value_load(npair_i[0:1, 0:1], min_val=NE // 2, max_val=NBP // 2)

            def take_rows(need, u):
                act.wait_ge(s("xg_turned0"), need)
                f(xgT[u][:, 0:4, :], psum[:, 0, :].rearrange("p (q n) -> p q n", q=4)).then_inc(s("xgT_ready"), 1)

            take_rows(1, 0)
            with act.Fori(0, n_pairs) as ip:
                for u in range(2):
                    n = ip * 2 + u
                    act.wait_ge(s("egu_full"), n + 1)
                    f(eh[:, u, :], psum[:, 2, 0:DE], ACT.Silu).then_inc(s("esilu_ready"), 1)
                    take_rows(n + 2, 1 - u)
                    act.wait_ge(s("eh_turned"), n + 1)
                    f(ehT[u], psum[:, 3, 0:2 * P].rearrange("p (k n) -> p k n", k=2)).then_inc(s("ehT_ready"), 1)
                    act.wait_ge(s(f"y_stored{u}"), ip * 16 + 16)
                    act.wait_ge(s("edn_full0"), n + 1)
                    f(yb[u][:, 0:512], psum[:, 4 + 2 * u, :], ACT.Copy,
                      scale=gcol[:, u:u + 1]).then_inc(s("y_slot_ready"), 1)

            for i in range(NT):
                r = rows(i)
                act.wait_ge(s("var_ready"), NT + i + 1)
                f(lst[0:r, 1:2], lst[0:r, 0:1], ACT.Sqrt).then_inc(s("std_ready"), 1)
                act.wait_ge(s("rstd_ready"), NT + i + 1)
                f(bas[0:r, i % 2, :], bas[0:r, i % 2, :], ACT.Identity, bias=lst[0:r, 3:4],
                  scale=lst[0:r, 2:3]).then_inc(s("normed"), 1)

        @block.vector
        def _(dve):
            steps = [0]

            def step(ins):
                steps[0] += 1
                ins.then_inc(dve_step, 1)
                dve.wait_ge(dve_step, steps[0])

            tt, ts, stt = dve.tensor_tensor, dve.tensor_scalar, dve.scalar_tensor_tensor

            for t in (pst[64:80, :],):
                dve.wait_ge(s("params_loaded"), 16 * 5)
                dve.tensor_copy(t.rearrange("q (e n) -> q e n", e=2),
                                ldt[64:80, :].unsqueeze(2).broadcast_to([GP, 2, NS])).then_inc(s("param_rows"), 1)
            ar, ai = par[:, 0, :], par[:, 1, :]
            dve.wait_ge(s("par_ready"), 1)
            dve.wait_ge(s("trig_ready"), 1)
            tt(sm[:, 1, :], sm[:, 0, :], ar, ALU.mult)
            step(tt(sm[:, 6, :], sm[:, 0, :], ai, ALU.mult))
            step(ts(sm[:, 7, :], sm[:, 6, :], 1.0 / TWO_PI, ROUND, ALU.mult, ALU.add))
            step(ts(sm[:, 7, :], sm[:, 7, :], ROUND, None, ALU.subtract))
            step(stt(sm[:, 8, :], sm[:, 7, :], -6.28125, sm[:, 6, :], ALU.mult, ALU.add))
            step(stt(sm[:, 8, :], sm[:, 7, :], -0.0019350051879882812, sm[:, 8, :], ALU.mult, ALU.add))
            step(stt(sm[:, 8, :], sm[:, 7, :], -(TWO_PI - 6.28125 - 0.0019350051879882812), sm[:, 8, :],
                     ALU.mult, ALU.add))
            ts(sm[:, 2, :], sm[:, 8, :], 3.1415925, -3.1415925, ALU.min, ALU.max).then_inc(s("angle_ready"), 1)
            tt(sm[:, 9, :], ar, ar, ALU.mult)
            step(tt(sm[:, 10, :], ai, ai, ALU.mult))
            step(tt(sm[:, 9, :], sm[:, 9, :], sm[:, 10, :], ALU.add))
            step(dve.reciprocal(sm[:, 10, :], sm[:, 9, :]))
            dve.memset(pw[:, 0, 0, :], 1.0)
            dve.memset(pw[:, 1, 0, :], 0.0)
            dve.wait_ge(s("trig_ready"), 2)
            step(tt(sm[:, 11, :], sm[:, 5, :], sm[:, 5, :], ALU.mult))
            step(ts(sm[:, 11, :], sm[:, 11, :], -2.0, 1.0, ALU.mult, ALU.add))
            tt(pw[:, 0, 1, :], sm[:, 3, :], sm[:, 11, :], ALU.mult)
            step(tt(pw[:, 1, 1, :], sm[:, 3, :], sm[:, 4, :], ALU.mult))
            step(ts(sm[:, 12, :], pw[:, 0, 1, :], -1.0, None, ALU.add))
            tt(sm[:, 13, :], sm[:, 12, :], ar, ALU.mult)
            tt(sm[:, 14, :], pw[:, 1, 1, :], ai, ALU.mult)
            tt(sm[:, 15, :], pw[:, 1, 1, :], ar, ALU.mult)
            step(tt(sm[:, 6, :], sm[:, 12, :], ai, ALU.mult))
            tt(sm[:, 13, :], sm[:, 13, :], sm[:, 14, :], ALU.add)
            step(tt(sm[:, 15, :], sm[:, 15, :], sm[:, 6, :], ALU.subtract))
            tt(sm[:, 13, :], sm[:, 13, :], sm[:, 10, :], ALU.mult)
            step(tt(sm[:, 14, :], sm[:, 15, :], sm[:, 10, :], ALU.mult))
            for n in (1, 2, 4):
                xr, xi = pw[:, 0, 1:n + 1, :], pw[:, 1, 1:n + 1, :]
                wr, wi = (pw[:, q, n:n + 1, :].broadcast_to([P, n, GP]) for q in range(2))
                q = [v[:, 0:n * GP].rearrange("p (n g) -> p n g", n=n)
                     for v in (t1, t2, t1[:, 1024:2048], t2[:, 1024:2048])]
                tt(q[0], xr, wr, ALU.mult)
                tt(q[1], xi, wi, ALU.mult)
                tt(q[2], xr, wi, ALU.mult)
                step(tt(q[3], xi, wr, ALU.mult))
                tt(pw[:, 0, n + 1:2 * n + 1, :], q[0], q[1], ALU.subtract)
                step(tt(pw[:, 1, n + 1:2 * n + 1, :], q[2], q[3], ALU.add))
            dve.tensor_copy(a8[:, 0, 0, :], pw[:, 0, 8, :])
            dve.tensor_copy(a8[:, 0, 1, :], pw[:, 0, 8, :])
            dve.tensor_copy(a8[:, 1, 0, :], pw[:, 1, 8, :])
            ts(a8[:, 1, 1, :], pw[:, 1, 8, :], -1.0, None, ALU.mult).then_inc(s("s5_operators"), 1)
            dve.wait_ge(s("b_loaded"), 32)
            cr, ci = (sm[:, q, :].unsqueeze(2).broadcast_to([P, GP, GC]) for q in (13, 14))
            q = [v[:, o:o + 256].rearrange("p (g c) -> p g c", c=GC) for v in (t1, t2) for o in (0, 256)]
            tt(q[0], cr, braw[:, 0, :, :], ALU.mult)
            tt(q[1], ci, braw[:, 1, :, :], ALU.mult)
            tt(q[2], cr, braw[:, 1, :, :], ALU.mult)
            step(tt(q[3], ci, braw[:, 0, :, :], ALU.mult))
            tt(bbar[:, 0, :, :], q[0], q[1], ALU.subtract)
            step(tt(bbar[:, 1, :, :], q[2], q[3], ALU.add))
            for part_ in range(2):
                for t in range(BL):
                    w = [pw[:, q_, 7 - t, :].unsqueeze(2).broadcast_to([P, GP, GC]) for q_ in range(2)]
                    o = slice(t * 256, (t + 1) * 256)
                    tt(t1[:, o].rearrange("p (g c) -> p g c", c=GC), w[0], bbar[:, part_, :, :], ALU.mult)
                    last = tt(t2[:, o].rearrange("p (g c) -> p g c", c=GC), w[1], bbar[:, 1 - part_, :, :], ALU.mult)
                step(last)
                v = [x[:, 0:2048].rearrange("p (t g c) -> p g t c", t=BL, g=GP) for x in (t1, t2)]
                step(tt(ba[:, part_, :, :, :], v[0], v[1], ALU.add if part_ else ALU.subtract))
            dve.memset(slot[:], 0.0).then_inc(s("s5_operators"), 1)
            dve.wait_ge(s("c_turned"), 1)
            w = [pw[:, q_, :, :].rearrange("p k g -> p g k").unsqueeze(3).broadcast_to([P, GP, 9, GC])
                 for q_ in range(2)]
            c_ = [craw[:, q_, :, :].unsqueeze(2).broadcast_to([P, GP, 9, GC]) for q_ in range(2)]
            v = [x.rearrange("p (g k c) -> p g k c", g=GP, k=9) for x in (t1, t2)]
            tt(v[0], w[0], c_[0], ALU.mult)
            step(tt(v[1], w[1], c_[1], ALU.mult))
            step(tt(ca[:, 0, :, :, :], v[0], v[1], ALU.subtract))
            tt(v[0], w[0], c_[1], ALU.mult)
            step(tt(v[1], w[1], c_[0], ALU.mult))
            step(stt(ca[:, 1, :, :, :].rearrange("p g k c -> p (g k c)"), t1, -1.0, t2, ALU.mult, ALU.subtract))
            dve.memset(cum[:], 0.0).then_inc(s("s5_operators"), 1)
            await_bank(dve, ("b", GP - 1))
            dve.memset(kpad[:, :, 0:7, :], 0.0)
            dve.wait_ge(s("d_loaded"), 16)
            dve.wait_ge(s("constants"), 8)
            skip = t1[0:GC, 0:512].rearrange("c (g o) -> c g o", o=GC)
            step(tt(skip, ident[0:GC, 0:GC].unsqueeze(1).broadcast_to([GC, NG, GC]),
                    dsk[:].unsqueeze(2).broadcast_to([GC, NG, GC]), ALU.mult))
            dve.wait_ge(s("k_ready"), 8)
            tt(kpad[:, :, 7, :], kpad[:, :, 7, :], skip, ALU.add).then_inc(s("s5_operators"), 1)

            dve.wait_ge(s("s5_operators"), 4)
            step(dve.memset(mk[:, 0:MASK_AT[2]], 0.0))
            for i in range(2):
                e = MASK_AT[i] + keys(i)[1]
                step(dve.memset(mk[0:64, e - 64:e], HID))
            mask_step = {0: steps[0], 1: steps[0]}

            def add_scores(i):
                r = rows(i)
                for _, c0, n in score_keys(i):
                    o = mk[0:r, MASK_AT[i] + c0:MASK_AT[i] + c0 + n]
                    for h in range(NH):
                        m = score_no[i, c0, h]
                        w, x = iws[0:r, i, h:h + 1], rel[0:r, m % 4, 0:n]
                        dve.wait_ge(s("rel_ready"), m + 1)
                        if h == 0:
                            ins = ts(o, x, w, None, ALU.mult)
                        else:
                            dve.wait_ge(s("rel_used"), m)
                            ins = stt(o, x, w, o, ALU.mult, ALU.add)
                        ins.then_inc(s("rel_used"), 1)
                dve.wait_ge(s("rel_used"), m + 1)
                if i < NT - 1:
                    e = MASK_AT[i] + keys(i)[1]
                    step(dve.memset(mk[0:64, e - 64:e], HID))

            at_round = [0]

            def choose(us):
                while us > 0 and at_round[0] < len(CHOOSING) * TOPK // 8:
                    i, r_ = CHOOSING[at_round[0] // (TOPK // 8)], at_round[0] % (TOPK // 8)
                    r, n = rows(i), keys(i)[1]
                    sc = mk[0:r, MASK_AT[i]:MASK_AT[i] + n]
                    step(dve.max(best[0:r, :], sc))
                    step(dve.match_replace(sc, best[0:r, :], sc, TAKEN))
                    if r_ == TOPK // 8 - 1:
                        step(ts(sc, sc, TAKEN / 2, HID, ALU.is_gt, ALU.mult))
                        mask_step[i] = steps[0]
                    at_round[0] += 1
                    us -= 2 * (n / 960 + 0.07)

            for i in CHOOSING:
                add_scores(i)
                choose({2: 6, 3: 6, 4: 8, 5: 8, 6: 8, 7: 4}.get(i, 35))

            m = 0
            for d in range(DK):
                for c, (t0, n) in enumerate(TOK_CHUNKS):
                    dve.wait_ge(s("sg_ready"), 2 * m + 2)
                    await_bank(dve, ("val", d, c))
                    v_ = sg[:, 2 * (m % 2), 0:n]
                    tt(v_, bank(("val", d, c))[:, 0:n], v_, ALU.mult).then_inc(s("val_used"), 1)
                    choose(8.5)
                    m += 1
            choose(85)

            maskings = [0]

            def mask(n):
                i, h = ATT[n]
                r = rows(i)
                dve.wait_ge(dve_step, mask_step[i])
                chunks = split(keys(i)[1], 1024)
                for q, (c0, w) in enumerate(chunks):
                    key = ("l", n, c0)
                    nb = len(split(w, 512))
                    for j in range(nb):
                        await_bank(dve, key, j)
                    f0 = banks.at[key][0]
                    lg = psum[0:r, f0:f0 + nb, :].rearrange("p b n -> p (b n)")[:, 0:w]
                    dve.tensor_tensor_reduce(out=pr[0:r, n % 2, c0:c0 + w], in0=lg,
                                             in1=mk[0:r, MASK_AT[i] + c0:MASK_AT[i] + c0 + w], scale=1.0,
                                             scalar=TAKEN, op0=ALU.add, op1=ALU.max,
                                             accum_out=mx[0:r, n % 2, q:q + 1]).then_inc(s("masked"), 1)
                    maskings[0] += 1
                dve.wait_ge(s("masked"), maskings[0])
                top = mx[0:r, n % 2, 0:1]
                if len(chunks) > 1:
                    top = mx[0:r, n % 2, 3:4]
                    step(dve.reduce_max(top, mx[0:r, n % 2, 0:len(chunks)], AX.X))
                ts(nbias[0:r, n % 2:n % 2 + 1], top, -HD ** -0.5, None, ALU.mult).then_inc(s("nbias_ready"), 1)

            await_bank(dve, ("l", 0, 0))
            dve.memset(zeros, 0.0).then_inc(s("zeros_ready"), 1)
            mask(0)
            for n, (i, h) in enumerate(ATT):
                r = rows(i)
                if n + 1 < len(ATT):
                    if ATT[n + 1][0] == NT - 1:
                        choose(1e9)
                    mask(n + 1)
                dve.wait_ge(s("probs"), n + 1)
                ri = rinv[0:r, n % 2:n % 2 + 1]
                step(dve.reciprocal(ri, rsum[0:r, n % 2:n % 2 + 1]))
                ts(diag[0:r, n % 2, 0:r], ident[0:r, 0:r], ri, None, ALU.mult).then_inc(s("diag_ready"), 1)
                choose(2)

            m = 0
            for d in range(DK):
                for c, (t0, n) in enumerate(TOK_CHUNKS):
                    dve.wait_ge(s("sga_ready"), m + 1)
                    await_bank(dve, ("ao", d, c))
                    v_ = sga[:, m % 4, 0:n]
                    tt(v_, bank(("ao", d, c))[:, 0:n], v_, ALU.mult).then_inc(s("ao_used"), 1)
                    m += 1

            def statistics(x, r, n):
                if n > 0:
                    dve.wait_ge(s("normed"), n)
                for q_ in range(2):
                    last = dve.bn_stats(stats[0:r, q_, :], x[:, q_ * 512:(q_ + 1) * 512])
                step(last)
                step(dve.bn_aggr(mv[0:r, :], stats[0:r, :, :].rearrange("p a b -> p (a b)")))
                ts(lst[0:r, 0:1], mv[0:r, 1:2], EPS, None, ALU.add).then_inc(s("var_ready"), 1)
                dve.wait_ge(s("std_ready"), n + 1)
                step(dve.reciprocal(lst[0:r, 2:3], lst[0:r, 1:2]))
                stt(lst[0:r, 3:4], mv[0:r, 0:1], -1.0, lst[0:r, 2:3], ALU.mult,
                    ALU.mult).then_inc(s("rstd_ready"), 1)

            def residual(i):
                r = rows(i)
                dve.wait_ge(s(f"xre_loaded{i % 2}"), 16 * (i // 2 + 1))
                f0 = banks.at[("wo", i)][0]
                for j in range(2):
                    await_bank(dve, ("wo", i), j)
                x = xre[0:r, i % 2, :]
                stt(x, x, ALPHA, psum[0:r, f0:f0 + 2, :].rearrange("p b n -> p (b n)"), ALU.mult,
                    ALU.add).then_inc(s("res_ready"), 1)
                dve.wait_ge(s("res_ready"), i + 1)
                statistics(x, r, i)

            def expert_match(i):
                r = rows(i)
                step(tt(oh[0:r], iota64[0:r, 0:NE].unsqueeze(1).broadcast_to([r, MK, NE]),
                        idx[0:r, i, 0:MK].unsqueeze(2).broadcast_to([r, MK, NE]), ALU.is_equal))

            def route(i):
                r = rows(i)
                sc = rsc[0:r, i % 2, :]
                dve.wait_ge(s("rsc_ready"), i + 1)
                if i == 0:
                    dve.wait_ge(s("w_s_loaded"), 64)
                biased = sb64[0:r, :]
                step(tt(biased, sc, rbias[0:r, :], ALU.add))
                step(dve.max(v8[0:r, :], biased))
                step(dve.max_index(i8[0:r, :], v8[0:r, :], biased))
                step(dve.tensor_copy(idx[0:r, i, :], i8[0:r, :]))
                expert_match(i)
                step(tt(oh2[0:r], oh[0:r], sc.unsqueeze(1).broadcast_to([r, MK, NE]), ALU.mult))
                g = gate[0:r, i, 0:MK]
                step(dve.reduce_sum(g, oh2[0:r], AX.X))
                step(dve.reduce_sum(gsum[0:r, 0:1], g, AX.X))
                step(dve.reciprocal(gsum[0:r, 1:2], gsum[0:r, 0:1]))
                ts(g, g, gsum[0:r, 1:2], ROUTED_SCALE, ALU.mult, ALU.mult)
                dve.reduce_sum(sel[0:r, i % 2, :], oh[0:r].rearrange("p k e -> p e k"),
                               AX.X).then_inc(s("sel_ready"), 1)
                dve.wait_ge(s("silu_ready"), i + 1)
                await_bank(dve, ("sg", i))
                h = hsh[0:r, i % 2, :]
                tt(h, h, bank(("sg", i))[0:r, DE:2 * DE], ALU.mult).then_inc(s("hsh_ready"), 1)

            def rank_and_base(i):
                r = rows(i)
                await_bank(dve, ("rk", i))
                dve.tensor_copy(rk[0:r, i, :], bank(("rk", i))[0:r, 0:NE]).then_inc(s("rk_ready"), 1)
                dve.wait_ge(s("sel_ready"), i + 1)
                if i > 0:
                    dve.wait_ge(s("cum_ready"), i)
                tt(cum[0:r, :], cum[0:r, :], sel[0:r, i % 2, :], ALU.add).then_inc(s("cum_ready"), 1)
                dve.wait_ge(s(f"x1_stored{i % 3}"), 16 * (i // 3 + 1))
                f0 = banks.at[("sd", i)][0]
                for j in range(2):
                    await_bank(dve, ("sd", i), j)
                x = x1b[0:r, i % 3, :]
                stt(x, x, ALPHA, psum[0:r, f0:f0 + 2, :].rearrange("p b n -> p (b n)"), ALU.mult,
                    ALU.add).then_inc(s("base_ready"), 1)

            for i in range(NT + 2):
                if i < NT:
                    residual(i)
                if 0 <= i - 1 < NT:
                    route(i - 1)
                if 0 <= i - 2 < NT:
                    rank_and_base(i - 2)

            await_bank(dve, "cnt")
            cn, nb_, bend, base_ = (cnt[:, q_, :] for q_ in range(4))
            dve.tensor_copy(cn, bank("cnt")[:, 0:NE]).then_inc(s("blocks_planned"), 1)
            dve.wait_ge(s("blocks_planned"), 1)
            step(ts(nb_, cn, 63.5, 1.0 / P, ALU.add, ALU.mult))
            step(ts(nb_, nb_, ROUND, None, ALU.add))
            step(ts(nb_, nb_, -ROUND, 1.0, ALU.add, ALU.max))
            step(dve.tensor_tensor_scan(bend, ones[:, 0:NE], nb_, 0.0, ALU.mult, ALU.add))
            step(tt(base_, bend, nb_, ALU.subtract))
            step(ts(base_, base_, float(P), None, ALU.mult))
            step(ts(npair[0:1, 0:1], bend[0:1, NE - 1:NE], 0.5, 0.5, ALU.add, ALU.mult))
            step(ts(npair[0:1, 1:2], npair[0:1, 0:1], ROUND, None, ALU.add))
            ts(npair_i[0:1, 0:1], npair[0:1, 1:2], -ROUND, None, ALU.add)
            ts(npair_i[0:1, 1:2], npair[0:1, 1:2], -ROUND, -1.0, ALU.add, ALU.add).then_inc(s("blocks_planned"), 1)
            step(ts(oh[:, 0, :], bend, bexp[:, 0:1], None, ALU.is_le))
            step(dve.reduce_sum(bexp[:, 1:2], oh[:, 0, :], AX.X))
            ts(bexp_i[:], bexp[:, 1:2], float(NE - 1), None, ALU.min).then_inc(s("blocks_planned"), 1)
            for i in range(NT):
                r = rows(i)
                step(tt(rk[0:r, i, :], rk[0:r, i, :], base_[0:r, :], ALU.add))
                expert_match(i)
                step(tt(oh2[0:r], oh[0:r], rk[0:r, i, :].unsqueeze(1).broadcast_to([r, MK, NE]), ALU.mult))
                step(dve.reduce_sum(slot[0:r, i, 0:MK], oh2[0:r], AX.X))
            dve.tensor_copy(slot_i[:], slot[:])
            step(ts(sblk[:], slot[:], -63.5, 1.0 / P, ALU.add, ALU.mult))
            step(ts(sblk[:], sblk[:], ROUND, None, ALU.add))
            step(ts(sblk[:], sblk[:], -ROUND, None, ALU.add))
            step(stt(sin_[:], sblk[:], -float(P), slot[:], ALU.mult, ALU.add))
            m = 0
            for i in range(NT):
                r = rows(i)
                for k in range(MK):
                    if m >= 2:
                        dve.wait_ge(s("onehot_used"), m - 1)
                    o = onehot[0:r, m % 2, :]
                    ts(o[:, 0:P], iota64[0:r, :], sin_[0:r, i, k:k + 1], None, ALU.is_equal)
                    for q_, v_ in enumerate((tokid[0:r, i:i + 1], gate[0:r, i, k:k + 1])):
                        last = ts(o[:, P + q_ * NBP:P + (q_ + 1) * NBP], iota64[0:r, 0:NBP], sblk[0:r, i, k:k + 1], v_,
                                  ALU.is_equal, ALU.mult)
                    last.then_inc(s("onehot_ready"), 1)
                    m += 1
            await_bank(dve, "tab")
            dve.tensor_copy(tab[:].rearrange("p a b -> p (a b)"), bank("tab")[:, 0:2 * NBP]).then_inc(s("tab_ready"), 1)
            dve.wait_ge(s("tab_ready"), 1)

            n_pairs = dve.value_load(npair_i[0:1, 0:1], min_val=NE // 2, max_val=NBP // 2)

            def take_rows(need, u):
                dve.wait_ge(s("xg_turned1"), need)
                dve.tensor_copy(xgT[u][:, 4:8, :], psum[:, 1, :].rearrange("p (q n) -> p q n", q=4)
                                ).then_inc(s("xgT_ready"), 1)

            ts(tid[0][:], tab[:, 0, 0:1], 1.0, None, ALU.mult).then_inc(s("tid_ready"), 1)
            take_rows(1, 0)
            with dve.Fori(0, n_pairs) as ip:
                for u in range(2):
                    n = ip * 2 + u
                    dve.wait_ge(s(f"y_stored{u}"), ip * 16 + 16)
                    ts(gcol[:, u:u + 1], tab[:, 1, bass.ds(n, 1)], 1.0, None, ALU.mult)
                    ts(tid[1 - u][:], tab[:, 0, bass.ds(n + 1, 1)], 1.0, None, ALU.mult).then_inc(s("tid_ready"), 1)
                    dve.wait_ge(s("esilu_ready"), n + 1)
                    tt(eh[:, 2 + u, :], eh[:, u, :], psum[:, 2, DE:2 * DE], ALU.mult).then_inc(s("eh_ready"), 1)
                    take_rows(n + 2, 1 - u)
                    dve.wait_ge(s("edn_full1"), n + 1)
                    ts(yb[u][:, 512:1024], psum[:, 5 + 2 * u, :], gcol[:, u:u + 1], None,
                       ALU.mult).then_inc(s("y_slot_ready"), 1)

            for i in range(NT):
                r = rows(i)
                x = bas[0:r, i % 2, :]
                dve.wait_ge(s(f"bas_loaded{i % 2}"), 16 * (i // 2 + 1))
                for k in range(MK):
                    m = i * MK + k
                    dve.wait_ge(s(f"part_loaded{m % 8}"), 16 * (m // 8 + 1))
                    tt(x, x, part[0:r, m % 8, :], ALU.add).then_inc(s("part_used"), 1)
                    dve.wait_ge(s("part_used"), m + 1)
                statistics(x, r, NT + i)


_INS = ["x_prompt", "x_sample", "cache_k", "cache_v", "cache_idx_k", "state_ssm_re", "state_ssm_im",
        "w_in", "ssm_a_re", "ssm_a_im", "ssm_log_dt", "ssm_b_re", "ssm_b_im", "ssm_c_re", "ssm_c_im", "ssm_d",
        "w_glu", "w_attn_proj", "w_out", "ln1_g", "ln1_b", "w_router", "router_bias",
        "w_exp_gu", "w_exp_down", "w_sh_gu", "w_sh_down", "ln2_g", "ln2_b"]
_OUTS = [("y_p", (1, SEQ, DM)), ("y_s", (1, DEC, DM)),
         ("k_p", (1, 1, SEQ, NKV, HD)), ("v_p", (1, 1, SEQ, NKV, HD)), ("ik_p", (1, 1, SEQ, HD)),
         ("hre_p", (1, 1, NG, NS)), ("him_p", (1, 1, NG, NS)),
         ("k_s", (1, 1, DEC, NKV, HD)), ("v_s", (1, 1, DEC, NKV, HD)), ("ik_s", (1, 1, DEC, HD)),
         ("hre_s", (1, 1, NG, NS)), ("him_s", (1, 1, NG, NS))]


def rope_table():
    pos = np.zeros(NT * P, np.float32)
    pos[:SEQ] = np.arange(SEQ)
    pos[SEQ:T] = PAST + np.arange(DEC)
    inv = np.float32(500000.0) ** (-np.arange(8, dtype=np.float32) * np.float32(2.0) / np.float32(16.0))
    ang = (pos[:, None] * inv.astype(np.float32)).astype(np.float32)
    return np.stack([np.cos(ang), np.sin(ang)], axis=1).astype(np.float32)


def kernel(**inputs):
    import concourse.bacc as _bacc
    from concourse.bass_utils import run_bass_kernel_spmd as _run

    nc = _bacc.Bacc("TRN2", target_bir_lowering=False, num_devices=1)
    arrays, a, out = {}, {}, {}
    for name in _INS:
        x = np.ascontiguousarray(inputs[name])
        arrays[f"in_{name}"] = x
        a[name] = nc.dram_tensor(f"in_{name}", x.shape, F32, kind="ExternalInput").ap()
    arrays["in_rope_table"] = rope_table()
    a["rope_table"] = nc.dram_tensor("in_rope_table", arrays["in_rope_table"].shape, F32, kind="ExternalInput").ap()
    for name, shape in _OUTS:
        out[name] = nc.dram_tensor(f"out_{name}", shape, F32, kind="ExternalOutput").ap()
    layer_program(nc, a, out)
    r = _run(nc, [arrays], core_ids=[0])
    return tuple(r.results[0][f"out_{name}"] for name, _ in _OUTS)
```

```python
from contextlib import ExitStack

import numpy as np

import concourse.bass as bass
from concourse import mybir

F32, I32, U32 = mybir.dt.float32, mybir.dt.int32, mybir.dt.uint32
ALU, ACT, AX = mybir.AluOpType, mybir.ActivationFunctionType, mybir.AxisListType

P = 128
DM = 1024
SEQ, DEC, PAST = 1024, 64, 2048
T = SEQ + DEC
NT = 9
DK = DM // P
HD, NH, NKV = 64, 8, 2
DS, GC, NG, NS = 512, 16, 32, 64
GP = NG // 2
BL = 8
NJ, NJS = SEQ // BL, DEC // BL
UC = NJ + 1 + NJS
HC = UC + 1
TOPK = 256
NE, MK, DE = 64, 6, 256
EPS = 1e-5
ALPHA = 2.0 ** 0.25
ROUTED_SCALE = 2.5
HID = -1e30
TAKEN = -3e38
KEYS = SEQ + PAST + DEC
NB_MAX = (T * MK) // P + NE
NBP = NB_MAX + 2
TWO_PI = 6.283185307179586
ROUND = 12582912.0


def rows(i):
    return P if i < NT - 1 else DEC


def tok(i):
    return slice(i * P, i * P + rows(i))


def keys(i):
    return (0, P * (i + 1)) if i < NT - 1 else (SEQ, PAST + DEC)


def split(n, m):
    return [(a, min(m, n - a)) for a in range(0, n, m)]


MASK_AT = [sum(keys(j)[1] for j in range(i)) for i in range(NT)]
MASK_W = sum(keys(j)[1] for j in range(NT))
TOK_CHUNKS = [(0, 384), (384, 384), (768, 320)]
CHOOSING = list(range(2, NT))


class Banks:

    def __init__(self):
        self.fills, self.turn, self.at, self.counts, self.reader = [0] * 8, {}, {}, {}, [None] * 8

    def take(self, key, reader, pool, n, value, signals):
        t = (self.turn.get(pool, 0) + n - 1) // n * n % len(pool)
        self.turn[pool] = t + n
        first = pool[t]
        before = [self.reader[b] for b in range(first, first + n)]
        self.at[key] = (first, self.fills[first:first + n])
        if value is None:
            value = self.counts[reader] = self.counts.get(reader, 0) + 1
        for b in range(first, first + n):
            self.reader[b] = (reader, value)
            self.fills[b] += signals
        return first, before


def layer_program(nc, a, out):
    banks = Banks()
    with ExitStack() as ctx:
        def sb(name, shape, dt=F32):
            return ctx.enter_context(nc.sbuf_tensor(name, shape, dt))

        def sem(name):
            return ctx.enter_context(nc.semaphore(name))

        def dram(name, shape, dt=F32):
            return nc.dram_tensor(name, shape, dt, kind="Internal").ap()

        kpad_d = dram("kpad_d", (NG, GC, 15 * GC))
        x1_d = dram("x1_d", (T, DM))
        slots_d = dram("slots_d", (NBP * P, DM))
        blk_d = dram("blk_d", (P, 1), I32)

        psum = ctx.enter_context(nc.psum_tensor("psum", [P, 8, 512], F32))

        arena = sb("arena", [P, 49792])

        def at(off, *shape):
            n = int(np.prod(shape))
            v = arena[:, off:off + n]
            if len(shape) == 1:
                return v
            names = "abcde"[:len(shape)]
            return v.rearrange(f"p ({' '.join(names)}) -> p {' '.join(names)}",
                               **{c: s for c, s in zip(names[1:], shape[1:])})

        xT = at(0, DK, T)
        x1T = xT
        mk = at(8704, MASK_W)
        t1, t2 = at(8704, 2304), at(8704 + 2304, 2304)
        braw, bbar, craw = at(8704 + 4608, 2, GP, GC), at(8704 + 5120, 2, GP, GC), at(8704 + 5632, 2, GP, GC)
        g1 = at(15424, DK, T)
        w_u = at(15424, DK, DS)
        m_op = at(15424, NG, P)
        ca = at(15424 + 4096, 2, GP, 9, GC)
        R = 24128
        uT = at(R, NG, UC)
        hp = at(R + 4384, HC, 2, GP)
        u2 = at(32928, NG, BL, GC)
        u2s = at(37024, NG, BL, GC)
        ba = at(41120, 2, GP, BL, GC)
        bopT = at(45216, 2, GP, P)
        xin = at(45216, 2, DM)
        kpad = at(41120, NG, 15, GC)[0:GC]
        cst = at(14848, 2, 2, P)
        u64 = at(32000, DS)
        w_i = at(32928, DK, 584)
        iqT = at(37600, 4, T - 2 * P)
        ikT = at(40928, KEYS)
        zi = at(44064, 2, 640)
        rel = at(45344, 4, 512)
        cikd = at(47392, 16, P)
        rtmp = at(49440, 4, 10, 8)
        y2 = at(32928, BL, DS)
        y2s = at(37024, BL, DS)
        yT = at(41120, 4, T)
        y64 = at(45472, DS)
        wgs = at(R, 2, 16, P)
        sg = at(R + 4096, 4, 384)
        w_q = at(34816, DK, 768)
        qT = at(41088, 4, T)
        zq = at(45440, 2, 768)
        kT = at(R, NKV, KEYS)
        v_tm = at(30400, 25, P)
        kdup = at(33600, 2, 256)
        ckd = at(46976, 4, 256)
        pr = [at(34816, 2, SEQ), at(34816 + 2 * SEQ, 2, SEQ)]
        pr_s = [at(8704, 2, PAST + DEC), at(34816, 2, PAST + DEC)]
        pT = at(39040, 3, 512)
        zeros = at(40576, 512)
        aT = at(45440, 4, T)
        wap = at(8704, 2, 12, P)
        sga = at(8704 + 3072, 4, 384)
        w_o = at(R, DK, DM)
        xre = at(47104, 2, DM)
        x1 = at(34816, NT, DM)
        ln1 = at(44032, 2, DM)
        w_sg = at(8704, DK, 2 * DE)
        w_sd = at(32320, 2, DM)
        w_r = at(12800, DK, NE)
        hsh = at(13312, 2, DE)
        hst = at(48000, 4, P)
        gcol = sb("gcol", [P, 2])
        sb64 = sb("sb64", [P, NE])
        gsum = sb("gsum", [P, 2])
        hshT = at(13824, 2, DE)
        rk = at(14336, NT, NE)
        cnt = at(14912, 4, NE)
        oh = at(49152, MK, NE)
        oh2 = at(34368, MK, NE)
        ewg = [at(15424, DK, 2 * DE), at(21568, DK, 2 * DE)]
        ewd = [at(15424 + 4096, 2, DM), at(21568 + 4096, 2, DM)]
        xg = [at(0, DM), at(1024, DM)]
        xgT = [at(2048, DK, P), at(3072, DK, P)]
        yb = [at(4096, DM), at(5120, DM)]
        eh = at(6144, 4, DE)
        ehT = [at(7168, 2, P), at(7424, 2, P)]
        onehot = at(27712, 12, P + 2 * NBP)
        part = at(15424, 8, DM)
        ln2 = at(10752, 2, DM)

        ident = sb("ident", [P, P])
        tri = sb("tri", [P, P])
        ones = sb("ones", [P, P])
        iota64 = sb("iota64", [P, P])
        rope = sb("rope", [P, NT, 2, 8])
        pst = sb("pst", [P, P])
        ldt = sb("ldt", [P, 2])
        carry = sb("carry", [1, 1])
        par = sb("par", [P, 5, GP])
        sm = sb("sm", [P, 16, GP])
        pw = sb("pw", [P, 2, 9, GP])
        a8 = sb("a8", [P, 2, 2, GP])
        sct = sb("sct", [P, 2, 2, GP])
        dsk = sb("dsk", [GC, NG])
        iws = sb("iws", [P, NT, 8])
        best = sb("best", [P, 8])
        mx = sb("mx", [P, 2, 8])
        mx1 = sb("mx1", [P, 2])
        nbias = sb("nbias", [P, 2, 2])
        rsum = sb("rsum", [P, 2, 2])
        rinv = sb("rinv", [P, 2, 2])
        stats = sb("stats", [P, 2, 6])
        mv = sb("mv", [P, 2])
        lst = sb("lst", [P, 4])
        rsc = sb("rsc", [P, 2, NE])
        rbias = sb("rbias", [P, NE])
        v8 = sb("v8", [P, 8])
        i8 = sb("i8", [P, 8], U32)
        idx = sb("idx", [P, NT, 8])
        gate = sb("gate", [P, NT, 8])
        sel = sb("sel", [P, 2, NE])
        cum = sb("cum", [P, NE])
        slot = sb("slot", [P, NT, 8])
        slot_i = sb("slot_i", [P, NT, 8], I32)
        sblk = sb("sblk", [P, NT, 8])
        sin_ = sb("sin_", [P, NT, 8])
        tokid = sb("tokid", [P, NT])
        tab = sb("tab", [P, 2, NBP])
        tid = [sb(f"tid{u}", [P, 1], I32) for u in range(2)]
        bexp = sb("bexp", [P, 4])
        bexp_i = sb("bexp_i", [P, 1], I32)
        brow = sb("brow", [1, P], I32)
        npair = sb("npair", [1, 8])
        npair_i = sb("npair_i", [1, 8], I32)

        full = [sem(f"bank_full{b}") for b in range(8)]
        dve_step = sem("dve_step")
        pool_step = sem("pool_step")
        S = {}

        def s(name):
            if name not in S:
                S[name] = sem(name)
            return S[name]

        def bank(key, j=0):
            f, c = banks.at[key]
            return psum[:, f + j, :]

        def await_bank(eng, key, j=0):
            f, c = banks.at[key]
            eng.wait_ge(full[f + j], c[j] + 1)

        block = ctx.enter_context(nc.Block())
        planned_in = lambda i: range(max(0, 9 * (i - 3)), max(0, min(NT * MK, 9 * (i - 2))))
        score_keys = lambda i: [(i, a0, n0) for a0, n0 in split(keys(i)[1], 512)]
        ATT = [(i, hp_) for i in range(NT) for hp_ in range(NH // 2)]
        key_tiles = lambda i: split(keys(i)[1], P)
        key_groups = lambda i: split(len(key_tiles(i)), 2)
        group_no = {}
        for n, (i, _) in enumerate(ATT):
            for q in range(len(key_groups(i))):
                group_no[n, q] = len(group_no)

        def probs_at(n):
            return pr[n % 2] if ATT[n][0] < NT - 1 else pr_s[n % 2]

        score_no = {}
        for i in CHOOSING:
            for _, c0, w in score_keys(i):
                for h in range(NH):
                    score_no[i, c0, h] = len(score_no)

        @block.tensor
        def _(pe):
            def claim(key, reader, value=None, pool=tuple(range(8)), n=1, signals=1):
                first, before = banks.take(key, reader, pool, n, value, signals)
                for name, v in {b for b in before if b}:
                    pe.wait_ge(s(name), v)
                return first

            def filled(ins, key, j=0):
                ins.then_inc(full[banks.at[key][0] + j], 1)

            mm, tr = pe.matmul, pe.transpose

            pe.wait_ge(s("constants"), 8)
            for i in range(NT):
                r = rows(i)
                pe.wait_ge(s(f"x_loaded{i % 2}"), 16 * (i // 2 + 1))
                for half in range(2):
                    b = claim(("x", i, half), "xT_ready")
                    for q in range(4):
                        k = 4 * half + q
                        last = tr(psum[:, b, q * P:q * P + r], xin[0:r, i % 2, k::DK], ident[0:r, 0:r])
                    filled(last, ("x", i, half))
            pe.wait_ge(s("param_rows"), 1)
            b = claim("par", "par_ready")
            filled(tr(psum[:, b, 0:80], pst[0:80, :], ident[0:80, 0:80]), "par")
            pe.wait_ge(s("xT_ready"), 2 * NT)
            pe.wait_ge(s("w_u_loaded"), 16)
            for t in range(BL):
                b = claim(("u", t), "u2_ready")
                for k in range(DK):
                    last = mm(psum[:, b, :], xT[:, k, t:SEQ:BL], w_u[:, k, :], start=k == 0, stop=k == DK - 1)
                filled(last, ("u", t))
            b = claim("u_s", "u64_ready")
            for k in range(DK):
                last = mm(psum[0:DEC, b, :], xT[:, k, SEQ:T], w_u[:, k, :], start=k == 0, stop=k == DK - 1)
            filled(last, "u_s")
            pe.wait_ge(s("c_loaded"), 16 * 8)
            b = claim("c", "c_turned")
            for part_ in range(2):
                for e in range(2):
                    last = tr(psum[:, b, (2 * part_ + e) * P:(2 * part_ + e + 1) * P], cst[:, part_, e, :], ident[:])
            filled(last, "c")
            pe.wait_ge(s("u2_ready"), BL)
            for q4 in range(8):
                b = claim(("ut", q4), "uT_ready")
                for q in range(4):
                    g = 4 * q4 + q
                    last = tr(psum[:, b, q * P:(q + 1) * P], u2[:, g, :, :].rearrange("p t c -> p (t c)"), ident[:])
                filled(last, ("ut", q4))
            pe.wait_ge(s("u2s_ready"), 16 * NJS)
            b = claim("uts", "uT_ready")
            for g in range(NG):
                last = tr(psum[:, b, g * NJS:(g + 1) * NJS],
                          u2s[0:NJS, g, :, :].rearrange("p t c -> p (t c)"), ident[0:NJS, 0:NJS])
            filled(last, "uts")
            pe.wait_ge(s("s5_operators"), 2)
            for q4 in range(8):
                b = claim(("bt", q4), "bopT_ready")
                for q in range(4):
                    n = 4 * q4 + q
                    last = tr(psum[:, b, q * P:(q + 1) * P],
                              ba[:, n // GP, n % GP, :, :].rearrange("p t c -> p (t c)"), ident[:])
                filled(last, ("bt", q4))
            pe.wait_ge(s("uT_ready"), 9)
            pe.wait_ge(s("bopT_ready"), 8)
            for gp in range(GP):
                b = claim(("b", gp), "b_ready")
                for part_ in range(2):
                    for e in range(2):
                        last = mm(psum[e * 64:(e + 1) * 64, b, part_ * UC:(part_ + 1) * UC],
                                  bopT[:, part_, gp, e * 64:(e + 1) * 64], uT[:, 2 * gp + e, :],
                                  start=True, stop=True)
                filled(last, ("b", gp))
            pe.wait_ge(s("s5_operators"), 3)
            for q4 in range(4):
                for e in range(2):
                    claim(("k", q4, e), "k_ready")
                for q in range(4):
                    for e in range(2):
                        b, _ = banks.at["k", q4, e]
                        for part_ in range(2):
                            last = mm(psum[0:GC, b, q * P:(q + 1) * P], bbar[e * 64:(e + 1) * 64, part_, 4 * q4 + q, :],
                                      ca[e * 64:(e + 1) * 64, part_, 4 * q4 + q, 0:BL, :].rearrange("p t c -> p (t c)"),
                                      start=part_ == 0, stop=part_ == 1)
                        if q == 3:
                            filled(last, ("k", q4, e))

            def z_index(i):
                r = rows(i)
                if i == 0:
                    pe.wait_ge(s("w_i_loaded"), 16)
                for key, c0, n in (("iq", 0, 512), ("ik", 512, 72)):
                    b = claim((key, i), "zi_ready", i + 1)
                    for k in range(DK):
                        last = mm(psum[0:r, b, 0:n], xT[:, k, tok(i)], w_i[:, k, c0:c0 + n],
                                  start=k == 0, stop=k == DK - 1)
                    filled(last, (key, i))

            def turn_index(i):
                r = rows(i)
                pe.wait_ge(s("zi_roped"), i + 1)
                b = claim(("ikT", i), "ikT_ready")
                filled(tr(psum[:, b, 0:r], zi[0:r, i % 2, 512:640], ident[0:r, 0:r]), ("ikT", i))
                if i in CHOOSING:
                    b = claim(("iqT", i), "iqT_ready")
                    for q in range(4):
                        last = tr(psum[:, b, q * P:q * P + r], zi[0:r, i % 2, q * P:(q + 1) * P], ident[0:r, 0:r])
                    filled(last, ("iqT", i))

            def scores(i):
                r = rows(i)
                pe.wait_ge(s("ikT_ready"), i + 1)
                if i == NT - 1:
                    pe.wait_ge(s("cik_ready"), 4)
                pe.wait_ge(s("iqT_ready"), i - 1)
                for _, c0, n in score_keys(i):
                    for h in range(NH):
                        b = claim(("s", i, c0, h), "rel_ready")
                        e = h % 2
                        filled(mm(psum[0:r, b, 0:n],
                                  iqT[e * 64:(e + 1) * 64, h // 2, (i - 2) * P:(i - 2) * P + r],
                                  ikT[e * 64:(e + 1) * 64, keys(i)[0] + c0:keys(i)[0] + c0 + n],
                                  start=True, stop=True), ("s", i, c0, h))

            for i in range(NT):
                z_index(i)
                if i > 0:
                    turn_index(i - 1)
                    if i - 1 in CHOOSING:
                        scores(i - 1)
                if i == 7:
                    pe.wait_ge(s("cik_loaded"), 32)
                    for q4 in range(4):
                        b = claim(("cik", q4), "cik_ready")
                        for q in range(4):
                            last = tr(psum[:, b, q * P:(q + 1) * P], cikd[:, 4 * q4 + q, :], ident[:])
                        filled(last, ("cik", q4))
            turn_index(NT - 1)
            scores(NT - 1)

            pe.wait_ge(s("m_loaded"), 16 * BL)
            pe.wait_ge(s("state_ready"), 1)
            for sample in range(2):
                r, j0 = (NJS, NJ + 1) if sample else (NJ, 0)
                for q4 in range(4):
                    for e in range(2):
                        claim(("y", sample, q4, e), "y2s_ready" if sample else "y_ready")
                    for q in range(4):
                        gp = 4 * q4 + q
                        o = [psum[0:r, banks.at["y", sample, q4, e][0], q * P:(q + 1) * P] for e in range(2)]
                        for e in range(2):
                            mm(o[e], uT[:, 2 * gp + e, j0:j0 + r], m_op[:, 2 * gp + e, :], start=True, stop=False)
                        for part_ in range(2):
                            for e in range(2):
                                last = mm(o[e], hp[e * 64:(e + 1) * 64, j0:j0 + r, part_, gp],
                                          ca[e * 64:(e + 1) * 64, part_, gp, 1:9, :].rearrange("p t c -> p (t c)"),
                                          start=False, stop=part_ == 1)
                                if q == 3 and part_ == 1:
                                    filled(last, ("y", sample, q4, e))
            pe.wait_ge(s("y_ready"), 8)
            b = claim("hst", "states_ready")
            for q in range(4):
                last = tr(psum[0:GP, b, q * P:(q + 1) * P], hp[:, (NJ, HC - 1)[q // 2], q % 2, :], ident[:])
            filled(last, "hst")
            for t in range(BL):
                b = claim(("yt", t), "yT_ready")
                for q in range(4):
                    last = tr(psum[:, b, q * P:(q + 1) * P], y2[:, t, q * P:(q + 1) * P], ident[:])
                filled(last, ("yt", t))
            pe.wait_ge(s("y64_ready"), 16 * NJS)
            b = claim("yts", "yT_ready")
            for q in range(4):
                last = tr(psum[:, b, q * DEC:(q + 1) * DEC], y64[0:DEC, q * P:(q + 1) * P], ident[0:DEC, 0:DEC])
            filled(last, "yts")

            pe.wait_ge(s("yT_ready"), 9)
            for d in range(DK):
                pe.wait_ge(s(f"wgs_loaded{d % 2}"), 48 * (d // 2 + 1))
                for c, (t0, n) in enumerate(TOK_CHUNKS):
                    for key, w0, src, nk in (("val", 8, yT, 4), ("glu", 12, yT, 4), ("gs", 0, xT, DK)):
                        b = claim((key, d, c), "val_used" if key == "val" else "sg_ready")
                        for k in range(nk):
                            last = mm(psum[:, b, 0:n], wgs[:, d % 2, w0 + k, :], src[:, k, t0:t0 + n],
                                      start=k == 0, stop=k == nk - 1)
                        filled(last, (key, d, c))

            def z_qkv(i):
                r = rows(i)
                if i == 0:
                    pe.wait_ge(s("w_q_loaded"), 16)
                for key, c0, n in (("q", 0, 512), ("kv", 512, 256)):
                    b = claim((key, i), "zq_ready", i + 1)
                    for k in range(DK):
                        last = mm(psum[0:r, b, 0:n], xT[:, k, tok(i)], w_q[:, k, c0:c0 + n],
                                  start=k == 0, stop=k == DK - 1)
                    filled(last, (key, i))

            def turn_qkv(i):
                r = rows(i)
                pe.wait_ge(s("zq_roped"), i + 1)
                b = claim(("qT", i), "qT_ready")
                for q in range(4):
                    last = tr(psum[:, b, q * P:q * P + r], zq[0:r, i % 2, q * P:(q + 1) * P], ident[0:r, 0:r])
                filled(last, ("qT", i))
                b = claim(("kT", i), "qT_ready")
                for q in range(2):
                    last = tr(psum[:, b, q * P:q * P + r], kdup[0:r, i % 2, q * P:(q + 1) * P], ident[0:r, 0:r])
                filled(last, ("kT", i))

            for i in range(NT):
                z_qkv(i)
                if i > 0:
                    turn_qkv(i - 1)
            turn_qkv(NT - 1)
            for j in range(16):
                pe.wait_ge(s(f"ck_loaded{j % 4}"), 32 * (j // 4 + 1))
                b = claim(("ck", j), "ckT_ready")
                for q in range(2):
                    last = tr(psum[:, b, q * P:(q + 1) * P], ckd[:, j % 4, q * P:(q + 1) * P], ident[:])
                filled(last, ("ck", j))

            LOGITS, TURNED, OUTS = (0, 1, 2, 3), (4, 5), (6, 7)

            def logits(n):
                i, hp_ = ATT[n]
                r = rows(i)
                if n == 0:
                    pe.wait_ge(s("qT_ready"), 2 * NT)
                    pe.wait_ge(s("ckT_ready"), 16)
                    pe.wait_ge(s("cv_loaded"), 16)
                for c0, m in split(keys(i)[1], 512):
                    for e in range(2):
                        b = claim(("l", n, c0, e), "masked", pool=LOGITS)
                        k0 = keys(i)[0] + c0
                        filled(mm(psum[0:r, b, 0:m], qT[e * 64:(e + 1) * 64, hp_, tok(i)],
                                  kT[e * 64:(e + 1) * 64, hp_ // 2, k0:k0 + m], start=True, stop=True),
                               ("l", n, c0, e))

            def turn_probs(n, q):
                i, _ = ATT[n]
                r = rows(i)
                if q == 0:
                    pe.wait_ge(s("probs_scaled"), 2 * (n + 1))
                b = claim(("p", n, q), "pT_ready", pool=TURNED)
                g0, gn = key_groups(i)[q]
                for c in range(gn):
                    k0, w = key_tiles(i)[g0 + c]
                    for e in range(2):
                        last = tr(psum[0:w, b, (2 * c + e) * P:(2 * c + e) * P + r], probs_at(n)[0:r, e, k0:k0 + w],
                                  ident[0:r, 0:r])
                filled(last, ("p", n, q))

            def values(n, q):
                i, hp_ = ATT[n]
                r, nk = rows(i), keys(i)[1]
                if hp_ == 0 and q == 0:
                    claim(("o", i), "aT_ready", pool=OUTS, signals=0)
                gq = group_no[n, q]
                g0, gn = key_groups(i)[q]
                pe.wait_ge(s("pT_ready"), gq + 1)
                for c in range(gn):
                    k0, w = key_tiles(i)[g0 + c]
                    v0 = k0 // P + (8 if i == NT - 1 else 0)
                    for e in range(2):
                        o = psum[e * 64:(e + 1) * 64, banks.at[("o", i)][0], hp_ * P:hp_ * P + r]
                        last = mm(o, v_tm[0:w, v0, (hp_ // 2) * HD:(hp_ // 2 + 1) * HD],
                                  pT[0:w, gq % 3, (2 * c + e) * P:(2 * c + e) * P + r],
                                  start=k0 == 0, stop=k0 + w == nk)
                last.then_inc(s("pT_used"), 1)

            logits(0)
            groups = list(group_no)
            for m, (n, q) in enumerate(groups):
                if q == 0 and n + 1 < len(ATT):
                    logits(n + 1)
                turn_probs(n, q)
                if m > 0:
                    values(*groups[m - 1])
            values(*groups[-1])

            pe.wait_ge(s("aT_ready"), NT)
            for d in range(DK):
                pe.wait_ge(s(f"wap_loaded{d % 2}"), 32 * (d // 2 + 1))
                for c, (t0, n) in enumerate(TOK_CHUNKS):
                    for key, w0, src, nk in (("ga", 0, xT, DK), ("ao", 8, aT, 4)):
                        b = claim((key, d, c), "sga_ready" if key == "ga" else "ao_used")
                        for k in range(nk):
                            last = mm(psum[:, b, 0:n], wap[:, d % 2, w0 + k, :], src[:, k, t0:t0 + n],
                                      start=k == 0, stop=k == nk - 1)
                        filled(last, (key, d, c))

            def project(i):
                r = rows(i)
                claim(("wo", i), "res_ready", n=2)
                for j in range(2):
                    for k in range(DK):
                        last = mm(psum[0:r, banks.at[("wo", i)][0] + j, :], g1[:, k, tok(i)],
                                  w_o[:, k, j * 512:(j + 1) * 512], start=k == 0, stop=k == DK - 1)
                    filled(last, ("wo", i), j)

            def turn_x1(i):
                r = rows(i)
                pe.wait_ge(s("x1_ready"), i + 1)
                for half in range(2):
                    b = claim(("x1", i, half), "x1T_ready")
                    for q in range(4):
                        last = tr(psum[:, b, q * P:q * P + r], x1[0:r, i, 4 * half + q::DK], ident[0:r, 0:r])
                    filled(last, ("x1", i, half))

            def project_x1(i, key, w, n, reader):
                r = rows(i)
                b = claim((key, i), reader)
                for k in range(DK):
                    last = mm(psum[0:r, b, 0:n], x1T[:, k, tok(i)], w[:, k, :], start=k == 0, stop=k == DK - 1)
                filled(last, (key, i))

            def rank(i):
                r = rows(i)
                pe.wait_ge(s("sel_ready"), i + 1)
                b = claim(("rk", i), "rk_ready")
                if i > 0:
                    pe.wait_ge(s("cum_ready"), i)
                    mm(psum[0:r, b, 0:NE], ones[:, 0:r], cum[:], start=True, stop=False)
                filled(mm(psum[0:r, b, 0:NE], tri[0:r, 0:r], sel[0:r, i % 2, :], start=i == 0, stop=True), ("rk", i))

            def turn_hidden(i):
                r = rows(i)
                pe.wait_ge(s("hsh_ready"), i + 1)
                b = claim(("ht", i), "hshT_ready", pool=PLANNING)
                for k in range(2):
                    last = tr(psum[:, b, k * P:k * P + r], hsh[0:r, i % 2, k::2], ident[0:r, 0:r])
                filled(last, ("ht", i))

            def shared_down(i):
                r = rows(i)
                pe.wait_ge(s("hshT_ready"), i + 1)
                claim(("sd", i), "base_ready", n=2, pool=PLANNING)
                for j in range(2):
                    for k in range(2):
                        last = mm(psum[0:r, banks.at[("sd", i)][0] + j, :], hshT[:, i % 2, k * P:k * P + r],
                                  w_sd[:, k, j * 512:(j + 1) * 512], start=k == 0, stop=k == 1)
                    filled(last, ("sd", i), j)

            pe.wait_ge(s("mixed_ready"), DK * 3)
            pe.wait_ge(s("w_o_loaded"), 16)
            for i in range(NT + 2):
                if i < NT:
                    project(i)
                if 0 <= i - 1 < NT:
                    turn_x1(i - 1)
                if 0 <= i - 2 < NT:
                    rank(i - 2)
                if 0 <= i - 1 < NT:
                    pe.wait_ge(s("x1T_ready"), 2 * i)
                    if i == 1:
                        pe.wait_ge(s("w_s_loaded"), 64)
                    project_x1(i - 1, "r", w_r, NE, "rsc_ready")

            PLANNING = (0, 1, 2, 3, 4, 5)
            claim("tab", "tab_ready", pool=(6,))
            for i in range(NT + 1):
                if i < NT:
                    b = claim(("sg", i), "hsh_ready", pool=PLANNING)
                    for k in range(DK):
                        last = mm(psum[0:rows(i), b, 0:2 * DE], x1T[:, k, tok(i)], w_sg[:, k, :],
                                  start=k == 0, stop=k == DK - 1)
                    filled(last, ("sg", i))
                if i == 0:
                    pe.wait_ge(s("cum_ready"), NT)
                    b = claim("cnt", "blocks_planned", 1, pool=(7,))
                    filled(mm(psum[:, b, 0:NE], ones[:], cum[:], start=True, stop=True), "cnt")
                else:
                    turn_hidden(i - 1)
                    for m in planned_in(i - 1):
                        r, o = rows(m // MK), onehot[:, m % 12, :]
                        pe.wait_ge(s("onehot_ready"), m + 1)
                        pe.wait_ge(s("token_ready"), m + 1)
                        last = mm(psum[:, banks.at["tab"][0], 0:2 * NBP], o[0:r, 0:P], o[0:r, P:P + 2 * NBP],
                                  start=m == 0, stop=m == NT * MK - 1)
                        if m < NT * MK - 1:
                            last.then_inc(s("onehot_used"), 1)
                        else:
                            filled(last, "tab")
                    shared_down(i - 1)

            pe.wait_ge(s("blocks_planned"), 2)
            last_pair = pe.value_load(npair_i[0:1, 1:2], min_val=NE // 2 - 1, max_val=NBP // 2 - 1)

            def turn_rows(u, loads):
                pe.wait_ge(s(f"xg_loaded{u}"), loads)
                for half in range(2):
                    for q in range(4):
                        last = tr(psum[:, half, q * P:(q + 1) * P], xg[u][:, 4 * half + q::DK], ident[:])
                    last.then_inc(s(f"xg_turned{half}"), 1)

            def gate_and_up(u, blocks, loads):
                pe.wait_ge(s("xgT_ready"), blocks * 2)
                pe.wait_ge(s(f"ewg_loaded{u}"), loads)
                for k in range(DK):
                    last = mm(psum[:, 2, :], xgT[u][:, k, :], ewg[u][:, k, :], start=k == 0, stop=k == DK - 1)
                last.then_inc(s("egu_full"), 1)

            def turn_eh(u, blocks):
                pe.wait_ge(s("eh_ready"), blocks)
                for k in range(2):
                    last = tr(psum[:, 3, k * P:(k + 1) * P], eh[:, 2 + u, k::2], ident[:])
                last.then_inc(s("eh_turned"), 1)

            def down(u, blocks, loads):
                pe.wait_ge(s("ehT_ready"), blocks)
                pe.wait_ge(s(f"ewd_loaded{u}"), loads)
                for j in range(2):
                    for k in range(2):
                        last = mm(psum[:, 4 + 2 * u + j, :], ehT[u][:, k, :], ewd[u][:, k, j * 512:(j + 1) * 512],
                                  start=k == 0, stop=k == 1)
                    last.then_inc(s(f"edn_full{j}"), 1)

            turn_rows(0, 16)
            gate_and_up(0, 1, 16)
            turn_rows(1, 16)
            turn_eh(0, 1)
            with pe.Fori(0, last_pair) as ip:
                for u in range(2):
                    n = ip * 2 + u
                    gate_and_up(1 - u, n + 2, ip * 16 + 16 + 16 * u)
                    turn_rows(u, ip * 16 + 32)
                    down(u, n + 1, ip * 16 + 16)
                    turn_eh(1 - u, n + 2)
            gate_and_up(1, last_pair * 2 + 2, last_pair * 16 + 16)
            down(0, last_pair * 2 + 1, last_pair * 16 + 16)
            turn_eh(1, last_pair * 2 + 2)
            down(1, last_pair * 2 + 2, last_pair * 16 + 16)

        @block.sync
        def _(sp):
            def ld(dst, src, name, small=False):
                sp.dma_start(dst, src, allow_slow_non_contiguous=small).then_inc(s(name), 16)

            def load_x(i):
                if i >= 2:
                    await_bank(sp, ("x", i - 2, 1))
                r = rows(i)
                src = a["x_prompt"][0, tok(i), :] if i < NT - 1 else a["x_sample"][0]
                ld(xin[0:r, i % 2, :], src, f"x_loaded{i % 2}")

            w_in = a["w_in"][0]
            w_glu = a["w_glu"][0]
            by_chunk = lambda w: w.rearrange("(p k) f -> p k f", k=DK)
            load_x(0)
            load_x(1)
            flat = lambda ap: ap.rearrange("(q e) n -> q (e n)", e=2)
            for q, name in enumerate(("ssm_a_re", "ssm_a_im")):
                ld(pst[q * GP:(q + 1) * GP, :], flat(a[name][0]), "params_loaded")
            for q, name in enumerate(("state_ssm_re", "state_ssm_im")):
                ld(pst[(q + 2) * GP:(q + 3) * GP, :], flat(a[name][0, 0]), "params_loaded")
            ld(ldt[64:80, :], a["ssm_log_dt"][0].rearrange("(q e) -> q e", e=2), "params_loaded")
            ld(w_u, by_chunk(w_in[:, 0:DS]), "w_u_loaded")
            for q, name in enumerate(("ssm_b_re", "ssm_b_im")):
                ld(braw[:, q, :, :], a[name][0].rearrange("(q e) n c -> (e n) q c", e=2), "b_loaded")
            for q, name in enumerate(("ssm_c_re", "ssm_c_im")):
                for half in range(2):
                    for g8 in range(8):
                        g = 16 * half + 2 * g8
                        ld(cst[g8 * GC:(g8 + 1) * GC, q, half, :].rearrange("c (e n) -> c e n", e=2),
                           a[name][0, g:g + 2].rearrange("e c n -> c e n"), "c_loaded")
            ld(dsk[:], a["ssm_d"][0].rearrange("(g c) -> c g", c=GC), "d_loaded", small=True)
            ld(rope[:], a["rope_table"].rearrange("(t p) a f -> p t a f", p=P), "rope_loaded")
            for i in range(2, NT):
                load_x(i)
            sp.wait_ge(s("u64_ready"), 1)
            for t in range(BL):
                ld(u2s[0:NJS, :, t, :], u64[t:DEC:BL, :].rearrange("p (g c) -> p g c", c=GC), "u2s_ready")
            sp.wait_ge(s("uT_ready"), 9)
            ld(w_i, by_chunk(w_in[:, 1280:1864]), "w_i_loaded")
            sp.wait_ge(s("s5_operators"), 4)
            ld(kpad_d.rearrange("g c (l o) -> c g l o", o=GC), kpad, "kpad_stored")
            sp.wait_ge(s("kpad_stored"), 16)
            for t in range(BL):
                ld(m_op[t * GC:(t + 1) * GC, :, :],
                   kpad_d.rearrange("g c l -> c g l")[:, :, (7 - t) * GC:(7 - t) * GC + P], "m_loaded")
            for rep in range(2):
                ld(cikd[:, :, rep * HD:(rep + 1) * HD], a["cache_idx_k"][0, 0].rearrange("(j p) d -> p j d", p=P),
                   "cik_loaded")
            for i in range(NT):
                sp.wait_ge(s("zi_roped"), i + 1)
                dst = out["ik_p"][0, 0, tok(i), :] if i < NT - 1 else out["ik_s"][0, 0]
                ld(dst, zi[0:rows(i), i % 2, 512:576], f"ik_stored{i % 2}")
            sp.wait_ge(s("y2s_ready"), 8)
            sp.wait_ge(s("rel_used"), len(score_no))
            for t in range(BL):
                ld(y64[t:DEC:BL, :], y2s[0:NJS, t, :], "y64_ready")
            sp.wait_ge(s("states_ready"), 1)
            for q, key in enumerate(("hre_p", "him_p")):
                ld(out[key][0, 0].rearrange("(q e) n -> q (e n)", e=2), hst[0:16, q, :], "h_stored")
            for q, key in enumerate(("hre_s", "him_s")):
                ld(out[key][0, 0].rearrange("(q e) n -> q (e n)", e=2), hst[0:16, 2 + q, :], "h_stored")

            def load_wgs(d):
                if d >= 2:
                    await_bank(sp, ("gs", d - 2, 2))
                u, c = d % 2, slice(d * P, (d + 1) * P)
                ld(wgs[:, u, 0:8, :], by_chunk(w_in[:, 1864 + d * P:1864 + (d + 1) * P]), f"wgs_loaded{u}")
                ld(wgs[:, u, 8:12, :], w_glu[:, c].rearrange("(k p) f -> p k f", p=P), f"wgs_loaded{u}")
                ld(wgs[:, u, 12:16, :], w_glu[:, DM + d * P:DM + (d + 1) * P].rearrange("(k p) f -> p k f", p=P),
                   f"wgs_loaded{u}")

            load_wgs(0)
            load_wgs(1)
            sp.wait_ge(s("yT_ready"), 9)
            ld(w_q, by_chunk(w_in[:, 512:1280]), "w_q_loaded")
            ld(v_tm[:, 8:24, :], a["cache_v"][0, 0].rearrange("(j p) h d -> p j (h d)", p=P), "cv_loaded")
            for d in range(2, DK):
                load_wgs(d)
            for i in range(NT):
                r = rows(i)
                sp.wait_ge(s("zq_roped"), i + 1)
                kd, vd = (out["k_p"][0, 0, tok(i)], out["v_p"][0, 0, tok(i)]) if i < NT - 1 else \
                    (out["k_s"][0, 0], out["v_s"][0, 0])
                ld(kd.rearrange("t h d -> t (h d)"), zq[0:r, i % 2, 512:640], f"k_stored{i % 2}")
                ld(vd.rearrange("t h d -> t (h d)"), v_tm[0:r, i if i < NT - 1 else 24, :], "v_stored")
            ck = a["cache_k"][0, 0].rearrange("(j p) h d -> j p h d", p=P)
            for j in range(16):
                if j >= 4:
                    await_bank(sp, ("ck", j - 4))
                for rep in range(2):
                    ld(ckd[:, j % 4, :].rearrange("p (h r d) -> p h r d", h=2, r=2)[:, :, rep, :], ck[j],
                       f"ck_loaded{j % 4}")

            sp.wait_ge(s("zeros_ready"), 1)
            for j in range(2):
                ld(slots_d[NE * P:, j * 512:(j + 1) * 512].rearrange("(b p) f -> p b f", p=P),
                   zeros.unsqueeze(1).broadcast_to([P, NBP - NE, 512]), "slots_cleared")
            w_ap = a["w_attn_proj"][0]

            def load_wap(d):
                if d >= 2:
                    await_bank(sp, ("ao", d - 2, 2))
                u = d % 2
                ld(wap[:, u, 0:8, :], by_chunk(w_in[:, 2888 + d * P:2888 + (d + 1) * P]), f"wap_loaded{u}")
                ld(wap[:, u, 8:12, :], w_ap[:, d * P:(d + 1) * P].rearrange("(k p) f -> p k f", p=P),
                   f"wap_loaded{u}")

            sp.wait_ge(s("pT_ready"), group_no[len(ATT) - 2, len(key_groups(NT - 1)) - 1] + 1)
            load_wap(0)
            load_wap(1)
            sp.wait_ge(s("aT_ready"), NT)
            ld(w_o, a["w_out"][0].rearrange("(k p) f -> p k f", p=P), "w_o_loaded")
            ld(w_sd, a["w_sh_down"][0].rearrange("(p k) f -> p k f", k=2), "w_s_loaded")
            for d in range(2, DK):
                load_wap(d)

            def load_xre(i):
                if i >= 2:
                    sp.wait_ge(s("normed"), i - 1)
                src = a["x_prompt"][0, tok(i), :] if i < NT - 1 else a["x_sample"][0]
                ld(xre[0:rows(i), i % 2, :], src, f"xre_loaded{i % 2}")

            sp.wait_ge(s("mixed_ready"), 3 * DK)
            load_xre(0)
            load_xre(1)
            for q, name in enumerate(("ln1_g", "ln1_b")):
                ld(ln1[:, q, :], a[name].broadcast_to([P, DM]), "ln1_loaded")
            ld(w_sg, by_chunk(a["w_sh_gu"][0]), "w_s_loaded")
            ld(w_r, by_chunk(a["w_router"][0]), "w_s_loaded")
            ld(rbias[:], a["router_bias"].broadcast_to([P, NE]), "w_s_loaded")
            for i in range(NT):
                if i >= 2:
                    load_xre(i)
                sp.wait_ge(s("x1_ready"), i + 1)
                ld(x1_d[tok(i), :], x1[0:rows(i), i, :], "x1_stored")

            sp.wait_ge(s("blocks_planned"), 3)
            ld(blk_d, bexp_i[:], "blk_stored")
            sp.wait_ge(s("blk_stored"), 16)
            ld(brow[:], blk_d.rearrange("p a -> a p"), "blk_stored")
            sp.wait_ge(s("blk_stored"), 32)
            sp.wait_ge(s("blocks_planned"), 2)
            last_pair = sp.value_load(npair_i[0:1, 1:2], min_val=NE // 2 - 1, max_val=NBP // 2 - 1)

            def expert(n):
                return sp.value_load(brow[0:1, bass.ds(n, 1)], min_val=0, max_val=NE - 1)

            def load_gu(e, u):
                ld(ewg[u], a["w_exp_gu"][0, bass.ds(e, 1)].rearrange("a (p k) f -> (a p) k f", k=DK), f"ewg_loaded{u}")

            def load_dn(e, u):
                ld(ewd[u], a["w_exp_down"][0, bass.ds(e, 1)].rearrange("a (p k) f -> (a p) k f", k=2),
                   f"ewd_loaded{u}")

            for u in range(2):
                e = expert(u)
                load_gu(e, u)
                load_dn(e, u)
            sp.wait_ge(s("egu_full"), 1)
            load_gu(expert(2), 0)
            with sp.Fori(0, last_pair) as ip:
                for u in range(2):
                    n = ip * 2 + u
                    e, after = expert(n + 2), expert(n + 3)
                    sp.wait_ge(s("egu_full"), n + 2)
                    load_gu(after, 1 - u)
                    sp.wait_ge(s("edn_full1"), n + 1)
                    load_dn(e, u)
            for q, name in enumerate(("ln2_g", "ln2_b")):
                ld(ln2[:, q, :], a[name].broadcast_to([P, DM]), "ln2_loaded")
            sp.wait_ge(s("ewg_loaded0"), last_pair * 16 + 32)
            for u in range(2):
                sp.wait_ge(s(f"y_stored{u}"), last_pair * 16 + 32)
            sp.nop().then_inc(s("slots_done"), 1)

            for i in range(NT):
                sp.wait_ge(s("out_ready"), i + 1)
                ld(out["y_p"][0, tok(i), :] if i < NT - 1 else out["y_s"][0], x1[0:rows(i), i, :], "out_stored")
            sp.wait_ge(s("out_stored"), 16 * NT)
            sp.wait_ge(s("v_stored"), 16 * NT)
            sp.wait_ge(s("k_stored0"), 16 * 5)
            sp.wait_ge(s("k_stored1"), 16 * 4)
            sp.wait_ge(s("ik_stored0"), 16 * 5)
            sp.wait_ge(s("ik_stored1"), 16 * 4)
            sp.wait_ge(s("h_stored"), 64)

        @block.gpsimd
        def _(pool):
            steps = [0]

            def step(ins):
                steps[0] += 1
                ins.then_inc(pool_step, 1)
                pool.wait_ge(pool_step, steps[0])

            tt = pool.tensor_tensor
            step(pool.memset(ident[:], 0.0))
            pool.affine_select(out=ident[:], in_=ident[:], compare_op=ALU.not_equal, fill=1.0, base=0,
                               pattern=[[-1, P]], channel_multiplier=1).then_inc(s("constants"), 1)
            step(pool.memset(tri[:], 0.0))
            pool.affine_select(out=tri[:], in_=tri[:], compare_op=ALU.is_ge, fill=1.0, base=0,
                               pattern=[[-1, P]], channel_multiplier=1).then_inc(s("constants"), 1)
            pool.memset(ones[:], 1.0).then_inc(s("constants"), 1)
            pool.iota(iota64[:], [[1, P]], base=0, channel_multiplier=0,
                      allow_small_or_imprecise_dtypes=True).then_inc(s("constants"), 1)
            pool.iota(tokid[:], [[P, NT]], base=0, channel_multiplier=1,
                      allow_small_or_imprecise_dtypes=True).then_inc(s("constants"), 1)
            pool.memset(uT[:, :, NJ], 0.0).then_inc(s("constants"), 1)
            pool.memset(hp[:, 0, :, :], 0.0).then_inc(s("constants"), 1)
            pool.iota(bexp[:, 0:1], [[0, 1]], base=0, channel_multiplier=1,
                      allow_small_or_imprecise_dtypes=True).then_inc(s("constants"), 1)

            pool.wait_ge(s("b_ready"), GP)
            pool.wait_ge(s("s5_operators"), 1)
            step(pool.tensor_copy(hp[:, NJ + 1, :, :], par[:, 2:4, :]))
            to_scan = list(range(NJ)) + list(range(NJ + 1, HC - 1))

            def scan(n):
                for j in to_scan[:n]:
                    hn = hp[:, j + 1, :, :]
                    step(tt(sct[:], a8[:], hp[:, j, :, :].unsqueeze(1).broadcast_to([P, 2, 2, GP]), ALU.mult))
                    step(tt(hn, hn, sct[:, :, 0, :], ALU.add))
                    step(tt(hn, hn, sct[:, :, 1, :], ALU.add))
                del to_scan[:n]
                if not to_scan:
                    pool.memset(sct[:], 0.0).then_inc(s("state_ready"), 1)

            def rotate(z, r, i, h0, nh):
                v = z.rearrange("p (h d) -> p h d", d=HD)[:, h0:h0 + nh, :]
                lo, hi = v[:, :, 0:8], v[:, :, 8:16]
                cos = rope[0:r, i, 0, :].unsqueeze(1).broadcast_to([r, nh, 8])
                sin = rope[0:r, i, 1, :].unsqueeze(1).broadcast_to([r, nh, 8])
                tmp = [rtmp[0:r, q, 0:nh, :] for q in range(4)]
                for q, (x, w) in enumerate(((lo, cos), (hi, sin), (lo, sin), (hi, cos))):
                    steps[0] += 1
                    tt(tmp[q], x, w, ALU.mult).then_inc(pool_step, 1)
                pool.wait_ge(pool_step, steps[0])
                steps[0] += 1
                tt(lo, tmp[0], tmp[1], ALU.subtract).then_inc(pool_step, 1)
                step(tt(hi, tmp[2], tmp[3], ALU.add))

            pool.wait_ge(s("rope_loaded"), 16)
            for i in range(NT):
                r = rows(i)
                pool.wait_ge(s("zi_ready"), i + 1)
                rotate(zi[0:r, i % 2, 0:576], r, i, 0, 9)
                pool.tensor_copy(zi[0:r, i % 2, 576:640], zi[0:r, i % 2, 512:576]).then_inc(s("zi_roped"), 1)
                scan((2, 2, 6, 10, 14, 18, 22, 26, HC)[i])
            m = 0
            for d in range(DK):
                for c, (t0, n) in enumerate(TOK_CHUNKS):
                    pool.wait_ge(s("val_used"), m + 1)
                    tt(g1[:, d, t0:t0 + n], sg[:, 2 * (m % 2), 0:n], sg[:, 2 * (m % 2) + 1, 0:n],
                       ALU.mult).then_inc(s("sg_used"), 1)
                    m += 1
            for i in range(NT):
                r = rows(i)
                pool.wait_ge(s("zq_ready"), i + 1)
                if i >= 2:
                    await_bank(pool, ("kT", i - 2))
                rotate(zq[0:r, i % 2, 0:640], r, i, 0, 10)
                dup = kdup[0:r, i % 2, :].rearrange("p (h e d) -> p h e d", h=2, e=2)
                k2 = zq[0:r, i % 2, 512:640].rearrange("p (h d) -> p h d", h=2)
                step(pool.tensor_copy(dup[:, :, 0, :], k2))
                pool.tensor_copy(dup[:, :, 1, :], k2).then_inc(s("zq_roped"), 1)

            m = 0
            for d in range(DK):
                for c, (t0, n) in enumerate(TOK_CHUNKS):
                    pool.wait_ge(s("ao_used"), m + 1)
                    tt(g1[:, d, t0:t0 + n], g1[:, d, t0:t0 + n], sga[:, m % 4, 0:n],
                       ALU.add).then_inc(s("mixed_ready"), 1)
                    m += 1

            pool.wait_ge(s("ln1_loaded"), 32)
            for i in range(NT):
                r = rows(i)
                x = x1[0:r, i, :]
                pool.wait_ge(s("normed"), i + 1)
                step(tt(x, x, ln1[0:r, 0, :], ALU.mult))
                tt(x, x, ln1[0:r, 1, :], ALU.add).then_inc(s("x1_ready"), 1)

            pool.wait_ge(s("slots_ready"), 1)
            for m in range(NT * MK):
                i, k = m // MK, m % MK
                if m >= 12:
                    pool.wait_ge(s("onehot_used"), m - 11)
                pool.tensor_scalar(onehot[0:rows(i), m % 12, P:P + NBP], iota64[0:rows(i), 0:NBP],
                                   sblk[0:rows(i), i, k:k + 1], tokid[0:rows(i), i:i + 1],
                                   ALU.is_equal, ALU.mult).then_inc(s("token_ready"), 1)

            pool.wait_ge(s("blocks_planned"), 2)
            pool.wait_ge(s("tab_ready"), 1)
            pool.wait_ge(s("x1_stored"), 16 * NT)
            def gather(u):
                pool.indirect_dma_start(xg[u], None, x1_d,
                                        bass.IndirectOffsetOnAxis(ap=tid[u][:, 0:1], axis=0)
                                        ).then_inc(s(f"xg_loaded{u}"), 16)

            def carry_wait():
                tt(carry[:], ones[0:1, 0:1], ones[0:1, 0:1], ALU.mult).then_inc(s("carried"), 1)

            for m in range(3):
                pool.wait_ge(s("tid_ready"), m + 1)
                if m == 0:
                    carry_wait()
                gather(m % 2)
            last_pair = pool.value_load(npair_i[0:1, 1:2], min_val=NE // 2 - 1, max_val=NBP // 2 - 1)
            with pool.Fori(0, last_pair) as ip:
                for u in range(2):
                    n = ip * 2 + u
                    pool.wait_ge(s("carried"), n + 1)
                    pool.wait_ge(s("tid_ready"), n + 4)
                    carry_wait()
                    gather(1 - u)

            pool.wait_ge(s("slots_done"), 1)
            pool.wait_ge(s("ln2_loaded"), 32)
            for i in range(NT + 1):
                for k in range(MK if i < NT else 0):
                    m = i * MK + k
                    if m >= 8:
                        pool.wait_ge(s("part_used"), m - 7)
                    pool.indirect_dma_start(part[0:rows(i), m % 8, :], None, slots_d,
                                            bass.IndirectOffsetOnAxis(ap=slot_i[0:rows(i), i, k:k + 1], axis=0)
                                            ).then_inc(s(f"part_loaded{m % 8}"), 16)
                if i >= 1:
                    r, y = rows(i - 1), x1[0:rows(i - 1), i - 1, :]
                    pool.wait_ge(s("normed"), NT + i)
                    step(tt(y, y, ln2[0:r, 0, :], ALU.mult))
                    tt(y, y, ln2[0:r, 1, :], ALU.add).then_inc(s("out_ready"), 1)

        @block.scalar
        def _(act):
            def f(dst, src, fn=ACT.Copy, **kw):
                return act.activation(dst, src, fn, **kw)

            def take(key, dst, src, name, fn=ACT.Copy, **kw):
                await_bank(act, key)
                f(dst, src, fn, **kw).then_inc(s(name), 1)

            quad = lambda key, n=P: bank(key)[:, 0:4 * P].rearrange("p (q n) -> p q n", q=4)[:, :, 0:n]

            for i in range(NT):
                for half in range(2):
                    take(("x", i, half), xT[:, 4 * half:4 * half + 4, tok(i)], quad(("x", i, half), rows(i)), "xT_ready")
            take("par", par[:].rearrange("p a b -> p (a b)"), bank("par")[:, 0:80], "par_ready")
            act.wait_ge(s("par_ready"), 1)
            f(sm[:, 0, :], par[:, 4, :], ACT.Exp).then_inc(s("trig_ready"), 1)
            act.wait_ge(s("angle_ready"), 1)
            f(sm[:, 3, :], sm[:, 1, :], ACT.Exp)
            f(sm[:, 4, :], sm[:, 2, :], ACT.Sin)
            f(sm[:, 5, :], sm[:, 2, :], ACT.Sin, scale=0.5).then_inc(s("trig_ready"), 1)
            for t in range(BL):
                take(("u", t), u2[:, :, t, :], bank(("u", t)).rearrange("p (g c) -> p g c", c=GC), "u2_ready")
            take("u_s", u64[0:DEC, :], bank("u_s")[0:DEC, :], "u64_ready")
            take("c", craw.rearrange("p a b c -> p (a b c)"), bank("c"), "c_turned")
            for q4 in range(8):
                take(("ut", q4), uT[:, 4 * q4:4 * q4 + 4, 0:NJ], quad(("ut", q4)), "uT_ready")
            take("uts", uT[:, :, NJ + 1:UC], bank("uts")[:, 0:NG * NJS].rearrange("p (g j) -> p g j", j=NJS),
                 "uT_ready")
            bopT_flat = bopT.rearrange("p a b n -> p (a b) n")
            for q4 in range(8):
                take(("bt", q4), bopT_flat[:, 4 * q4:4 * q4 + 4, :], quad(("bt", q4)), "bopT_ready")
            act.wait_ge(s("constants"), 8)
            for gp in range(GP):
                take(("b", gp), hp[:, 1:1 + UC, :, gp].rearrange("p j a -> p a j"),
                     bank(("b", gp))[:, 0:2 * UC].rearrange("p (a j) -> p a j", a=2), "b_ready")
            for q4 in range(4):
                for e in range(2):
                    b = ("k", q4, e)
                    take(b, kpad[:, 8 * q4 + e:8 * q4 + e + 7:2, 7:15, :].rearrange("p g l o -> p g (l o)"),
                         quad(b)[0:GC], "k_ready")

            def take_zi(i):
                r, z = rows(i), zi[0:rows(i), i % 2, :]
                if i == 0:
                    act.wait_ge(s("kpad_stored"), 16)
                if i >= 2:
                    await_bank(act, ("iqT", i - 2) if i - 2 in CHOOSING else ("ikT", i - 2))
                    act.wait_ge(s(f"ik_stored{i % 2}"), 16 * (i // 2))
                await_bank(act, ("iq", i))
                f(z[:, 0:512], bank(("iq", i))[0:r, :])
                await_bank(act, ("ik", i))
                f(z[:, 512:576], bank(("ik", i))[0:r, 0:64])
                f(iws[0:r, i, :], bank(("ik", i))[0:r, 64:72], scale=8 ** -0.5).then_inc(s("zi_ready"), 1)

            def take_turned(i):
                r = rows(i)
                k0 = i * P if i < NT - 1 else SEQ + PAST
                take(("ikT", i), ikT[:, k0:k0 + r], bank(("ikT", i))[:, 0:r], "ikT_ready")
                if i in CHOOSING:
                    take(("iqT", i), iqT[:, :, (i - 2) * P:(i - 2) * P + r], quad(("iqT", i), r), "iqT_ready")

            def take_scores(i):
                r = rows(i)
                for _, c0, n in score_keys(i):
                    for h in range(NH):
                        m = score_no[i, c0, h]
                        if m >= 4:
                            act.wait_ge(s("rel_used"), m - 3)
                        take(("s", i, c0, h), rel[0:r, m % 4, 0:n], bank(("s", i, c0, h))[0:r, 0:n], "rel_ready",
                             ACT.Relu, scale=HD ** -0.5)

            for i in range(NT):
                take_zi(i)
                if i > 0:
                    take_turned(i - 1)
                    if i - 1 in CHOOSING:
                        take_scores(i - 1)
                if i == 7:
                    for q4 in range(4):
                        take(("cik", q4), ikT[:, SEQ + q4 * 512:SEQ + (q4 + 1) * 512], bank(("cik", q4)), "cik_ready")
            take_turned(NT - 1)
            take_scores(NT - 1)

            for sample in range(2):
                r, y = (NJS, y2s) if sample else (NJ, y2)
                for key in [("y", sample, q4, e) for q4 in range(4) for e in range(2)]:
                    take(key, y[0:r].rearrange("p t (q g e c) -> p q e g t c", q=4, g=4, e=2)[:, key[2], key[3]],
                         bank(key)[0:r].rearrange("p (g t c) -> p g t c", g=4, t=BL),
                         "y2s_ready" if sample else "y_ready", ACT.Gelu_apprx_tanh)
            act.wait_ge(s("rel_used"), len(score_no))
            for u in range(2):
                act.wait_ge(s(f"ik_stored{u}"), 16 * (5 - u))
            take("hst", hst[0:16].rearrange("p a n -> p (a n)"), bank("hst")[0:16, :], "states_ready")
            for t in range(BL):
                take(("yt", t), yT[:, :, t:SEQ:BL], quad(("yt", t)), "yT_ready")
            take("yts", yT[:, :, SEQ:T], bank("yts")[:, 0:4 * DEC].rearrange("p (q n) -> p q n", q=4), "yT_ready")

            m = 0
            for d in range(DK):
                for c, (t0, n) in enumerate(TOK_CHUNKS):
                    if m >= 2:
                        act.wait_ge(s("sg_used"), m - 1)
                    for q, key in enumerate(("glu", "gs")):
                        take((key, d, c), sg[:, 2 * (m % 2) + q, 0:n], bank((key, d, c))[:, 0:n], "sg_ready",
                             ACT.Sigmoid)
                    m += 1

            def take_qkv(i):
                r, z = rows(i), zq[0:rows(i), i % 2, :]
                if i >= 2:
                    await_bank(act, ("qT", i - 2))
                    act.wait_ge(s(f"k_stored{i % 2}"), 16 * (i // 2))
                if i == 0:
                    act.wait_ge(s("sg_used"), 3 * DK)
                await_bank(act, ("q", i))
                f(z[:, 0:512], bank(("q", i))[0:r, :])
                await_bank(act, ("kv", i))
                f(z[:, 512:640], bank(("kv", i))[0:r, 0:128])
                f(v_tm[0:r, i if i < NT - 1 else 24, :], bank(("kv", i))[0:r, 128:256]).then_inc(s("zq_ready"), 1)

            def take_qk_turned(i):
                r = rows(i)
                k0 = i * P if i < NT - 1 else SEQ + PAST
                take(("qT", i), qT[:, :, tok(i)], quad(("qT", i), r), "qT_ready")
                take(("kT", i), kT[:, :, k0:k0 + r], quad(("kT", i), r)[:, 0:2, :], "qT_ready")

            for i in range(NT):
                take_qkv(i)
                if i > 0:
                    take_qk_turned(i - 1)
            take_qk_turned(NT - 1)
            for j in range(16):
                take(("ck", j), kT[:, :, SEQ + j * P:SEQ + (j + 1) * P], quad(("ck", j))[:, 0:2, :], "ckT_ready")

            def soften(n):
                i, _ = ATT[n]
                r, nk = rows(i), keys(i)[1]
                act.wait_ge(s("nbias_ready"), n + 1)
                for e in range(2):
                    p = probs_at(n)[0:r, e, 0:nk]
                    f(p, p, ACT.Exp, bias=nbias[0:r, n % 2, e:e + 1], scale=HD ** -0.5,
                      accum_out=rsum[0:r, n % 2, e:e + 1]).then_inc(s("probs"), 1)

            def take_pT(n, q):
                i, _ = ATT[n]
                r, gq = rows(i), group_no[n, q]
                g0, gn = key_groups(i)[q]
                if gq >= 3:
                    act.wait_ge(s("pT_used"), gq - 2)
                w = key_tiles(i)[g0][1]
                take(("p", n, q), pT[0:w, gq % 3, :].rearrange("p (c n) -> p c n", c=4)[:, 0:2 * gn, 0:r],
                     quad(("p", n, q), r)[0:w, 0:2 * gn, :], "pT_ready")

            def take_values(i):
                if i == 0:
                    act.wait_ge(s("h_stored"), 64)
                    act.wait_ge(s("k_stored0"), 16 * 5)
                    act.wait_ge(s("k_stored1"), 16 * 4)
                n = 4 * i + 3
                act.wait_ge(s("pT_used"), group_no[n, len(key_groups(i)) - 1] + 1)
                f(aT[:, :, tok(i)], quad(("o", i), rows(i))).then_inc(s("aT_ready"), 1)

            soften(0)
            for m, (n, q) in enumerate(group_no):
                take_pT(n, q)
                if q == 0 and n + 1 < len(ATT):
                    soften(n + 1)
                if q == 0 and n % 4 == 0 and n > 0:
                    take_values(ATT[n][0] - 1)
            take_values(NT - 1)

            m = 0
            for d in range(DK):
                for c, (t0, n) in enumerate(TOK_CHUNKS):
                    if m >= 4:
                        act.wait_ge(s("mixed_ready"), m - 3)
                    take(("ga", d, c), sga[:, m % 4, 0:n], bank(("ga", d, c))[:, 0:n], "sga_ready", ACT.Sigmoid)
                    m += 1

            def norm(i):
                r = rows(i)
                act.wait_ge(s("var_ready"), i + 1)
                f(lst[0:r, 1:2], lst[0:r, 0:1], ACT.Sqrt).then_inc(s("std_ready"), 1)
                act.wait_ge(s("rstd_ready"), i + 1)
                if i == 0:
                    act.wait_ge(s("slots_cleared"), 32)
                f(x1[0:r, i, :], xre[0:r, i % 2, :], ACT.Identity, bias=lst[0:r, 3:4],
                  scale=lst[0:r, 2:3]).then_inc(s("normed"), 1)

            def after_norm(i):
                r = rows(i)
                if i >= 2:
                    act.wait_ge(s("sel_ready"), i - 1)
                take(("r", i), rsc[0:r, i % 2, :], bank(("r", i))[0:r, 0:NE], "rsc_ready", ACT.Sigmoid)

            for i in range(NT + 2):
                if 0 <= i - 1 < NT:
                    for half in range(2):
                        key = ("x1", i - 1, half)
                        take(key, x1T[:, 4 * half:4 * half + 4, tok(i - 1)], quad(key, rows(i - 1)), "x1T_ready")
                if i < NT:
                    norm(i)
                if 0 <= i - 1 < NT:
                    after_norm(i - 1)
            for i in range(NT + 1):
                if i < NT:
                    await_bank(act, ("sg", i))
                    if i >= 2:
                        await_bank(act, ("ht", i - 2))
                    f(hsh[0:rows(i), i % 2, :], bank(("sg", i))[0:rows(i), 0:DE], ACT.Silu
                      ).then_inc(s("silu_ready"), 1)
                if i > 0:
                    r = rows(i - 1)
                    take(("ht", i - 1), hshT[:, (i - 1) % 2, :].rearrange("p (k n) -> p k n", k=2)[:, :, 0:r],
                         quad(("ht", i - 1), r)[:, 0:2, :], "hshT_ready")

            act.wait_ge(s("blocks_planned"), 2)
            last_pair = act.value_load(npair_i[0:1, 1:2], min_val=NE // 2 - 1, max_val=NBP // 2 - 1)

            def half_rows(u, blocks):
                act.wait_ge(s("xg_turned0"), blocks)
                f(xgT[u][:, 0:4, :], psum[:, 0, :].rearrange("p (q n) -> p q n", q=4)).then_inc(s("xgT_ready"), 1)

            def silu(u, blocks):
                act.wait_ge(s("egu_full"), blocks)
                f(eh[:, u, :], psum[:, 2, 0:DE], ACT.Silu).then_inc(s("esilu_ready"), 1)

            def take_eh(u, blocks):
                act.wait_ge(s("eh_turned"), blocks)
                f(ehT[u], psum[:, 3, 0:2 * P].rearrange("p (k n) -> p k n", k=2)).then_inc(s("ehT_ready"), 1)

            def half_y(u, blocks, stores):
                act.wait_ge(s("gcol_ready"), blocks)
                act.wait_ge(s("edn_full0"), blocks)
                f(yb[u][:, 0:512], psum[:, 4 + 2 * u, :], ACT.Copy,
                  scale=gcol[:, u:u + 1]).then_inc(s("y_half"), 1)

            def store_y(u, n):
                act.wait_ge(s("y_half"), (n + 1) * 2)
                act.dma_start(slots_d[bass.ds(n * P, P), :], yb[u]).then_inc(s(f"y_stored{u}"), 16)

            act.wait_ge(s("slots_cleared"), 32)
            act.wait_ge(s("tab_ready"), 1)
            for u in range(2):
                act.dma_start(slots_d[(NBP - 1) * P:NBP * P, u * P:(u + 1) * P], ident[:]
                              ).then_inc(s(f"y_stored{u}"), 16)
            half_rows(0, 1)
            silu(0, 1)
            half_rows(1, 2)
            take_eh(0, 1)
            with act.Fori(0, last_pair) as ip:
                for u in range(2):
                    n = ip * 2 + u
                    silu(1 - u, n + 2)
                    half_rows(u, n + 3)
                    half_y(u, n + 1, ip * 16 + 16)
                    take_eh(1 - u, n + 2)
                    store_y(u, n)
            silu(1, last_pair * 2 + 2)
            half_y(0, last_pair * 2 + 1, last_pair * 16 + 16)
            take_eh(1, last_pair * 2 + 2)
            store_y(0, last_pair * 2)
            half_y(1, last_pair * 2 + 2, last_pair * 16 + 16)
            store_y(1, last_pair * 2 + 1)

            for i in range(NT):
                r = rows(i)
                act.wait_ge(s("var_ready"), NT + i + 1)
                f(lst[0:r, 1:2], lst[0:r, 0:1], ACT.Sqrt).then_inc(s("std_ready"), 1)
                act.wait_ge(s("rstd_ready"), NT + i + 1)
                f(x1[0:r, i, :], x1[0:r, i, :], ACT.Identity, bias=lst[0:r, 3:4],
                  scale=lst[0:r, 2:3]).then_inc(s("normed"), 1)

        @block.vector
        def _(dve):
            steps = [0]

            def step(ins):
                steps[0] += 1
                ins.then_inc(dve_step, 1)
                dve.wait_ge(dve_step, steps[0])

            tt, ts, stt = dve.tensor_tensor, dve.tensor_scalar, dve.scalar_tensor_tensor

            for t in (pst[64:80, :],):
                dve.wait_ge(s("params_loaded"), 16 * 5)
                dve.tensor_copy(t.rearrange("q (e n) -> q e n", e=2),
                                ldt[64:80, :].unsqueeze(2).broadcast_to([GP, 2, NS])).then_inc(s("param_rows"), 1)
            ar, ai = par[:, 0, :], par[:, 1, :]
            dve.wait_ge(s("par_ready"), 1)
            dve.wait_ge(s("trig_ready"), 1)
            tt(sm[:, 1, :], sm[:, 0, :], ar, ALU.mult)
            step(tt(sm[:, 6, :], sm[:, 0, :], ai, ALU.mult))
            step(ts(sm[:, 7, :], sm[:, 6, :], 1.0 / TWO_PI, ROUND, ALU.mult, ALU.add))
            step(ts(sm[:, 7, :], sm[:, 7, :], ROUND, None, ALU.subtract))
            step(stt(sm[:, 8, :], sm[:, 7, :], -6.28125, sm[:, 6, :], ALU.mult, ALU.add))
            step(stt(sm[:, 8, :], sm[:, 7, :], -0.0019350051879882812, sm[:, 8, :], ALU.mult, ALU.add))
            step(stt(sm[:, 8, :], sm[:, 7, :], -(TWO_PI - 6.28125 - 0.0019350051879882812), sm[:, 8, :],
                     ALU.mult, ALU.add))
            ts(sm[:, 2, :], sm[:, 8, :], 3.1415925, -3.1415925, ALU.min, ALU.max).then_inc(s("angle_ready"), 1)
            tt(sm[:, 9, :], ar, ar, ALU.mult)
            step(tt(sm[:, 10, :], ai, ai, ALU.mult))
            step(tt(sm[:, 9, :], sm[:, 9, :], sm[:, 10, :], ALU.add))
            step(dve.reciprocal(sm[:, 10, :], sm[:, 9, :]))
            dve.memset(pw[:, 0, 0, :], 1.0)
            dve.memset(pw[:, 1, 0, :], 0.0)
            dve.wait_ge(s("trig_ready"), 2)
            step(tt(sm[:, 11, :], sm[:, 5, :], sm[:, 5, :], ALU.mult))
            step(ts(sm[:, 11, :], sm[:, 11, :], -2.0, 1.0, ALU.mult, ALU.add))
            tt(pw[:, 0, 1, :], sm[:, 3, :], sm[:, 11, :], ALU.mult)
            step(tt(pw[:, 1, 1, :], sm[:, 3, :], sm[:, 4, :], ALU.mult))
            step(ts(sm[:, 12, :], pw[:, 0, 1, :], -1.0, None, ALU.add))
            tt(sm[:, 13, :], sm[:, 12, :], ar, ALU.mult)
            tt(sm[:, 14, :], pw[:, 1, 1, :], ai, ALU.mult)
            tt(sm[:, 15, :], pw[:, 1, 1, :], ar, ALU.mult)
            step(tt(sm[:, 6, :], sm[:, 12, :], ai, ALU.mult))
            tt(sm[:, 13, :], sm[:, 13, :], sm[:, 14, :], ALU.add)
            step(tt(sm[:, 15, :], sm[:, 15, :], sm[:, 6, :], ALU.subtract))
            tt(sm[:, 13, :], sm[:, 13, :], sm[:, 10, :], ALU.mult)
            step(tt(sm[:, 14, :], sm[:, 15, :], sm[:, 10, :], ALU.mult))
            for n in (1, 2, 4):
                xr, xi = pw[:, 0, 1:n + 1, :], pw[:, 1, 1:n + 1, :]
                wr, wi = (pw[:, q, n:n + 1, :].broadcast_to([P, n, GP]) for q in range(2))
                q = [v[:, 0:n * GP].rearrange("p (n g) -> p n g", n=n)
                     for v in (t1, t2, t1[:, 1024:2048], t2[:, 1024:2048])]
                tt(q[0], xr, wr, ALU.mult)
                tt(q[1], xi, wi, ALU.mult)
                tt(q[2], xr, wi, ALU.mult)
                step(tt(q[3], xi, wr, ALU.mult))
                tt(pw[:, 0, n + 1:2 * n + 1, :], q[0], q[1], ALU.subtract)
                step(tt(pw[:, 1, n + 1:2 * n + 1, :], q[2], q[3], ALU.add))
            dve.tensor_copy(a8[:, 0, 0, :], pw[:, 0, 8, :])
            dve.tensor_copy(a8[:, 1, 1, :], pw[:, 0, 8, :])
            dve.tensor_copy(a8[:, 1, 0, :], pw[:, 1, 8, :])
            ts(a8[:, 0, 1, :], pw[:, 1, 8, :], -1.0, None, ALU.mult).then_inc(s("s5_operators"), 1)
            dve.wait_ge(s("b_loaded"), 32)
            cr, ci = (sm[:, q, :].unsqueeze(2).broadcast_to([P, GP, GC]) for q in (13, 14))
            q = [v[:, o:o + 256].rearrange("p (g c) -> p g c", c=GC) for v in (t1, t2) for o in (0, 256)]
            tt(q[0], cr, braw[:, 0, :, :], ALU.mult)
            tt(q[1], ci, braw[:, 1, :, :], ALU.mult)
            tt(q[2], cr, braw[:, 1, :, :], ALU.mult)
            step(tt(q[3], ci, braw[:, 0, :, :], ALU.mult))
            tt(bbar[:, 0, :, :], q[0], q[1], ALU.subtract)
            step(tt(bbar[:, 1, :, :], q[2], q[3], ALU.add))
            for part_ in range(2):
                for t in range(BL):
                    w = [pw[:, q_, 7 - t, :].unsqueeze(2).broadcast_to([P, GP, GC]) for q_ in range(2)]
                    o = slice(t * 256, (t + 1) * 256)
                    tt(t1[:, o].rearrange("p (g c) -> p g c", c=GC), w[0], bbar[:, part_, :, :], ALU.mult)
                    last = tt(t2[:, o].rearrange("p (g c) -> p g c", c=GC), w[1], bbar[:, 1 - part_, :, :], ALU.mult)
                step(last)
                v = [x[:, 0:2048].rearrange("p (t g c) -> p g t c", t=BL, g=GP) for x in (t1, t2)]
                step(tt(ba[:, part_, :, :, :], v[0], v[1], ALU.add if part_ else ALU.subtract))
            dve.memset(slot[:], 0.0).then_inc(s("s5_operators"), 1)
            dve.wait_ge(s("c_turned"), 1)
            w = [pw[:, q_, :, :].rearrange("p k g -> p g k").unsqueeze(3).broadcast_to([P, GP, 9, GC])
                 for q_ in range(2)]
            c_ = [craw[:, q_, :, :].unsqueeze(2).broadcast_to([P, GP, 9, GC]) for q_ in range(2)]
            v = [x.rearrange("p (g k c) -> p g k c", g=GP, k=9) for x in (t1, t2)]
            tt(v[0], w[0], c_[0], ALU.mult)
            step(tt(v[1], w[1], c_[1], ALU.mult))
            step(tt(ca[:, 0, :, :, :], v[0], v[1], ALU.subtract))
            tt(v[0], w[0], c_[1], ALU.mult)
            step(tt(v[1], w[1], c_[0], ALU.mult))
            step(stt(ca[:, 1, :, :, :].rearrange("p g k c -> p (g k c)"), t1, -1.0, t2, ALU.mult, ALU.subtract))
            dve.memset(cum[:], 0.0).then_inc(s("s5_operators"), 1)
            await_bank(dve, ("b", GP - 1))
            dve.memset(kpad[:, :, 0:7, :], 0.0)
            dve.wait_ge(s("d_loaded"), 16)
            dve.wait_ge(s("constants"), 8)
            skip = t1[0:GC, 0:512].rearrange("c (g o) -> c g o", o=GC)
            step(tt(skip, ident[0:GC, 0:GC].unsqueeze(1).broadcast_to([GC, NG, GC]),
                    dsk[:].unsqueeze(2).broadcast_to([GC, NG, GC]), ALU.mult))
            dve.wait_ge(s("k_ready"), 8)
            tt(kpad[:, :, 7, :], kpad[:, :, 7, :], skip, ALU.add).then_inc(s("s5_operators"), 1)

            dve.wait_ge(s("s5_operators"), 4)
            step(dve.memset(mk[:, 0:MASK_AT[2]], 0.0))
            for i in range(2):
                e = MASK_AT[i] + keys(i)[1]
                step(dve.memset(mk[0:64, e - 64:e], HID))
            mask_step = {0: steps[0], 1: steps[0]}

            def add_scores(i):
                r = rows(i)
                for _, c0, n in score_keys(i):
                    o = mk[0:r, MASK_AT[i] + c0:MASK_AT[i] + c0 + n]
                    for h in range(NH):
                        m = score_no[i, c0, h]
                        w, x = iws[0:r, i, h:h + 1], rel[0:r, m % 4, 0:n]
                        dve.wait_ge(s("rel_ready"), m + 1)
                        if h == 0:
                            ins = ts(o, x, w, None, ALU.mult)
                        else:
                            dve.wait_ge(s("rel_used"), m)
                            ins = stt(o, x, w, o, ALU.mult, ALU.add)
                        ins.then_inc(s("rel_used"), 1)
                dve.wait_ge(s("rel_used"), m + 1)
                if i < NT - 1:
                    e = MASK_AT[i] + keys(i)[1]
                    step(dve.memset(mk[0:64, e - 64:e], HID))

            at_round = [0]

            def choose(us):
                while us > 0 and at_round[0] < len(CHOOSING) * TOPK // 8:
                    i, r_ = CHOOSING[at_round[0] // (TOPK // 8)], at_round[0] % (TOPK // 8)
                    r, n = rows(i), keys(i)[1]
                    sc = mk[0:r, MASK_AT[i]:MASK_AT[i] + n]
                    step(dve.max(best[0:r, :], sc))
                    step(dve.match_replace(sc, best[0:r, :], sc, TAKEN))
                    if r_ == TOPK // 8 - 1:
                        step(ts(sc, sc, TAKEN / 2, HID, ALU.is_gt, ALU.mult))
                        mask_step[i] = steps[0]
                    at_round[0] += 1
                    us -= 2 * (n / 960 + 0.07)

            for i in CHOOSING:
                add_scores(i)
                choose({2: 6, 3: 6, 4: 8, 5: 8, 6: 8, 7: 4}.get(i, 35))

            m = 0
            for d in range(DK):
                for c, (t0, n) in enumerate(TOK_CHUNKS):
                    dve.wait_ge(s("sg_ready"), 2 * m + 2)
                    await_bank(dve, ("val", d, c))
                    v_ = sg[:, 2 * (m % 2), 0:n]
                    tt(v_, bank(("val", d, c))[:, 0:n], v_, ALU.mult).then_inc(s("val_used"), 1)
                    choose(8.5)
                    m += 1
            choose(85)

            maskings = [0]

            def mask(n):
                i, _ = ATT[n]
                r, p = rows(i), probs_at(n)
                dve.wait_ge(dve_step, mask_step[i])
                chunks = split(keys(i)[1], 512)
                for q, (c0, w) in enumerate(chunks):
                    for e in range(2):
                        key = ("l", n, c0, e)
                        await_bank(dve, key)
                        dve.tensor_tensor_reduce(out=p[0:r, e, c0:c0 + w], in0=bank(key)[0:r, 0:w],
                                                 in1=mk[0:r, MASK_AT[i] + c0:MASK_AT[i] + c0 + w], scale=1.0,
                                                 scalar=TAKEN, op0=ALU.add, op1=ALU.max,
                                                 accum_out=mx[0:r, e, q:q + 1]).then_inc(s("masked"), 1)
                        maskings[0] += 1
                dve.wait_ge(s("masked"), maskings[0])
                top = mx[0:r, :, 0]
                if len(chunks) > 1:
                    top = mx1[0:r, :]
                    step(dve.reduce_max(top, mx[0:r, :, 0:len(chunks)], AX.X))
                ts(nbias[0:r, n % 2, :], top, -HD ** -0.5, None, ALU.mult).then_inc(s("nbias_ready"), 1)

            await_bank(dve, ("l", 0, 0, 0))
            dve.memset(zeros, 0.0).then_inc(s("zeros_ready"), 1)
            mask(0)
            for n, (i, _) in enumerate(ATT):
                r, nk = rows(i), keys(i)[1]
                for e in range(2):
                    dve.wait_ge(s("probs"), 2 * n + e + 1)
                    ri = rinv[0:r, n % 2, e:e + 1]
                    step(dve.reciprocal(ri, rsum[0:r, n % 2, e:e + 1]))
                    p = probs_at(n)[0:r, e, 0:nk]
                    ts(p, p, ri, None, ALU.mult).then_inc(s("probs_scaled"), 1)
                if n + 1 < len(ATT):
                    if ATT[n + 1][0] == NT - 1:
                        choose(1e9)
                    mask(n + 1)
                choose(4)

            m = 0
            for d in range(DK):
                for c, (t0, n) in enumerate(TOK_CHUNKS):
                    dve.wait_ge(s("sga_ready"), m + 1)
                    await_bank(dve, ("ao", d, c))
                    v_ = sga[:, m % 4, 0:n]
                    tt(v_, bank(("ao", d, c))[:, 0:n], v_, ALU.mult).then_inc(s("ao_used"), 1)
                    m += 1

            def statistics(x, r, n):
                if n > 0:
                    dve.wait_ge(s("normed"), n)
                for q_ in range(2):
                    last = dve.bn_stats(stats[0:r, q_, :], x[:, q_ * 512:(q_ + 1) * 512])
                step(last)
                step(dve.bn_aggr(mv[0:r, :], stats[0:r, :, :].rearrange("p a b -> p (a b)")))
                ts(lst[0:r, 0:1], mv[0:r, 1:2], EPS, None, ALU.add).then_inc(s("var_ready"), 1)
                dve.wait_ge(s("std_ready"), n + 1)
                step(dve.reciprocal(lst[0:r, 2:3], lst[0:r, 1:2]))
                stt(lst[0:r, 3:4], mv[0:r, 0:1], -1.0, lst[0:r, 2:3], ALU.mult,
                    ALU.mult).then_inc(s("rstd_ready"), 1)

            def residual(i):
                r = rows(i)
                dve.wait_ge(s(f"xre_loaded{i % 2}"), 16 * (i // 2 + 1))
                f0 = banks.at[("wo", i)][0]
                for j in range(2):
                    await_bank(dve, ("wo", i), j)
                x = xre[0:r, i % 2, :]
                stt(x, x, ALPHA, psum[0:r, f0:f0 + 2, :].rearrange("p b n -> p (b n)"), ALU.mult,
                    ALU.add).then_inc(s("res_ready"), 1)
                dve.wait_ge(s("res_ready"), i + 1)
                statistics(x, r, i)

            def expert_match(i):
                r = rows(i)
                step(tt(oh[0:r], iota64[0:r, 0:NE].unsqueeze(1).broadcast_to([r, MK, NE]),
                        idx[0:r, i, 0:MK].unsqueeze(2).broadcast_to([r, MK, NE]), ALU.is_equal))

            def route(i):
                r = rows(i)
                sc = rsc[0:r, i % 2, :]
                dve.wait_ge(s("rsc_ready"), i + 1)
                if i == 0:
                    dve.wait_ge(s("w_s_loaded"), 64)
                biased = sb64[0:r, :]
                step(tt(biased, sc, rbias[0:r, :], ALU.add))
                step(dve.max(v8[0:r, :], biased))
                step(dve.max_index(i8[0:r, :], v8[0:r, :], biased))
                step(dve.tensor_copy(idx[0:r, i, :], i8[0:r, :]))
                expert_match(i)
                step(tt(oh2[0:r], oh[0:r], sc.unsqueeze(1).broadcast_to([r, MK, NE]), ALU.mult))
                g = gate[0:r, i, 0:MK]
                step(dve.reduce_sum(g, oh2[0:r], AX.X))
                step(dve.reduce_sum(gsum[0:r, 0:1], g, AX.X))
                step(dve.reciprocal(gsum[0:r, 1:2], gsum[0:r, 0:1]))
                ts(g, g, gsum[0:r, 1:2], ROUTED_SCALE, ALU.mult, ALU.mult)
                dve.reduce_sum(sel[0:r, i % 2, :], oh[0:r].rearrange("p k e -> p e k"),
                               AX.X).then_inc(s("sel_ready"), 1)

            def gate_shared(i):
                r = rows(i)
                dve.wait_ge(s("silu_ready"), i + 1)
                await_bank(dve, ("sg", i))
                h = hsh[0:r, i % 2, :]
                tt(h, h, bank(("sg", i))[0:r, DE:2 * DE], ALU.mult).then_inc(s("hsh_ready"), 1)

            def count(i):
                r = rows(i)
                await_bank(dve, ("rk", i))
                dve.tensor_copy(rk[0:r, i, :], bank(("rk", i))[0:r, 0:NE]).then_inc(s("rk_ready"), 1)
                dve.wait_ge(s("sel_ready"), i + 1)
                if i > 0:
                    dve.wait_ge(s("cum_ready"), i)
                tt(cum[0:r, :], cum[0:r, :], sel[0:r, i % 2, :], ALU.add).then_inc(s("cum_ready"), 1)

            def add_shared(i):
                r = rows(i)
                f0 = banks.at[("sd", i)][0]
                for j in range(2):
                    await_bank(dve, ("sd", i), j)
                x = x1[0:r, i, :]
                stt(x, x, ALPHA, psum[0:r, f0:f0 + 2, :].rearrange("p b n -> p (b n)"), ALU.mult,
                    ALU.add).then_inc(s("base_ready"), 1)

            for i in range(NT + 2):
                if i < NT:
                    residual(i)
                if 0 <= i - 2 < NT:
                    count(i - 2)
                if 0 <= i - 1 < NT:
                    route(i - 1)

            await_bank(dve, "cnt")
            cn, nb_, bend, base_ = (cnt[:, q_, :] for q_ in range(4))
            dve.tensor_copy(cn, bank("cnt")[:, 0:NE]).then_inc(s("blocks_planned"), 1)
            dve.wait_ge(s("blocks_planned"), 1)
            step(ts(nb_, cn, 63.5, 1.0 / P, ALU.add, ALU.mult))
            step(ts(nb_, nb_, ROUND, None, ALU.add))
            step(ts(nb_, nb_, -ROUND, 1.0, ALU.add, ALU.max))
            step(dve.tensor_tensor_scan(bend, ones[:, 0:NE], nb_, 0.0, ALU.mult, ALU.add))
            step(tt(base_, bend, nb_, ALU.subtract))
            step(ts(base_, base_, float(P), None, ALU.mult))
            step(ts(npair[0:1, 0:1], bend[0:1, NE - 1:NE], 0.5, 0.5, ALU.add, ALU.mult))
            step(ts(npair[0:1, 1:2], npair[0:1, 0:1], ROUND, None, ALU.add))
            ts(npair_i[0:1, 0:1], npair[0:1, 1:2], -ROUND, None, ALU.add)
            ts(npair_i[0:1, 1:2], npair[0:1, 1:2], -ROUND, -1.0, ALU.add, ALU.add).then_inc(s("blocks_planned"), 1)
            step(ts(oh[:, 0, :], bend, bexp[:, 0:1], None, ALU.is_le))
            step(dve.reduce_sum(bexp[:, 1:2], oh[:, 0, :], AX.X))
            ts(bexp_i[:], bexp[:, 1:2], float(NE - 1), None, ALU.min).then_inc(s("blocks_planned"), 1)

            def slots(i):
                r = rows(i)
                step(tt(rk[0:r, i, :], rk[0:r, i, :], base_[0:r, :], ALU.add))
                expert_match(i)
                step(tt(oh2[0:r], oh[0:r], rk[0:r, i, :].unsqueeze(1).broadcast_to([r, MK, NE]), ALU.mult))
                step(dve.reduce_sum(slot[0:r, i, 0:MK], oh2[0:r], AX.X))

            def block_and_place():
                dve.tensor_copy(slot_i[:], slot[:])
                step(ts(sblk[:], slot[:], -63.5, 1.0 / P, ALU.add, ALU.mult))
                step(ts(sblk[:], sblk[:], ROUND, None, ALU.add))
                step(ts(sblk[:], sblk[:], -ROUND, None, ALU.add))
                stt(sin_[:], sblk[:], -float(P), slot[:], ALU.mult, ALU.add).then_inc(s("slots_ready"), 1)
                dve.wait_ge(s("slots_ready"), 1)

            dve.wait_ge(s("x1_stored"), 16 * NT)
            for i in range(NT + 1):
                if i < NT:
                    gate_shared(i)
                if i > 0:
                    add_shared(i - 1)
                if i < 3:
                    for j in range(3 * i, 3 * i + 3):
                        slots(j)
                if i == 2:
                    block_and_place()
                for m in planned_in(i):
                    r, k = rows(m // MK), m % MK
                    if m >= 12:
                        dve.wait_ge(s("onehot_used"), m - 11)
                    o = onehot[0:r, m % 12, :]
                    ts(o[:, 0:P], iota64[0:r, :], sin_[0:r, m // MK, k:k + 1], None, ALU.is_equal)
                    ts(o[:, P + NBP:], iota64[0:r, 0:NBP], sblk[0:r, m // MK, k:k + 1],
                       gate[0:r, m // MK, k:k + 1], ALU.is_equal, ALU.mult).then_inc(s("onehot_ready"), 1)
            await_bank(dve, "tab")
            dve.tensor_copy(tab[:].rearrange("p a b -> p (a b)"), bank("tab")[:, 0:2 * NBP]).then_inc(s("tab_ready"), 1)
            dve.wait_ge(s("tab_ready"), 1)
            dve.wait_ge(s("base_ready"), NT)

            last_pair = dve.value_load(npair_i[0:1, 1:2], min_val=NE // 2 - 1, max_val=NBP // 2 - 1)

            def list_rows(u, column):
                ts(tid[u][:], column, 1.0, None, ALU.mult).then_inc(s("tid_ready"), 1)

            def half_rows(u, blocks):
                dve.wait_ge(s("xg_turned1"), blocks)
                dve.tensor_copy(xgT[u][:, 4:8, :], psum[:, 1, :].rearrange("p (q n) -> p q n", q=4)
                                ).then_inc(s("xgT_ready"), 1)

            def gate_up(u, blocks):
                dve.wait_ge(s("esilu_ready"), blocks)
                tt(eh[:, 2 + u, :], eh[:, u, :], psum[:, 2, DE:2 * DE], ALU.mult).then_inc(s("eh_ready"), 1)

            def half_y(u, n, blocks, stores):
                dve.wait_ge(s(f"y_stored{u}"), stores)
                ts(gcol[:, u:u + 1], tab[:, 1, bass.ds(n, 1)], 1.0, None, ALU.mult).then_inc(s("gcol_ready"), 1)
                dve.wait_ge(s("gcol_ready"), blocks)
                dve.wait_ge(s("edn_full1"), blocks)
                ts(yb[u][:, 512:1024], psum[:, 5 + 2 * u, :], gcol[:, u:u + 1], None,
                   ALU.mult).then_inc(s("y_half"), 1)

            list_rows(0, tab[:, 0, 0:1])
            list_rows(1, tab[:, 0, 1:2])
            half_rows(0, 1)
            list_rows(0, tab[:, 0, 2:3])
            gate_up(0, 1)
            half_rows(1, 2)
            with dve.Fori(0, last_pair) as ip:
                for u in range(2):
                    n = ip * 2 + u
                    list_rows(1 - u, tab[:, 0, bass.ds(n + 3, 1)])
                    gate_up(1 - u, n + 2)
                    half_rows(u, n + 3)
                    half_y(u, n, n + 1, ip * 16 + 16)
            gate_up(1, last_pair * 2 + 2)
            half_y(0, last_pair * 2, last_pair * 2 + 1, last_pair * 16 + 16)
            half_y(1, last_pair * 2 + 1, last_pair * 2 + 2, last_pair * 16 + 16)

            for i in range(NT):
                r = rows(i)
                x = x1[0:r, i, :]
                for k in range(MK):
                    m = i * MK + k
                    dve.wait_ge(s(f"part_loaded{m % 8}"), 16 * (m // 8 + 1))
                    tt(x, x, part[0:r, m % 8, :], ALU.add).then_inc(s("part_used"), 1)
                    dve.wait_ge(s("part_used"), m + 1)
                statistics(x, r, NT + i)


_INS = ["x_prompt", "x_sample", "cache_k", "cache_v", "cache_idx_k", "state_ssm_re", "state_ssm_im",
        "w_in", "ssm_a_re", "ssm_a_im", "ssm_log_dt", "ssm_b_re", "ssm_b_im", "ssm_c_re", "ssm_c_im", "ssm_d",
        "w_glu", "w_attn_proj", "w_out", "ln1_g", "ln1_b", "w_router", "router_bias",
        "w_exp_gu", "w_exp_down", "w_sh_gu", "w_sh_down", "ln2_g", "ln2_b"]
_OUTS = [("y_p", (1, SEQ, DM)), ("y_s", (1, DEC, DM)),
         ("k_p", (1, 1, SEQ, NKV, HD)), ("v_p", (1, 1, SEQ, NKV, HD)), ("ik_p", (1, 1, SEQ, HD)),
         ("hre_p", (1, 1, NG, NS)), ("him_p", (1, 1, NG, NS)),
         ("k_s", (1, 1, DEC, NKV, HD)), ("v_s", (1, 1, DEC, NKV, HD)), ("ik_s", (1, 1, DEC, HD)),
         ("hre_s", (1, 1, NG, NS)), ("him_s", (1, 1, NG, NS))]


def rope_table():
    pos = np.zeros(NT * P, np.float32)
    pos[:SEQ] = np.arange(SEQ)
    pos[SEQ:T] = PAST + np.arange(DEC)
    inv = np.float32(500000.0) ** (-np.arange(8, dtype=np.float32) * np.float32(2.0) / np.float32(16.0))
    ang = (pos[:, None] * inv.astype(np.float32)).astype(np.float32)
    return np.stack([np.cos(ang), np.sin(ang)], axis=1).astype(np.float32)


def kernel(**inputs):
    import concourse.bacc as _bacc
    from concourse.bass_utils import run_bass_kernel_spmd as _run

    nc = _bacc.Bacc("TRN2", target_bir_lowering=False, num_devices=1)
    arrays, a, out = {}, {}, {}
    for name in _INS:
        x = np.ascontiguousarray(inputs[name])
        arrays[f"in_{name}"] = x
        a[name] = nc.dram_tensor(f"in_{name}", x.shape, F32, kind="ExternalInput").ap()
    arrays["in_rope_table"] = rope_table()
    a["rope_table"] = nc.dram_tensor("in_rope_table", arrays["in_rope_table"].shape, F32, kind="ExternalInput").ap()
    for name, shape in _OUTS:
        out[name] = nc.dram_tensor(f"out_{name}", shape, F32, kind="ExternalOutput").ap()
    layer_program(nc, a, out)
    r = _run(nc, [arrays], core_ids=[0])
    return tuple(r.results[0][f"out_{name}"] for name, _ in _OUTS)
```

```python
from contextlib import ExitStack

import numpy as np

import concourse.bass as bass
from concourse import mybir

F32, I32, U32 = mybir.dt.float32, mybir.dt.int32, mybir.dt.uint32
ALU, ACT, AX = mybir.AluOpType, mybir.ActivationFunctionType, mybir.AxisListType

P = 128
DM = 1024
SEQ, DEC, PAST = 1024, 64, 2048
T = SEQ + DEC
NT = 9
DK = DM // P
HD, NH, NKV = 64, 8, 2
DS, GC, NG, NS = 512, 16, 32, 64
GP = NG // 2
BL = 8
NJ, NJS = SEQ // BL, DEC // BL
UC = NJ + 1 + NJS
HC = UC + 1
TOPK = 256
NE, MK, DE = 64, 6, 256
EPS = 1e-5
ALPHA = 2.0 ** 0.25
ROUTED_SCALE = 2.5
HID = -1e30
TAKEN = -3e38
KEYS = SEQ + PAST + DEC
NB_MAX = (T * MK) // P + NE
NBP = NB_MAX + 2
TWO_PI = 6.283185307179586
ROUND = 12582912.0


def rows(i):
    return P if i < NT - 1 else DEC


def tok(i):
    return slice(i * P, i * P + rows(i))


def keys(i):
    return (0, P * (i + 1)) if i < NT - 1 else (SEQ, PAST + DEC)


def split(n, m):
    return [(a, min(m, n - a)) for a in range(0, n, m)]


MASK_AT = [sum(keys(j)[1] for j in range(i)) for i in range(NT)]
MASK_W = sum(keys(j)[1] for j in range(NT))
TOK_CHUNKS = [(0, 384), (384, 384), (768, 320)]
CHOOSING = list(range(2, NT))


class Banks:

    def __init__(self):
        self.fills, self.turn, self.at, self.counts, self.reader = [0] * 8, {}, {}, {}, [None] * 8

    def take(self, key, reader, pool, n, value, signals):
        t = (self.turn.get(pool, 0) + n - 1) // n * n % len(pool)
        self.turn[pool] = t + n
        first = pool[t]
        before = [self.reader[b] for b in range(first, first + n)]
        self.at[key] = (first, self.fills[first:first + n])
        if value is None:
            value = self.counts[reader] = self.counts.get(reader, 0) + 1
        for b in range(first, first + n):
            self.reader[b] = (reader, value)
            self.fills[b] += signals
        return first, before


def layer_program(nc, a, out):
    banks = Banks()
    with ExitStack() as ctx:
        def sb(name, shape, dt=F32):
            return ctx.enter_context(nc.sbuf_tensor(name, shape, dt))

        def sem(name):
            return ctx.enter_context(nc.semaphore(name))

        def dram(name, shape, dt=F32):
            return nc.dram_tensor(name, shape, dt, kind="Internal").ap()

        kpad_d = dram("kpad_d", (NG, GC, 15 * GC))
        x1_d = dram("x1_d", (T, DM))
        slots_d = dram("slots_d", (NBP * P, DM))
        blk_d = dram("blk_d", (P, 1), I32)

        psum = ctx.enter_context(nc.psum_tensor("psum", [P, 8, 512], F32))

        arena = sb("arena", [P, 49792])

        def at(off, *shape):
            n = int(np.prod(shape))
            v = arena[:, off:off + n]
            if len(shape) == 1:
                return v
            names = "abcde"[:len(shape)]
            return v.rearrange(f"p ({' '.join(names)}) -> p {' '.join(names)}",
                               **{c: s for c, s in zip(names[1:], shape[1:])})

        xT = at(0, DK, T)
        x1T = xT
        mk = at(8704, MASK_W)
        t1, t2 = at(8704, 2304), at(8704 + 2304, 2304)
        braw, bbar, craw = at(8704 + 4608, 2, GP, GC), at(8704 + 5120, 2, GP, GC), at(8704 + 5632, 2, GP, GC)
        g1 = at(15424, DK, T)
        w_u = at(15424, DK, DS)
        m_op = at(15424, NG, P)
        ca = at(15424 + 4096, 2, GP, 9, GC)
        R = 24128
        uT = at(R, NG, UC)
        hp = at(R + 4384, HC, 2, GP)
        u2 = at(32928, NG, BL, GC)
        u2s = at(37024, NG, BL, GC)
        ba = at(41120, 2, GP, BL, GC)
        bopT = at(45216, 2, GP, P)
        xin = [at(32928 + i * DM, DM) for i in range(NT - 1)] + [at(45216, DM)]
        kpad = at(41120, NG, 15, GC)[0:GC]
        cst = at(14848, 2, 2, P)
        u64 = at(32000, DS)
        w_i = at(32928, DK, 584)
        iqT = at(37600, 4, T - 2 * P)
        ikT = at(40928, KEYS)
        zi = at(44064, 2, 640)
        rel = at(45344, 4, 512)
        cikd = at(47392, 16, P)
        rtmp = at(49440, 4, 10, 8)
        y2 = at(32928, BL, DS)
        y2s = at(37024, BL, DS)
        yT = at(41120, 4, T)
        y64 = at(45472, DS)
        wgs = at(R, 2, 16, P)
        sg = at(R + 4096, 4, 384)
        w_q = at(34816, DK, 768)
        qT = at(41088, 4, T)
        zq = at(45440, 2, 768)
        kT = at(R, NKV, KEYS)
        v_tm = at(30400, 25, P)
        kdup = at(33600, 2, 256)
        ckd = at(46976, 4, 256)
        pr = [at(34816 + 2 * SEQ * j, 2, SEQ) for j in range(3)]
        pr_s = [at(8704, 2, PAST + DEC), at(34816, 2, PAST + DEC)]
        pT = at(33600, 2, 512)
        zeros = at(48512, 512)
        aT = at(45440, 4, T)
        wap = at(8704, 2, 12, P)
        sga = at(8704 + 3072, 4, 384)
        w_o = at(R, DK, DM)
        xre = at(47104, 2, DM)
        x1 = at(34816, NT, DM)
        ln1 = at(44032, 2, DM)
        w_sg = at(8704, DK, 2 * DE)
        w_sd = at(32320, 2, DM)
        w_r = at(12800, DK, NE)
        hsh = at(13312, 2, DE)
        hst = at(48000, 4, P)
        gcol = sb("gcol", [P, 2])
        sb64 = sb("sb64", [P, NE])
        gsum = sb("gsum", [P, 2])
        hshT = at(13824, 2, DE)
        rk = at(14336, NT, NE)
        cnt = at(14912, 4, NE)
        oh = at(49152, MK, NE)
        oh2 = at(34368, MK, NE)
        ewg = [at(15424, DK, 2 * DE), at(21568, DK, 2 * DE)]
        ewd = [at(15424 + 4096, 2, DM), at(21568 + 4096, 2, DM)]
        xg = [at(0, DM), at(1024, DM)]
        xgT = [at(2048, DK, P), at(3072, DK, P)]
        yb = [at(4096, DM), at(5120, DM)]
        eh = at(6144, 4, DE)
        ehT = [at(7168, 2, P), at(7424, 2, P)]
        onehot = at(27712, 12, P + 2 * NBP)
        part = at(15424, 8, DM)
        ln2 = at(10752, 2, DM)

        ident = sb("ident", [P, P])
        tri = sb("tri", [P, P])
        ones = sb("ones", [P, P])
        iota64 = sb("iota64", [P, P])
        rope = sb("rope", [P, NT, 2, 8])
        pst = sb("pst", [P, P])
        ldt = sb("ldt", [P, 2])
        carry = sb("carry", [1, 1])
        par = sb("par", [P, 5, GP])
        sm = sb("sm", [P, 16, GP])
        pw = sb("pw", [P, 2, 9, GP])
        a8 = sb("a8", [P, 2, 2, GP])
        sct = sb("sct", [P, 2, 2, GP])
        dsk = sb("dsk", [GC, NG])
        iws = sb("iws", [P, NT, 8])
        best = sb("best", [P, 8])
        mx = sb("mx", [P, 2, 2, 8])
        mx1 = sb("mx1", [P, 2])
        nbias = sb("nbias", [P, 2, 2])
        rsum = sb("rsum", [P, 2, 2])
        rinv = sb("rinv", [P, 4, 2])
        stats = sb("stats", [P, 2, 6])
        mv = sb("mv", [P, 2])
        lst = sb("lst", [P, 4])
        rsc = sb("rsc", [P, 2, NE])
        rbias = sb("rbias", [P, NE])
        v8 = sb("v8", [P, 8])
        i8 = sb("i8", [P, 8], U32)
        idx = sb("idx", [P, NT, 8])
        gate = sb("gate", [P, NT, 8])
        sel = sb("sel", [P, 2, NE])
        cum = sb("cum", [P, NE])
        slot = sb("slot", [P, NT, 8])
        slot_i = sb("slot_i", [P, NT, 8], I32)
        sblk = sb("sblk", [P, NT, 8])
        sin_ = sb("sin_", [P, NT, 8])
        tokid = sb("tokid", [P, NT])
        tab = sb("tab", [P, 2, NBP])
        tid = [sb(f"tid{u}", [P, 1], I32) for u in range(2)]
        bexp = sb("bexp", [P, 4])
        bexp_i = sb("bexp_i", [P, 1], I32)
        brow = sb("brow", [1, P], I32)
        npair = sb("npair", [1, 8])
        npair_i = sb("npair_i", [1, 8], I32)

        full = [sem(f"bank_full{b}") for b in range(8)]
        dve_step = sem("dve_step")
        pool_step = sem("pool_step")
        S = {}

        def s(name):
            if name not in S:
                S[name] = sem(name)
            return S[name]

        def bank(key, j=0):
            f, c = banks.at[key]
            return psum[:, f + j, :]

        def quad(key, n=P):
            return bank(key)[:, 0:4 * P].rearrange("p (q n) -> p q n", q=4)[:, :, 0:n]

        def await_bank(eng, key, j=0):
            f, c = banks.at[key]
            eng.wait_ge(full[f + j], c[j] + 1)

        def take_turned_probs(eng, move, n, q):
            i, _ = ATT[n]
            r, gq = rows(i), group_no[n, q]
            g0, gn = key_groups(i)[q]
            if gq >= 2:
                eng.wait_ge(s("pT_used"), gq - 1)
            w = key_tiles(i)[g0][1]
            await_bank(eng, ("p", n, q))
            move(pT[0:w, gq % 2, :].rearrange("p (c n) -> p c n", c=4)[:, 0:2 * gn, 0:r],
                 quad(("p", n, q), r)[0:w, 0:2 * gn, :]).then_inc(s(moved[n, q][0]), 1)

        block = ctx.enter_context(nc.Block())
        planned_in = lambda i: range(max(0, 11 * (i - 3)), max(0, min(NT * MK, 11 * (i - 2))))
        score_keys = lambda i: [(i, a0, n0) for a0, n0 in split(keys(i)[1], 512)]
        X_PARTS = ((0, 1), (1, 2), (2, 5), (5, NT - 1), (NT - 1, NT))
        x_part = lambda i: next(f"x_loaded{a0}" for a0, a1 in X_PARTS if a0 <= i < a1)
        ATT = [(i, hp_) for i in range(NT) for hp_ in range(NH // 2)]
        key_tiles = lambda i: split(keys(i)[1], P)
        key_groups = lambda i: split(len(key_tiles(i)), 2)
        group_no = {}
        for n, (i, _) in enumerate(ATT):
            for q in range(len(key_groups(i))):
                group_no[n, q] = len(group_no)

        PROMPT, SAMPLE = range(4 * (NT - 1)), range(4 * (NT - 1), 4 * NT)
        EARLY, LATE = [(d, c) for d in range(DK) for c in range(2)], [(d, 2) for d in range(DK)]
        STEPS = EARLY + LATE
        step_no = {dc: m for m, dc in enumerate(STEPS)}
        WAPS = [("early", d) for d in range(DK)] + [("late", d) for d in range(DK)]

        moved = {}
        for n, q in group_no:
            name = "pT_by_vector" if n in SAMPLE and q >= 2 else "pT_by_scalar"
            moved[n, q] = (name, 1 + sum(v[0] == name for v in moved.values()))
        CLEARED = split(NBP - NE, -(-(NBP - NE) // (DK // 2)))

        def ahead(n):
            return n - 2 if ATT[n][0] < NT - 1 else n - 1

        def probs_at(n):
            return pr[n % 3] if ATT[n][0] < NT - 1 else pr_s[n % 2]

        score_no = {}
        for i in CHOOSING:
            for _, c0, w in score_keys(i):
                for h in range(NH):
                    score_no[i, c0, h] = len(score_no)

        @block.tensor
        def _(pe):
            def claim(key, reader, value=None, pool=tuple(range(8)), n=1, signals=1):
                first, before = banks.take(key, reader, pool, n, value, signals)
                for name, v in {b for b in before if b}:
                    pe.wait_ge(s(name), v)
                return first

            def filled(ins, key, j=0):
                ins.then_inc(full[banks.at[key][0] + j], 1)

            mm, tr = pe.matmul, pe.transpose

            pe.wait_ge(s("constants"), 8)
            for i in range(NT):
                r = rows(i)
                pe.wait_ge(s(x_part(i)), 16)
                for half in range(2):
                    b = claim(("x", i, half), "xT_ready")
                    for q in range(4):
                        k = 4 * half + q
                        last = tr(psum[:, b, q * P:q * P + r], xin[i][0:r, k::DK], ident[0:r, 0:r])
                    filled(last, ("x", i, half))
            pe.wait_ge(s("param_rows"), 1)
            b = claim("par", "par_ready")
            filled(tr(psum[:, b, 0:80], pst[0:80, :], ident[0:80, 0:80]), "par")
            pe.wait_ge(s("xT_ready"), 2 * NT)
            pe.wait_ge(s("w_u_loaded"), 16)
            for t in range(BL):
                if t == 4:
                    pe.wait_ge(s("c_loaded"), 16 * 32)
                    b = claim("c", "c_turned")
                    for n in range(4):
                        last = tr(psum[:, b, n * P:(n + 1) * P], cst[:, n // 2, n % 2, :], ident[:])
                    filled(last, "c")
                b = claim(("u", t), "u2_ready")
                for k in range(DK):
                    last = mm(psum[:, b, :], xT[:, k, t:SEQ:BL], w_u[:, k, :], start=k == 0, stop=k == DK - 1)
                filled(last, ("u", t))
            b = claim("u_s", "u64_ready")
            for k in range(DK):
                last = mm(psum[0:DEC, b, :], xT[:, k, SEQ:T], w_u[:, k, :], start=k == 0, stop=k == DK - 1)
            filled(last, "u_s")
            pe.wait_ge(s("u2_ready"), BL)
            for q4 in range(8):
                b = claim(("ut", q4), "uT_ready")
                for q in range(4):
                    g = 4 * q4 + q
                    last = tr(psum[:, b, q * P:(q + 1) * P], u2[:, g, :, :].rearrange("p t c -> p (t c)"), ident[:])
                filled(last, ("ut", q4))
            pe.wait_ge(s("u2s_ready"), 16 * NJS)
            b = claim("uts", "uT_ready")
            for g in range(NG):
                last = tr(psum[:, b, g * NJS:(g + 1) * NJS],
                          u2s[0:NJS, g, :, :].rearrange("p t c -> p (t c)"), ident[0:NJS, 0:NJS])
            filled(last, "uts")
            pe.wait_ge(s("s5_operators"), 2)
            for q4 in range(8):
                b = claim(("bt", q4), "bopT_ready")
                for q in range(4):
                    n = 4 * q4 + q
                    last = tr(psum[:, b, q * P:(q + 1) * P],
                              ba[:, n // GP, n % GP, :, :].rearrange("p t c -> p (t c)"), ident[:])
                filled(last, ("bt", q4))
            pe.wait_ge(s("uT_ready"), 9)
            pe.wait_ge(s("bopT_ready"), 8)
            for gp in range(GP):
                b = claim(("b", gp), "b_ready")
                for part_ in range(2):
                    for e in range(2):
                        last = mm(psum[e * 64:(e + 1) * 64, b, part_ * UC:(part_ + 1) * UC],
                                  bopT[:, part_, gp, e * 64:(e + 1) * 64], uT[:, 2 * gp + e, :],
                                  start=True, stop=True)
                filled(last, ("b", gp))
            pe.wait_ge(s("s5_operators"), 3)
            for q4 in range(4):
                for e in range(2):
                    claim(("k", q4, e), "k_ready")
                for q in range(4):
                    for e in range(2):
                        b, _ = banks.at["k", q4, e]
                        for part_ in range(2):
                            last = mm(psum[0:GC, b, q * P:(q + 1) * P], bbar[e * 64:(e + 1) * 64, part_, 4 * q4 + q, :],
                                      ca[e * 64:(e + 1) * 64, part_, 4 * q4 + q, 0:BL, :].rearrange("p t c -> p (t c)"),
                                      start=part_ == 0, stop=part_ == 1)
                        if q == 3:
                            filled(last, ("k", q4, e))

            def z_index(i):
                r = rows(i)
                if i == 0:
                    pe.wait_ge(s("w_i_loaded"), 16)
                for key, c0, n in (("iq", 0, 512), ("ik", 512, 72)):
                    b = claim((key, i), "zi_ready", i + 1)
                    for k in range(DK):
                        last = mm(psum[0:r, b, 0:n], xT[:, k, tok(i)], w_i[:, k, c0:c0 + n],
                                  start=k == 0, stop=k == DK - 1)
                    filled(last, (key, i))

            def turn_index(i):
                r = rows(i)
                pe.wait_ge(s("zi_roped"), i + 1)
                b = claim(("ikT", i), "ikT_ready")
                filled(tr(psum[:, b, 0:r], zi[0:r, i % 2, 512:640], ident[0:r, 0:r]), ("ikT", i))
                if i in CHOOSING:
                    b = claim(("iqT", i), "iqT_ready")
                    for q in range(4):
                        last = tr(psum[:, b, q * P:q * P + r], zi[0:r, i % 2, q * P:(q + 1) * P], ident[0:r, 0:r])
                    filled(last, ("iqT", i))

            def scores(i):
                r = rows(i)
                pe.wait_ge(s("ikT_ready"), i + 1)
                if i == NT - 1:
                    pe.wait_ge(s("cik_ready"), 4)
                pe.wait_ge(s("iqT_ready"), i - 1)
                for _, c0, n in score_keys(i):
                    for h in range(NH):
                        b = claim(("s", i, c0, h), "rel_ready")
                        e = h % 2
                        filled(mm(psum[0:r, b, 0:n],
                                  iqT[e * 64:(e + 1) * 64, h // 2, (i - 2) * P:(i - 2) * P + r],
                                  ikT[e * 64:(e + 1) * 64, keys(i)[0] + c0:keys(i)[0] + c0 + n],
                                  start=True, stop=True), ("s", i, c0, h))

            for i in range(NT):
                z_index(i)
                if i > 0:
                    turn_index(i - 1)
                if i - 2 in CHOOSING:
                    scores(i - 2)
                if i == 7:
                    pe.wait_ge(s("cik_loaded"), 32)
                    for q4 in range(4):
                        b = claim(("cik", q4), "cik_ready")
                        for q in range(4):
                            last = tr(psum[:, b, q * P:(q + 1) * P], cikd[:, 4 * q4 + q, :], ident[:])
                        filled(last, ("cik", q4))
            turn_index(NT - 1)
            scores(NT - 2)
            scores(NT - 1)

            pe.wait_ge(s("m_loaded"), 16 * BL)
            for sample in (1, 0):
                r, j0 = (NJS, NJ + 1) if sample else (NJ, 0)
                o = lambda gp, e: psum[0:r, banks.at["y", sample, gp // 4, e][0], gp % 4 * P:(gp % 4 + 1) * P]
                for gp in range(GP):
                    for e in range(2):
                        if gp % 4 == 0:
                            claim(("y", sample, gp // 4, e), "y2s_ready" if sample else "y_ready")
                        mm(o(gp, e), uT[:, 2 * gp + e, j0:j0 + r], m_op[:, 2 * gp + e, :], start=gp % 4 == 0,
                           stop=False)
                pe.wait_ge(s("state_ready"), 2 - sample)
                for gp in range(GP):
                    for part_ in range(2):
                        for e in range(2):
                            last = mm(o(gp, e), hp[e * 64:(e + 1) * 64, j0:j0 + r, part_, gp],
                                      ca[e * 64:(e + 1) * 64, part_, gp, 1:9, :].rearrange("p t c -> p (t c)"),
                                      start=False, stop=gp % 4 == 3 and part_ == 1)
                            if gp % 4 == 3 and part_ == 1:
                                filled(last, ("y", sample, gp // 4, e))
            pe.wait_ge(s("y_ready"), 8)
            b = claim("hst", "states_ready")
            for q in range(4):
                last = tr(psum[0:GP, b, q * P:(q + 1) * P], hp[:, (NJ, HC - 1)[q // 2], q % 2, :], ident[:])
            filled(last, "hst")
            for t in range(BL):
                b = claim(("yt", t), "yT_ready")
                for q in range(4):
                    last = tr(psum[:, b, q * P:(q + 1) * P], y2[:, t, q * P:(q + 1) * P], ident[:])
                filled(last, ("yt", t))
            pe.wait_ge(s("y64_ready"), 16 * NJS)
            b = claim("yts", "yT_ready")
            for q in range(4):
                last = tr(psum[:, b, q * DEC:(q + 1) * DEC], y64[0:DEC, q * P:(q + 1) * P], ident[0:DEC, 0:DEC])
            filled(last, "yts")

            for d in range(DK):
                pe.wait_ge(s(f"wgs_loaded{d % 2}"), 48 * (d // 2 + 1))
                for c, (t0, n) in enumerate(TOK_CHUNKS):
                    for key, w0, src, nk in (("gs", 0, xT, DK), ("glu", 12, yT, 4), ("val", 8, yT, 4)):
                        if key == "glu" and d == 0 and c == 0:
                            pe.wait_ge(s("yT_ready"), 9)
                        b = claim((key, d, c), "val_used" if key == "val" else "sg_ready")
                        for k in range(nk):
                            last = mm(psum[:, b, 0:n], wgs[:, d % 2, w0 + k, :], src[:, k, t0:t0 + n],
                                      start=k == 0, stop=k == nk - 1)
                        filled(last, (key, d, c))

            def z_qkv(i):
                r = rows(i)
                if i == 0:
                    pe.wait_ge(s("w_q_loaded"), 16)
                for key, c0, n in (("q", 0, 512), ("kv", 512, 256)):
                    b = claim((key, i), "zq_ready", i + 1)
                    for k in range(DK):
                        last = mm(psum[0:r, b, 0:n], xT[:, k, tok(i)], w_q[:, k, c0:c0 + n],
                                  start=k == 0, stop=k == DK - 1)
                    filled(last, (key, i))

            def turn_qkv(i):
                r = rows(i)
                pe.wait_ge(s("zq_roped"), i + 1)
                b = claim(("qT", i), "qT_ready")
                for q in range(4):
                    last = tr(psum[:, b, q * P:q * P + r], zq[0:r, i % 2, q * P:(q + 1) * P], ident[0:r, 0:r])
                filled(last, ("qT", i))
                b = claim(("kT", i), "qT_ready")
                for q in range(2):
                    last = tr(psum[:, b, q * P:q * P + r], kdup[0:r, i % 2, q * P:(q + 1) * P], ident[0:r, 0:r])
                filled(last, ("kT", i))

            def turn_cached(j):
                pe.wait_ge(s(f"ck_loaded{j % 4}"), 32 * (j // 4 + 1))
                b = claim(("ck", j), "ckT_ready")
                for q in range(2):
                    last = tr(psum[:, b, q * P:(q + 1) * P], ckd[:, j % 4, q * P:(q + 1) * P], ident[:])
                filled(last, ("ck", j))

            for i in range(NT):
                z_qkv(i)
                if i > 0:
                    turn_qkv(i - 1)
                    turn_cached(2 * i - 2)
                    turn_cached(2 * i - 1)
            turn_qkv(NT - 1)

            LOGITS, TURNED, OUTS = (0, 1, 2, 3), (4, 5), (6, 7)

            def logits(n):
                i, hp_ = ATT[n]
                r = rows(i)
                if n == 0:
                    pe.wait_ge(s("qT_ready"), 2 * NT)
                    pe.wait_ge(s("ckT_ready"), 16)
                    pe.wait_ge(s("cv_loaded"), 16)
                for c0, m in split(keys(i)[1], 512):
                    for e in range(2):
                        b = claim(("l", n, c0, e), "masked", pool=LOGITS)
                        k0 = keys(i)[0] + c0
                        filled(mm(psum[0:r, b, 0:m], qT[e * 64:(e + 1) * 64, hp_, tok(i)],
                                  kT[e * 64:(e + 1) * 64, hp_ // 2, k0:k0 + m], start=True, stop=True),
                               ("l", n, c0, e))

            def turn_probs(n, q):
                i, _ = ATT[n]
                r = rows(i)
                if q == 0:
                    pe.wait_ge(s("probs"), 2 * (n + 1))
                b = claim(("p", n, q), moved[n, q][0], pool=TURNED)
                g0, gn = key_groups(i)[q]
                for c in range(gn):
                    k0, w = key_tiles(i)[g0 + c]
                    for e in range(2):
                        last = tr(psum[0:w, b, (2 * c + e) * P:(2 * c + e) * P + r], probs_at(n)[0:r, e, k0:k0 + w],
                                  ident[0:r, 0:r])
                filled(last, ("p", n, q))

            def values(n, q):
                i, hp_ = ATT[n]
                r, nk = rows(i), keys(i)[1]
                if n % 2 == 0 and q == 0:
                    claim(("o", n // 2), "aT_ready", pool=OUTS)
                b = banks.at[("o", n // 2)][0]
                gq = group_no[n, q]
                g0, gn = key_groups(i)[q]
                name, value = moved[n, q]
                pe.wait_ge(s(name), value)
                for c in range(gn):
                    k0, w = key_tiles(i)[g0 + c]
                    v0 = k0 // P + (8 if i == NT - 1 else 0)
                    for e in range(2):
                        o = psum[e * 64:(e + 1) * 64, b, (n % 2) * P:(n % 2) * P + r]
                        last = mm(o, v_tm[0:w, v0, (hp_ // 2) * HD:(hp_ // 2 + 1) * HD],
                                  pT[0:w, gq % 2, (2 * c + e) * P:(2 * c + e) * P + r],
                                  start=k0 == 0, stop=k0 + w == nk)
                last.then_inc(s("pT_used"), 1)

            def sums(n):
                r, b = rows(ATT[n][0]), banks.at[("o", n // 2)][0]
                pe.wait_ge(s("rinv_ready"), n + 1)
                for e in range(2):
                    last = mm(psum[e * 64:(e + 1) * 64, b, (2 + n % 2) * P:(2 + n % 2) * P + r],
                              rinv[0:r, n % 4, e:e + 1].broadcast_to([r, HD]), ident[0:r, 0:r],
                              start=True, stop=True)
                if n % 2:
                    filled(last, ("o", n // 2))

            def attend(ns):
                first = [n for n in ns if ahead(n) < ns[0]]
                for n in first:
                    logits(n)
                groups = [(n, q) for n, q in group_no if n in ns]
                for m, (n, q) in enumerate(groups):
                    for n2 in (n + 1, n + 2):
                        if q == 0 and n2 in ns and n2 not in first and ahead(n2) == n:
                            logits(n2)
                    turn_probs(n, q)
                    if m > 0:
                        values(*groups[m - 1])
                        if q == 0 and n - 2 >= ns[0]:
                            sums(n - 2)
                values(*groups[-1])
                for n in ns[-2:]:
                    sums(n)

            def gate_attention(steps):
                for d, c in steps:
                    t0, n = TOK_CHUNKS[c]
                    w = WAPS.index(("late" if c == 2 else "early", d))
                    pe.wait_ge(s(f"wap_loaded{w % 2}"), 32 * (w // 2 + 1))
                    for key, w0, src, nk in (("ga", 0, xT, DK), ("ao", 8, aT, 4)):
                        if (key, d, c) in (("ao", *EARLY[0]), ("ao", *LATE[0])):
                            pe.wait_ge(s("aT_ready"), len(ATT if c == 2 else PROMPT) // 2)
                        b = claim((key, d, c), "sga_ready" if key == "ga" else "ao_used")
                        for k in range(nk):
                            last = mm(psum[:, b, 0:n], wap[:, w % 2, w0 + k, :], src[:, k, t0:t0 + n],
                                      start=k == 0, stop=k == nk - 1)
                        filled(last, (key, d, c))

            attend(PROMPT)
            gate_attention(EARLY)
            attend(SAMPLE)
            gate_attention(LATE)

            SIX = (0, 1, 2, 3, 4, 5)

            def project(i):
                r = rows(i)
                claim(("wo", i), "res_ready", n=2, pool=SIX)
                for j in range(2):
                    for k in range(DK):
                        last = mm(psum[0:r, banks.at[("wo", i)][0] + j, :], g1[:, k, tok(i)],
                                  w_o[:, k, j * 512:(j + 1) * 512], start=k == 0, stop=k == DK - 1)
                    filled(last, ("wo", i), j)

            def turn_x1(i):
                r = rows(i)
                pe.wait_ge(s("x1_ready"), i + 1)
                for half in range(2):
                    b = claim(("x1", i, half), "x1T_ready", pool=SIX)
                    for q in range(4):
                        last = tr(psum[:, b, q * P:q * P + r], x1[0:r, i, 4 * half + q::DK], ident[0:r, 0:r])
                    filled(last, ("x1", i, half))

            def project_x1(i, key, w, n, reader):
                r = rows(i)
                b = claim((key, i), reader, pool=SIX)
                for k in range(DK):
                    last = mm(psum[0:r, b, 0:n], x1T[:, k, tok(i)], w[:, k, :], start=k == 0, stop=k == DK - 1)
                filled(last, (key, i))

            def rank(i):
                r = rows(i)
                pe.wait_ge(s("sel_ready"), i + 1)
                b = claim(("rk", i), "rk_ready", pool=SIX)
                if i > 0:
                    pe.wait_ge(s("cum_ready"), i)
                    mm(psum[0:r, b, 0:NE], ones[:, 0:r], cum[:], start=True, stop=False)
                filled(mm(psum[0:r, b, 0:NE], tri[0:r, 0:r], sel[0:r, i % 2, :], start=i == 0, stop=True), ("rk", i))

            def turn_hidden(i):
                r = rows(i)
                pe.wait_ge(s("hsh_ready"), i + 1)
                b = claim(("ht", i), "hshT_ready", pool=SIX)
                for k in range(2):
                    last = tr(psum[:, b, k * P:k * P + r], hsh[0:r, i % 2, k::2], ident[0:r, 0:r])
                filled(last, ("ht", i))

            def shared_down(i):
                r = rows(i)
                pe.wait_ge(s("hshT_ready"), i + 1)
                claim(("sd", i), "base_ready", n=2, pool=SIX)
                for j in range(2):
                    for k in range(2):
                        last = mm(psum[0:r, banks.at[("sd", i)][0] + j, :], hshT[:, i % 2, k * P:k * P + r],
                                  w_sd[:, k, j * 512:(j + 1) * 512], start=k == 0, stop=k == 1)
                    filled(last, ("sd", i), j)

            pe.wait_ge(s("mixed_ready"), DK * 3)
            pe.wait_ge(s("w_o_loaded"), 16)
            def shared_up(i):
                b = claim(("sg", i), "hsh_ready", pool=(6 + i,) if i < 2 else SIX)
                for k in range(DK):
                    last = mm(psum[0:rows(i), b, 0:2 * DE], x1T[:, k, tok(i)], w_sg[:, k, :],
                              start=k == 0, stop=k == DK - 1)
                filled(last, ("sg", i))

            for i in range(NT + 2):
                if i < NT:
                    project(i)
                else:
                    shared_up(i - NT)
                if 0 <= i - 1 < NT:
                    turn_x1(i - 1)
                if 0 <= i - 2 < NT:
                    rank(i - 2)
                if 0 <= i - 1 < NT:
                    pe.wait_ge(s("x1T_ready"), 2 * i)
                    if i == 1:
                        pe.wait_ge(s("w_s_loaded"), 64)
                    project_x1(i - 1, "r", w_r, NE, "rsc_ready")

            for i in range(NT + 1):
                if 2 <= i < NT:
                    shared_up(i)
                if i == 0:
                    pe.wait_ge(s("cum_ready"), NT)
                    b = claim("cnt", "blocks_planned", 1, pool=SIX)
                    filled(mm(psum[:, b, 0:NE], ones[:], cum[:], start=True, stop=True), "cnt")
                else:
                    turn_hidden(i - 1)
                    for m in planned_in(i - 1):
                        if m == 0:
                            claim("tab", "tab_ready", pool=(6,))
                        r, o = rows(m // MK), onehot[:, m % 12, :]
                        pe.wait_ge(s("onehot_ready"), m + 1)
                        pe.wait_ge(s("token_ready"), m + 1)
                        last = mm(psum[:, banks.at["tab"][0], 0:2 * NBP], o[0:r, 0:P], o[0:r, P:P + 2 * NBP],
                                  start=m == 0, stop=m == NT * MK - 1)
                        if m < NT * MK - 1:
                            last.then_inc(s("onehot_used"), 1)
                        else:
                            filled(last, "tab")
                    shared_down(i - 1)

            pe.wait_ge(s("blocks_planned"), 2)
            last_pair = pe.value_load(npair_i[0:1, 1:2], min_val=NE // 2 - 1, max_val=NBP // 2 - 1)

            def turn_rows(u, loads):
                pe.wait_ge(s(f"xg_loaded{u}"), loads)
                for half in range(2):
                    for q in range(4):
                        last = tr(psum[:, half, q * P:(q + 1) * P], xg[u][:, 4 * half + q::DK], ident[:])
                    last.then_inc(s(f"xg_turned{half}"), 1)

            def gate_and_up(u, blocks, loads):
                pe.wait_ge(s("xgT_ready"), blocks * 2)
                pe.wait_ge(s(f"ewg_loaded{u}"), loads)
                for k in range(DK):
                    last = mm(psum[:, 2, :], xgT[u][:, k, :], ewg[u][:, k, :], start=k == 0, stop=k == DK - 1)
                last.then_inc(s("egu_full"), 1)

            def turn_eh(u, blocks):
                pe.wait_ge(s("eh_ready"), blocks)
                for k in range(2):
                    last = tr(psum[:, 3, k * P:(k + 1) * P], eh[:, 2 + u, k::2], ident[:])
                last.then_inc(s("eh_turned"), 1)

            def down(u, blocks, loads):
                pe.wait_ge(s("ehT_ready"), blocks)
                pe.wait_ge(s(f"ewd_loaded{u}"), loads)
                for j in range(2):
                    for k in range(2):
                        last = mm(psum[:, 4 + 2 * u + j, :], ehT[u][:, k, :], ewd[u][:, k, j * 512:(j + 1) * 512],
                                  start=k == 0, stop=k == 1)
                    last.then_inc(s(f"edn_full{j}"), 1)

            pe.wait_ge(s("base_ready"), NT)
            turn_rows(0, 16)
            gate_and_up(0, 1, 16)
            turn_rows(1, 16)
            turn_eh(0, 1)
            with pe.Fori(0, last_pair) as ip:
                for u in range(2):
                    n = ip * 2 + u
                    gate_and_up(1 - u, n + 2, ip * 16 + 16 + 16 * u)
                    turn_rows(u, ip * 16 + 32)
                    down(u, n + 1, ip * 16 + 16)
                    turn_eh(1 - u, n + 2)
            gate_and_up(1, last_pair * 2 + 2, last_pair * 16 + 16)
            down(0, last_pair * 2 + 1, last_pair * 16 + 16)
            turn_eh(1, last_pair * 2 + 2)
            down(1, last_pair * 2 + 2, last_pair * 16 + 16)

        @block.sync
        def _(sp):
            def ld(dst, src, name, small=False):
                sp.dma_start(dst, src, allow_slow_non_contiguous=small).then_inc(s(name), 16)

            def load_x(a0, a1):
                if a0 == NT - 1:
                    ld(xin[a0][0:DEC, :], a["x_sample"][0], x_part(a0))
                else:
                    ld(at(32928 + a0 * DM, a1 - a0, DM),
                       a["x_prompt"][0, a0 * P:a1 * P, :].rearrange("(t p) f -> p t f", p=P), x_part(a0))

            w_in = a["w_in"][0]
            w_glu = a["w_glu"][0]
            by_chunk = lambda w: w.rearrange("(p k) f -> p k f", k=DK)
            load_x(*X_PARTS[0])
            load_x(*X_PARTS[1])
            flat = lambda ap: ap.rearrange("(q e) n -> q (e n)", e=2)
            for q, name in enumerate(("ssm_a_re", "ssm_a_im")):
                ld(pst[q * GP:(q + 1) * GP, :], flat(a[name][0]), "params_loaded")
            for q, name in enumerate(("state_ssm_re", "state_ssm_im")):
                ld(pst[(q + 2) * GP:(q + 3) * GP, :], flat(a[name][0, 0]), "params_loaded")
            ld(ldt[64:80, :], a["ssm_log_dt"][0].rearrange("(q e) -> q e", e=2), "params_loaded")
            for part_ in X_PARTS[2:]:
                load_x(*part_)
            ld(w_u, by_chunk(w_in[:, 0:DS]), "w_u_loaded")
            for q, name in enumerate(("ssm_b_re", "ssm_b_im")):
                ld(braw[:, q, :, :], a[name][0].rearrange("(q e) n c -> (e n) q c", e=2), "b_loaded")
            for q, name in enumerate(("ssm_c_re", "ssm_c_im")):
                for half in range(2):
                    for g8 in range(8):
                        g = 16 * half + 2 * g8
                        ld(cst[g8 * GC:(g8 + 1) * GC, q, half, :].rearrange("c (e n) -> c e n", e=2),
                           a[name][0, g:g + 2].rearrange("e c n -> c e n"), "c_loaded")
            ld(dsk[:], a["ssm_d"][0].rearrange("(g c) -> c g", c=GC), "d_loaded", small=True)
            ld(rope[:], a["rope_table"].rearrange("(t p) a f -> p t a f", p=P), "rope_loaded")
            sp.wait_ge(s("u64_ready"), 1)
            for t in range(BL):
                ld(u2s[0:NJS, :, t, :], u64[t:DEC:BL, :].rearrange("p (g c) -> p g c", c=GC), "u2s_ready")
            sp.wait_ge(s("uT_ready"), 9)
            ld(w_i, by_chunk(w_in[:, 1280:1864]), "w_i_loaded")
            sp.wait_ge(s("s5_operators"), 4)
            ld(kpad_d.rearrange("g c (l o) -> c g l o", o=GC), kpad, "kpad_stored")
            sp.wait_ge(s("kpad_stored"), 16)
            for t in range(BL):
                ld(m_op[t * GC:(t + 1) * GC, :, :],
                   kpad_d.rearrange("g c l -> c g l")[:, :, (7 - t) * GC:(7 - t) * GC + P], "m_loaded")
            for rep in range(2):
                ld(cikd[:, :, rep * HD:(rep + 1) * HD], a["cache_idx_k"][0, 0].rearrange("(j p) d -> p j d", p=P),
                   "cik_loaded")
            for i in range(NT):
                sp.wait_ge(s("zi_roped"), i + 1)
                dst = out["ik_p"][0, 0, tok(i), :] if i < NT - 1 else out["ik_s"][0, 0]
                ld(dst, zi[0:rows(i), i % 2, 512:576], f"ik_stored{i % 2}")
            sp.wait_ge(s("y2s_ready"), 8)
            sp.wait_ge(s("rel_used"), len(score_no))
            for t in range(BL):
                ld(y64[t:DEC:BL, :], y2s[0:NJS, t, :], "y64_ready")
            sp.wait_ge(s("states_ready"), 1)
            for q, key in enumerate(("hre_p", "him_p")):
                ld(out[key][0, 0].rearrange("(q e) n -> q (e n)", e=2), hst[0:16, q, :], "h_stored")
            for q, key in enumerate(("hre_s", "him_s")):
                ld(out[key][0, 0].rearrange("(q e) n -> q (e n)", e=2), hst[0:16, 2 + q, :], "h_stored")

            def load_wgs(d):
                if d >= 2:
                    await_bank(sp, ("val", d - 2, 2))
                u, c = d % 2, slice(d * P, (d + 1) * P)
                ld(wgs[:, u, 0:8, :], by_chunk(w_in[:, 1864 + d * P:1864 + (d + 1) * P]), f"wgs_loaded{u}")
                ld(wgs[:, u, 8:12, :], w_glu[:, c].rearrange("(k p) f -> p k f", p=P), f"wgs_loaded{u}")
                ld(wgs[:, u, 12:16, :], w_glu[:, DM + d * P:DM + (d + 1) * P].rearrange("(k p) f -> p k f", p=P),
                   f"wgs_loaded{u}")

            load_wgs(0)
            load_wgs(1)
            sp.wait_ge(s("yT_ready"), 9)
            ld(w_q, by_chunk(w_in[:, 512:1280]), "w_q_loaded")
            ld(v_tm[:, 8:24, :], a["cache_v"][0, 0].rearrange("(j p) h d -> p j (h d)", p=P), "cv_loaded")
            for d in range(2, DK):
                load_wgs(d)
            ck = a["cache_k"][0, 0].rearrange("(j p) h d -> j p h d", p=P)

            def load_cached(j):
                if j >= 4:
                    await_bank(sp, ("ck", j - 4))
                for rep in range(2):
                    ld(ckd[:, j % 4, :].rearrange("p (h r d) -> p h r d", h=2, r=2)[:, :, rep, :], ck[j],
                       f"ck_loaded{j % 4}")

            for j in range(4):
                load_cached(j)
            for i in range(NT):
                r = rows(i)
                if 2 <= i < NT - 1:
                    load_cached(2 * i)
                    load_cached(2 * i + 1)
                sp.wait_ge(s("zq_roped"), i + 1)
                kd, vd = (out["k_p"][0, 0, tok(i)], out["v_p"][0, 0, tok(i)]) if i < NT - 1 else \
                    (out["k_s"][0, 0], out["v_s"][0, 0])
                ld(kd.rearrange("t h d -> t (h d)"), zq[0:r, i % 2, 512:640], f"k_stored{i % 2}")
                ld(vd.rearrange("t h d -> t (h d)"), v_tm[0:r, i if i < NT - 1 else 24, :], "v_stored")
            w_ap = a["w_attn_proj"][0]

            def load_wap(w):
                part_, d = WAPS[w]
                if w >= 2:
                    before, d0 = WAPS[w - 2]
                    await_bank(sp, ("ao", d0, 2 if before == "late" else 1))
                ld(wap[:, w % 2, 0:8, :], by_chunk(w_in[:, 2888 + d * P:2888 + (d + 1) * P]), f"wap_loaded{w % 2}")
                ld(wap[:, w % 2, 8:12, :], w_ap[:, d * P:(d + 1) * P].rearrange("(k p) f -> p k f", p=P),
                   f"wap_loaded{w % 2}")

            sp.wait_ge(s("masked"), 2 * sum(len(split(keys(ATT[n][0])[1], 512)) for n in PROMPT))
            for w in range(DK):
                load_wap(w)
            name, value = moved[len(ATT) - 2, len(key_groups(NT - 1)) - 1]
            sp.wait_ge(s(name), value)
            load_wap(DK)
            load_wap(DK + 1)
            sp.wait_ge(s("aT_ready"), len(ATT) // 2)
            ld(w_o, a["w_out"][0].rearrange("(k p) f -> p k f", p=P), "w_o_loaded")
            sp.wait_ge(s("v_stored"), 16 * NT)
            ld(w_sd, a["w_sh_down"][0].rearrange("(p k) f -> p k f", k=2), "w_s_loaded")
            for w in range(DK + 2, 2 * DK):
                load_wap(w)

            def load_xre(i):
                if i >= 2:
                    sp.wait_ge(s("normed"), i - 1)
                src = a["x_prompt"][0, tok(i), :] if i < NT - 1 else a["x_sample"][0]
                ld(xre[0:rows(i), i % 2, :], src, f"xre_loaded{i % 2}")

            sp.wait_ge(s("mixed_ready"), 3 * DK)
            load_xre(0)
            load_xre(1)
            for q, name in enumerate(("ln1_g", "ln1_b")):
                ld(ln1[:, q, :], a[name].broadcast_to([P, DM]), "ln1_loaded")
            ld(w_sg, by_chunk(a["w_sh_gu"][0]), "w_s_loaded")
            ld(w_r, by_chunk(a["w_router"][0]), "w_s_loaded")
            ld(rbias[:], a["router_bias"].broadcast_to([P, NE]), "w_s_loaded")
            for i in range(NT):
                if i >= 2:
                    load_xre(i)
                sp.wait_ge(s("x1_ready"), i + 1)
                ld(x1_d[tok(i), :], x1[0:rows(i), i, :], "x1_stored")

            sp.wait_ge(s("blocks_planned"), 3)
            ld(blk_d, bexp_i[:], "blk_stored")
            sp.wait_ge(s("blk_stored"), 16)
            ld(brow[:], blk_d.rearrange("p a -> a p"), "blk_stored")
            sp.wait_ge(s("blk_stored"), 32)
            sp.wait_ge(s("blocks_planned"), 2)
            last_pair = sp.value_load(npair_i[0:1, 1:2], min_val=NE // 2 - 1, max_val=NBP // 2 - 1)

            def expert(n):
                return sp.value_load(brow[0:1, bass.ds(n, 1)], min_val=0, max_val=NE - 1)

            def load_gu(e, u):
                ld(ewg[u], a["w_exp_gu"][0, bass.ds(e, 1)].rearrange("a (p k) f -> (a p) k f", k=DK), f"ewg_loaded{u}")

            def load_dn(e, u):
                ld(ewd[u], a["w_exp_down"][0, bass.ds(e, 1)].rearrange("a (p k) f -> (a p) k f", k=2),
                   f"ewd_loaded{u}")

            for u in range(2):
                e = expert(u)
                load_gu(e, u)
                load_dn(e, u)
            sp.wait_ge(s("egu_full"), 1)
            load_gu(expert(2), 0)
            with sp.Fori(0, last_pair) as ip:
                for u in range(2):
                    n = ip * 2 + u
                    e, after = expert(n + 2), expert(n + 3)
                    sp.wait_ge(s("egu_full"), n + 2)
                    load_gu(after, 1 - u)
                    sp.wait_ge(s("edn_full1"), n + 1)
                    load_dn(e, u)
            for q, name in enumerate(("ln2_g", "ln2_b")):
                ld(ln2[:, q, :], a[name].broadcast_to([P, DM]), "ln2_loaded")
            sp.wait_ge(s("ewg_loaded0"), last_pair * 16 + 32)
            for u in range(2):
                sp.wait_ge(s(f"y_stored{u}"), last_pair * 16 + 32)
            sp.nop().then_inc(s("slots_done"), 1)

            for i in range(NT):
                sp.wait_ge(s("out_ready"), i + 1)
                ld(out["y_p"][0, tok(i), :] if i < NT - 1 else out["y_s"][0], x1[0:rows(i), i, :], "out_stored")
            sp.wait_ge(s("out_stored"), 16 * NT)
            sp.wait_ge(s("v_stored"), 16 * NT)
            sp.wait_ge(s("k_stored0"), 16 * 5)
            sp.wait_ge(s("k_stored1"), 16 * 4)
            sp.wait_ge(s("ik_stored0"), 16 * 5)
            sp.wait_ge(s("ik_stored1"), 16 * 4)
            sp.wait_ge(s("h_stored"), 64)

        @block.gpsimd
        def _(pool):
            steps = [0]

            def step(ins):
                steps[0] += 1
                ins.then_inc(pool_step, 1)
                pool.wait_ge(pool_step, steps[0])

            tt = pool.tensor_tensor
            step(pool.memset(ident[:], 0.0))
            pool.affine_select(out=ident[:], in_=ident[:], compare_op=ALU.not_equal, fill=1.0, base=0,
                               pattern=[[-1, P]], channel_multiplier=1).then_inc(s("constants"), 1)
            step(pool.memset(tri[:], 0.0))
            pool.affine_select(out=tri[:], in_=tri[:], compare_op=ALU.is_ge, fill=1.0, base=0,
                               pattern=[[-1, P]], channel_multiplier=1).then_inc(s("constants"), 1)
            pool.memset(ones[:], 1.0).then_inc(s("constants"), 1)
            pool.iota(iota64[:], [[1, P]], base=0, channel_multiplier=0,
                      allow_small_or_imprecise_dtypes=True).then_inc(s("constants"), 1)
            pool.iota(tokid[:], [[P, NT]], base=0, channel_multiplier=1,
                      allow_small_or_imprecise_dtypes=True).then_inc(s("constants"), 1)
            pool.memset(uT[:, :, NJ], 0.0).then_inc(s("constants"), 1)
            pool.memset(hp[:, 0, :, :], 0.0).then_inc(s("constants"), 1)
            pool.iota(bexp[:, 0:1], [[0, 1]], base=0, channel_multiplier=1,
                      allow_small_or_imprecise_dtypes=True).then_inc(s("constants"), 1)

            pool.wait_ge(s("b_ready"), GP)
            pool.wait_ge(s("s5_operators"), 1)
            step(pool.tensor_copy(hp[:, NJ + 1, :, :], par[:, 2:4, :]))
            to_scan = list(range(NJ + 1, HC - 1)) + list(range(NJ))

            def scan(n):
                for j in to_scan[:n]:
                    hn = hp[:, j + 1, :, :]
                    step(tt(sct[:], a8[:], hp[:, j, :, :].unsqueeze(1).broadcast_to([P, 2, 2, GP]), ALU.mult))
                    step(tt(hn, hn, sct[:, :, 0, :], ALU.add))
                    step(tt(hn, hn, sct[:, :, 1, :], ALU.add))
                    if j in (NJ - 1, HC - 2):
                        pool.memset(carry[:], 0.0).then_inc(s("state_ready"), 1)
                del to_scan[:n]

            def rotate(z, r, i, h0, nh):
                v = z.rearrange("p (h d) -> p h d", d=HD)[:, h0:h0 + nh, :]
                lo, hi = v[:, :, 0:8], v[:, :, 8:16]
                cos = rope[0:r, i, 0, :].unsqueeze(1).broadcast_to([r, nh, 8])
                sin = rope[0:r, i, 1, :].unsqueeze(1).broadcast_to([r, nh, 8])
                tmp = [rtmp[0:r, q, 0:nh, :] for q in range(4)]
                for q, (x, w) in enumerate(((lo, cos), (hi, sin), (lo, sin), (hi, cos))):
                    steps[0] += 1
                    tt(tmp[q], x, w, ALU.mult).then_inc(pool_step, 1)
                pool.wait_ge(pool_step, steps[0])
                steps[0] += 1
                tt(lo, tmp[0], tmp[1], ALU.subtract).then_inc(pool_step, 1)
                step(tt(hi, tmp[2], tmp[3], ALU.add))

            pool.wait_ge(s("rope_loaded"), 16)
            scan(20)
            for i in range(NT):
                r = rows(i)
                pool.wait_ge(s("zi_ready"), i + 1)
                rotate(zi[0:r, i % 2, 0:576], r, i, 0, 9)
                pool.tensor_copy(zi[0:r, i % 2, 576:640], zi[0:r, i % 2, 512:576]).then_inc(s("zi_roped"), 1)
                scan((6, 6, 6, 6, 11, 13, 15, 18, HC)[i])
            m = 0
            for d in range(DK):
                for c, (t0, n) in enumerate(TOK_CHUNKS):
                    pool.wait_ge(s("val_used"), m + 1)
                    tt(g1[:, d, t0:t0 + n], sg[:, 2 * (m % 2), 0:n], sg[:, 2 * (m % 2) + 1, 0:n],
                       ALU.mult).then_inc(s("sg_used"), 1)
                    m += 1
            for i in range(NT):
                r = rows(i)
                pool.wait_ge(s("zq_ready"), i + 1)
                if i >= 2:
                    await_bank(pool, ("kT", i - 2))
                rotate(zq[0:r, i % 2, 0:640], r, i, 0, 10)
                dup = kdup[0:r, i % 2, :].rearrange("p (h e d) -> p h e d", h=2, e=2)
                k2 = zq[0:r, i % 2, 512:640].rearrange("p (h d) -> p h d", h=2)
                step(pool.tensor_copy(dup[:, :, 0, :], k2))
                pool.tensor_copy(dup[:, :, 1, :], k2).then_inc(s("zq_roped"), 1)

            for m, (d, c) in enumerate(STEPS):
                t0, n = TOK_CHUNKS[c]
                pool.wait_ge(s("ao_used"), m + 1)
                tt(g1[:, d, t0:t0 + n], g1[:, d, t0:t0 + n], sga[:, m % 4, 0:n],
                   ALU.add).then_inc(s("mixed_ready"), 1)

            pool.wait_ge(s("ln1_loaded"), 32)
            for i in range(NT):
                r = rows(i)
                x = x1[0:r, i, :]
                pool.wait_ge(s("normed"), i + 1)
                step(tt(x, x, ln1[0:r, 0, :], ALU.mult))
                tt(x, x, ln1[0:r, 1, :], ALU.add).then_inc(s("x1_ready"), 1)

            pool.wait_ge(s("slots_ready"), 1)
            for m in range(NT * MK):
                i, k = m // MK, m % MK
                if m >= 12:
                    pool.wait_ge(s("onehot_used"), m - 11)
                pool.tensor_scalar(onehot[0:rows(i), m % 12, P:P + NBP], iota64[0:rows(i), 0:NBP],
                                   sblk[0:rows(i), i, k:k + 1], tokid[0:rows(i), i:i + 1],
                                   ALU.is_equal, ALU.mult).then_inc(s("token_ready"), 1)

            pool.wait_ge(s("blocks_planned"), 2)
            pool.wait_ge(s("tab_ready"), 1)
            pool.wait_ge(s("x1_stored"), 16 * NT)
            def gather(u):
                pool.indirect_dma_start(xg[u], None, x1_d,
                                        bass.IndirectOffsetOnAxis(ap=tid[u][:, 0:1], axis=0)
                                        ).then_inc(s(f"xg_loaded{u}"), 16)

            def carry_wait():
                tt(carry[:], ones[0:1, 0:1], ones[0:1, 0:1], ALU.mult).then_inc(s("carried"), 1)

            for m in range(3):
                pool.wait_ge(s("tid_ready"), m + 1)
                if m == 0:
                    carry_wait()
                gather(m % 2)
            last_pair = pool.value_load(npair_i[0:1, 1:2], min_val=NE // 2 - 1, max_val=NBP // 2 - 1)
            with pool.Fori(0, last_pair) as ip:
                for u in range(2):
                    n = ip * 2 + u
                    pool.wait_ge(s("carried"), n + 1)
                    pool.wait_ge(s("tid_ready"), n + 4)
                    carry_wait()
                    gather(1 - u)

            pool.wait_ge(s("slots_done"), 1)
            pool.wait_ge(s("ln2_loaded"), 32)
            for i in range(NT + 1):
                for k in range(MK if i < NT else 0):
                    m = i * MK + k
                    if m >= 8:
                        pool.wait_ge(s("part_used"), m - 7)
                    pool.indirect_dma_start(part[0:rows(i), m % 8, :], None, slots_d,
                                            bass.IndirectOffsetOnAxis(ap=slot_i[0:rows(i), i, k:k + 1], axis=0)
                                            ).then_inc(s(f"part_loaded{m % 8}"), 16)
                if i >= 1:
                    r, y = rows(i - 1), x1[0:rows(i - 1), i - 1, :]
                    pool.wait_ge(s("normed"), NT + i)
                    step(tt(y, y, ln2[0:r, 0, :], ALU.mult))
                    tt(y, y, ln2[0:r, 1, :], ALU.add).then_inc(s("out_ready"), 1)

        @block.scalar
        def _(act):
            def f(dst, src, fn=ACT.Copy, **kw):
                return act.activation(dst, src, fn, **kw)

            def take(key, dst, src, name, fn=ACT.Copy, **kw):
                await_bank(act, key)
                f(dst, src, fn, **kw).then_inc(s(name), 1)

            for i in range(NT):
                for half in range(2):
                    take(("x", i, half), xT[:, 4 * half:4 * half + 4, tok(i)], quad(("x", i, half), rows(i)), "xT_ready")
            take("par", par[:].rearrange("p a b -> p (a b)"), bank("par")[:, 0:80], "par_ready")
            act.wait_ge(s("par_ready"), 1)
            f(sm[:, 0, :], par[:, 4, :], ACT.Exp).then_inc(s("trig_ready"), 1)
            act.wait_ge(s("angle_ready"), 1)
            f(sm[:, 3, :], sm[:, 1, :], ACT.Exp)
            f(sm[:, 4, :], sm[:, 2, :], ACT.Sin)
            f(sm[:, 5, :], sm[:, 2, :], ACT.Sin, scale=0.5).then_inc(s("trig_ready"), 1)
            for t in range(BL):
                if t == 4:
                    take("c", craw.rearrange("p a b c -> p (a b c)"), bank("c"), "c_turned")
                take(("u", t), u2[:, :, t, :], bank(("u", t)).rearrange("p (g c) -> p g c", c=GC), "u2_ready")
            take("u_s", u64[0:DEC, :], bank("u_s")[0:DEC, :], "u64_ready")
            for q4 in range(8):
                take(("ut", q4), uT[:, 4 * q4:4 * q4 + 4, 0:NJ], quad(("ut", q4)), "uT_ready")
            take("uts", uT[:, :, NJ + 1:UC], bank("uts")[:, 0:NG * NJS].rearrange("p (g j) -> p g j", j=NJS),
                 "uT_ready")
            bopT_flat = bopT.rearrange("p a b n -> p (a b) n")
            for q4 in range(8):
                take(("bt", q4), bopT_flat[:, 4 * q4:4 * q4 + 4, :], quad(("bt", q4)), "bopT_ready")
            act.wait_ge(s("constants"), 8)
            for gp in range(GP):
                take(("b", gp), hp[:, 1:1 + UC, :, gp].rearrange("p j a -> p a j"),
                     bank(("b", gp))[:, 0:2 * UC].rearrange("p (a j) -> p a j", a=2), "b_ready")
            for q4 in range(4):
                for e in range(2):
                    b = ("k", q4, e)
                    take(b, kpad[:, 8 * q4 + e:8 * q4 + e + 7:2, 7:15, :].rearrange("p g l o -> p g (l o)"),
                         quad(b)[0:GC], "k_ready")

            def take_zi(i):
                r, z = rows(i), zi[0:rows(i), i % 2, :]
                if i == 0:
                    act.wait_ge(s("kpad_stored"), 16)
                if i >= 2:
                    await_bank(act, ("iqT", i - 2) if i - 2 in CHOOSING else ("ikT", i - 2))
                    act.wait_ge(s(f"ik_stored{i % 2}"), 16 * (i // 2))
                await_bank(act, ("iq", i))
                f(z[:, 0:512], bank(("iq", i))[0:r, :])
                await_bank(act, ("ik", i))
                f(z[:, 512:576], bank(("ik", i))[0:r, 0:64])
                f(iws[0:r, i, :], bank(("ik", i))[0:r, 64:72], scale=8 ** -0.5).then_inc(s("zi_ready"), 1)

            def take_turned(i):
                r = rows(i)
                k0 = i * P if i < NT - 1 else SEQ + PAST
                take(("ikT", i), ikT[:, k0:k0 + r], bank(("ikT", i))[:, 0:r], "ikT_ready")
                if i in CHOOSING:
                    take(("iqT", i), iqT[:, :, (i - 2) * P:(i - 2) * P + r], quad(("iqT", i), r), "iqT_ready")

            def take_scores(i):
                r = rows(i)
                for _, c0, n in score_keys(i):
                    for h in range(NH):
                        m = score_no[i, c0, h]
                        if m >= 4:
                            act.wait_ge(s("rel_used"), m - 3)
                        take(("s", i, c0, h), rel[0:r, m % 4, 0:n], bank(("s", i, c0, h))[0:r, 0:n], "rel_ready",
                             ACT.Relu, scale=HD ** -0.5)

            for i in range(NT):
                take_zi(i)
                if i > 0:
                    take_turned(i - 1)
                if i - 2 in CHOOSING:
                    take_scores(i - 2)
                if i == 7:
                    for q4 in range(4):
                        take(("cik", q4), ikT[:, SEQ + q4 * 512:SEQ + (q4 + 1) * 512], bank(("cik", q4)), "cik_ready")
            take_turned(NT - 1)
            take_scores(NT - 2)
            take_scores(NT - 1)

            for sample in (1, 0):
                r, y = (NJS, y2s) if sample else (NJ, y2)
                for key in [("y", sample, q4, e) for q4 in range(4) for e in range(2)]:
                    take(key, y[0:r].rearrange("p t (q g e c) -> p q e g t c", q=4, g=4, e=2)[:, key[2], key[3]],
                         bank(key)[0:r].rearrange("p (g t c) -> p g t c", g=4, t=BL),
                         "y2s_ready" if sample else "y_ready", ACT.Gelu_apprx_tanh)
            act.wait_ge(s("rel_used"), len(score_no))
            for u in range(2):
                act.wait_ge(s(f"ik_stored{u}"), 16 * (5 - u))
            take("hst", hst[0:16].rearrange("p a n -> p (a n)"), bank("hst")[0:16, :], "states_ready")
            for t in range(BL):
                take(("yt", t), yT[:, :, t:SEQ:BL], quad(("yt", t)), "yT_ready")
            take("yts", yT[:, :, SEQ:T], bank("yts")[:, 0:4 * DEC].rearrange("p (q n) -> p q n", q=4), "yT_ready")

            m = 0
            for d in range(DK):
                for c, (t0, n) in enumerate(TOK_CHUNKS):
                    if m >= 2:
                        act.wait_ge(s("sg_used"), m - 1)
                    for q, key in enumerate(("gs", "glu")):
                        take((key, d, c), sg[:, 2 * (m % 2) + q, 0:n], bank((key, d, c))[:, 0:n], "sg_ready",
                             ACT.Sigmoid)
                    m += 1
                if d == 0:
                    act.wait_ge(s("zeros_ready"), 1)
                b0, nb = CLEARED[d // 2]
                j = slice(d % 2 * 512, d % 2 * 512 + 512)
                act.dma_start(slots_d[(NE + b0) * P:(NE + b0 + nb) * P, j].rearrange("(b p) f -> p b f", p=P),
                              zeros.unsqueeze(1).broadcast_to([P, nb, 512])).then_inc(s("slots_cleared"), 16)

            def take_qkv(i):
                r, z = rows(i), zq[0:rows(i), i % 2, :]
                if i >= 2:
                    await_bank(act, ("qT", i - 2))
                    act.wait_ge(s(f"k_stored{i % 2}"), 16 * (i // 2))
                await_bank(act, ("q", i))
                f(z[:, 0:512], bank(("q", i))[0:r, :])
                await_bank(act, ("kv", i))
                f(z[:, 512:640], bank(("kv", i))[0:r, 0:128])
                f(v_tm[0:r, i if i < NT - 1 else 24, :], bank(("kv", i))[0:r, 128:256]).then_inc(s("zq_ready"), 1)

            def take_qk_turned(i):
                r = rows(i)
                if i == 0:
                    act.wait_ge(s("sg_used"), 3 * DK)
                k0 = i * P if i < NT - 1 else SEQ + PAST
                take(("qT", i), qT[:, :, tok(i)], quad(("qT", i), r), "qT_ready")
                take(("kT", i), kT[:, :, k0:k0 + r], quad(("kT", i), r)[:, 0:2, :], "qT_ready")

            for i in range(NT):
                take_qkv(i)
                if i > 0:
                    take_qk_turned(i - 1)
                    for j in (2 * i - 2, 2 * i - 1):
                        take(("ck", j), kT[:, :, SEQ + j * P:SEQ + (j + 1) * P], quad(("ck", j))[:, 0:2, :],
                             "ckT_ready")
            take_qk_turned(NT - 1)

            def soften(n, e):
                i, _ = ATT[n]
                r, nk = rows(i), keys(i)[1]
                act.wait_ge(s("nbias_ready"), n + 1)
                p = probs_at(n)[0:r, e, 0:nk]
                f(p, p, ACT.Exp, bias=nbias[0:r, n % 2, e:e + 1], scale=HD ** -0.5,
                  accum_out=rsum[0:r, n % 2, e:e + 1]).then_inc(s("probs"), 1)

            def attend(ns):
                for e in range(2):
                    soften(ns[0], e)
                for n, q in group_no:
                    if n in ns:
                        if ns is PROMPT or q < 2:
                            take_turned_probs(act, f, n, q)
                        for e in range(2):
                            if n + 1 in ns and q == (min(e, len(key_groups(ATT[n][0])) - 1) if ns is PROMPT else 1):
                                soften(n + 1, e)

            def gate_attention(steps):
                for d, c in steps:
                    m, n = step_no[d, c], TOK_CHUNKS[c][1]
                    if m >= 4:
                        act.wait_ge(s("mixed_ready"), m - 3)
                    take(("ga", d, c), sga[:, m % 4, 0:n], bank(("ga", d, c))[:, 0:n], "sga_ready", ACT.Sigmoid)

            attend(PROMPT)
            gate_attention(EARLY)
            attend(SAMPLE)
            gate_attention(LATE)

            def norm(i):
                r = rows(i)
                act.wait_ge(s("var_ready"), i + 1)
                f(lst[0:r, 1:2], lst[0:r, 0:1], ACT.Sqrt).then_inc(s("std_ready"), 1)
                act.wait_ge(s("rstd_ready"), i + 1)
                f(x1[0:r, i, :], xre[0:r, i % 2, :], ACT.Identity, bias=lst[0:r, 3:4],
                  scale=lst[0:r, 2:3]).then_inc(s("normed"), 1)

            def after_norm(i):
                r = rows(i)
                if i >= 2:
                    act.wait_ge(s("sel_ready"), i - 1)
                take(("r", i), rsc[0:r, i % 2, :], bank(("r", i))[0:r, 0:NE], "rsc_ready", ACT.Sigmoid)

            for i in range(NT + 2):
                if 0 <= i - 1 < NT:
                    for half in range(2):
                        key = ("x1", i - 1, half)
                        take(key, x1T[:, 4 * half:4 * half + 4, tok(i - 1)], quad(key, rows(i - 1)), "x1T_ready")
                if i < NT:
                    norm(i)
                if 0 <= i - 1 < NT:
                    after_norm(i - 1)
            for i in range(NT + 1):
                if i < NT:
                    await_bank(act, ("sg", i))
                    if i >= 2:
                        await_bank(act, ("ht", i - 2))
                    f(hsh[0:rows(i), i % 2, :], bank(("sg", i))[0:rows(i), 0:DE], ACT.Silu
                      ).then_inc(s("silu_ready"), 1)
                if i > 0:
                    r = rows(i - 1)
                    take(("ht", i - 1), hshT[:, (i - 1) % 2, :].rearrange("p (k n) -> p k n", k=2)[:, :, 0:r],
                         quad(("ht", i - 1), r)[:, 0:2, :], "hshT_ready")

            act.wait_ge(s("blocks_planned"), 2)
            last_pair = act.value_load(npair_i[0:1, 1:2], min_val=NE // 2 - 1, max_val=NBP // 2 - 1)

            def half_rows(u, blocks):
                act.wait_ge(s("xg_turned0"), blocks)
                f(xgT[u][:, 0:4, :], psum[:, 0, :].rearrange("p (q n) -> p q n", q=4)).then_inc(s("xgT_ready"), 1)

            def silu(u, blocks):
                act.wait_ge(s("egu_full"), blocks)
                f(eh[:, u, :], psum[:, 2, 0:DE], ACT.Silu).then_inc(s("esilu_ready"), 1)

            def take_eh(u, blocks):
                act.wait_ge(s("eh_turned"), blocks)
                f(ehT[u], psum[:, 3, 0:2 * P].rearrange("p (k n) -> p k n", k=2)).then_inc(s("ehT_ready"), 1)

            def half_y(u, blocks):
                act.wait_ge(s("gcol_ready"), blocks)
                act.wait_ge(s("edn_full0"), blocks)
                f(yb[u][:, 0:512], psum[:, 4 + 2 * u, :], ACT.Copy,
                  scale=gcol[:, u:u + 1]).then_inc(s("y_half"), 1)

            def store_y(u, n):
                act.wait_ge(s("y_half"), (n + 1) * 2)
                act.dma_start(slots_d[bass.ds(n * P, P), :], yb[u]).then_inc(s(f"y_stored{u}"), 16)

            act.wait_ge(s("tab_ready"), 1)
            for u in range(2):
                act.dma_start(slots_d[(NBP - 1) * P:NBP * P, u * P:(u + 1) * P], ident[:]
                              ).then_inc(s(f"y_stored{u}"), 16)
            half_rows(0, 1)
            silu(0, 1)
            half_rows(1, 2)
            take_eh(0, 1)
            with act.Fori(0, last_pair) as ip:
                for u in range(2):
                    n = ip * 2 + u
                    silu(1 - u, n + 2)
                    half_rows(u, n + 3)
                    half_y(u, n + 1)
                    take_eh(1 - u, n + 2)
                    store_y(u, n)
            silu(1, last_pair * 2 + 2)
            half_y(0, last_pair * 2 + 1)
            take_eh(1, last_pair * 2 + 2)
            store_y(0, last_pair * 2)
            half_y(1, last_pair * 2 + 2)
            store_y(1, last_pair * 2 + 1)

            for i in range(NT):
                r = rows(i)
                act.wait_ge(s("var_ready"), NT + i + 1)
                f(lst[0:r, 1:2], lst[0:r, 0:1], ACT.Sqrt).then_inc(s("std_ready"), 1)
                act.wait_ge(s("rstd_ready"), NT + i + 1)
                f(x1[0:r, i, :], x1[0:r, i, :], ACT.Identity, bias=lst[0:r, 3:4],
                  scale=lst[0:r, 2:3]).then_inc(s("normed"), 1)

        @block.vector
        def _(dve):
            steps = [0]

            def step(ins):
                steps[0] += 1
                ins.then_inc(dve_step, 1)
                dve.wait_ge(dve_step, steps[0])

            tt, ts, stt = dve.tensor_tensor, dve.tensor_scalar, dve.scalar_tensor_tensor

            dve.wait_ge(s("params_loaded"), 16 * 5)
            dve.tensor_copy(pst[64:80, :].rearrange("q (e n) -> q e n", e=2),
                            ldt[64:80, :].unsqueeze(2).broadcast_to([GP, 2, NS])).then_inc(s("param_rows"), 1)
            ar, ai = par[:, 0, :], par[:, 1, :]
            dve.wait_ge(s("par_ready"), 1)
            dve.wait_ge(s("trig_ready"), 1)
            tt(sm[:, 1, :], sm[:, 0, :], ar, ALU.mult)
            step(tt(sm[:, 6, :], sm[:, 0, :], ai, ALU.mult))
            step(ts(sm[:, 7, :], sm[:, 6, :], 1.0 / TWO_PI, ROUND, ALU.mult, ALU.add))
            step(ts(sm[:, 7, :], sm[:, 7, :], ROUND, None, ALU.subtract))
            step(stt(sm[:, 8, :], sm[:, 7, :], -6.28125, sm[:, 6, :], ALU.mult, ALU.add))
            step(stt(sm[:, 8, :], sm[:, 7, :], -0.0019350051879882812, sm[:, 8, :], ALU.mult, ALU.add))
            step(stt(sm[:, 8, :], sm[:, 7, :], -(TWO_PI - 6.28125 - 0.0019350051879882812), sm[:, 8, :],
                     ALU.mult, ALU.add))
            ts(sm[:, 2, :], sm[:, 8, :], 3.1415925, -3.1415925, ALU.min, ALU.max).then_inc(s("angle_ready"), 1)
            tt(sm[:, 9, :], ar, ar, ALU.mult)
            step(tt(sm[:, 10, :], ai, ai, ALU.mult))
            step(tt(sm[:, 9, :], sm[:, 9, :], sm[:, 10, :], ALU.add))
            step(dve.reciprocal(sm[:, 10, :], sm[:, 9, :]))
            dve.memset(pw[:, 0, 0, :], 1.0)
            dve.memset(pw[:, 1, 0, :], 0.0)
            dve.wait_ge(s("trig_ready"), 2)
            step(tt(sm[:, 11, :], sm[:, 5, :], sm[:, 5, :], ALU.mult))
            step(ts(sm[:, 11, :], sm[:, 11, :], -2.0, 1.0, ALU.mult, ALU.add))
            tt(pw[:, 0, 1, :], sm[:, 3, :], sm[:, 11, :], ALU.mult)
            step(tt(pw[:, 1, 1, :], sm[:, 3, :], sm[:, 4, :], ALU.mult))
            step(ts(sm[:, 12, :], pw[:, 0, 1, :], -1.0, None, ALU.add))
            tt(sm[:, 13, :], sm[:, 12, :], ar, ALU.mult)
            tt(sm[:, 14, :], pw[:, 1, 1, :], ai, ALU.mult)
            tt(sm[:, 15, :], pw[:, 1, 1, :], ar, ALU.mult)
            step(tt(sm[:, 6, :], sm[:, 12, :], ai, ALU.mult))
            tt(sm[:, 13, :], sm[:, 13, :], sm[:, 14, :], ALU.add)
            step(tt(sm[:, 15, :], sm[:, 15, :], sm[:, 6, :], ALU.subtract))
            tt(sm[:, 13, :], sm[:, 13, :], sm[:, 10, :], ALU.mult)
            step(tt(sm[:, 14, :], sm[:, 15, :], sm[:, 10, :], ALU.mult))
            for n in (1, 2, 4):
                xr, xi = pw[:, 0, 1:n + 1, :], pw[:, 1, 1:n + 1, :]
                wr, wi = (pw[:, q, n:n + 1, :].broadcast_to([P, n, GP]) for q in range(2))
                q = [v[:, 0:n * GP].rearrange("p (n g) -> p n g", n=n)
                     for v in (t1, t2, t1[:, 1024:2048], t2[:, 1024:2048])]
                tt(q[0], xr, wr, ALU.mult)
                tt(q[1], xi, wi, ALU.mult)
                tt(q[2], xr, wi, ALU.mult)
                step(tt(q[3], xi, wr, ALU.mult))
                tt(pw[:, 0, n + 1:2 * n + 1, :], q[0], q[1], ALU.subtract)
                step(tt(pw[:, 1, n + 1:2 * n + 1, :], q[2], q[3], ALU.add))
            dve.tensor_copy(a8[:, 0, 0, :], pw[:, 0, 8, :])
            dve.tensor_copy(a8[:, 1, 1, :], pw[:, 0, 8, :])
            dve.tensor_copy(a8[:, 1, 0, :], pw[:, 1, 8, :])
            ts(a8[:, 0, 1, :], pw[:, 1, 8, :], -1.0, None, ALU.mult).then_inc(s("s5_operators"), 1)
            dve.wait_ge(s("b_loaded"), 32)
            cr, ci = (sm[:, q, :].unsqueeze(2).broadcast_to([P, GP, GC]) for q in (13, 14))
            q = [v[:, o:o + 256].rearrange("p (g c) -> p g c", c=GC) for v in (t1, t2) for o in (0, 256)]
            tt(q[0], cr, braw[:, 0, :, :], ALU.mult)
            tt(q[1], ci, braw[:, 1, :, :], ALU.mult)
            tt(q[2], cr, braw[:, 1, :, :], ALU.mult)
            step(tt(q[3], ci, braw[:, 0, :, :], ALU.mult))
            tt(bbar[:, 0, :, :], q[0], q[1], ALU.subtract)
            step(tt(bbar[:, 1, :, :], q[2], q[3], ALU.add))
            for part_ in range(2):
                for t in range(BL):
                    w = [pw[:, q_, 7 - t, :].unsqueeze(2).broadcast_to([P, GP, GC]) for q_ in range(2)]
                    o = slice(t * 256, (t + 1) * 256)
                    tt(t1[:, o].rearrange("p (g c) -> p g c", c=GC), w[0], bbar[:, part_, :, :], ALU.mult)
                    last = tt(t2[:, o].rearrange("p (g c) -> p g c", c=GC), w[1], bbar[:, 1 - part_, :, :], ALU.mult)
                step(last)
                v = [x[:, 0:2048].rearrange("p (t g c) -> p g t c", t=BL, g=GP) for x in (t1, t2)]
                step(tt(ba[:, part_, :, :, :], v[0], v[1], ALU.add if part_ else ALU.subtract))
            dve.memset(slot[:], 0.0).then_inc(s("s5_operators"), 1)
            dve.wait_ge(s("c_turned"), 1)
            w = [pw[:, q_, :, :].rearrange("p k g -> p g k").unsqueeze(3).broadcast_to([P, GP, 9, GC])
                 for q_ in range(2)]
            c_ = [craw[:, q_, :, :].unsqueeze(2).broadcast_to([P, GP, 9, GC]) for q_ in range(2)]
            v = [x.rearrange("p (g k c) -> p g k c", g=GP, k=9) for x in (t1, t2)]
            tt(v[0], w[0], c_[0], ALU.mult)
            step(tt(v[1], w[1], c_[1], ALU.mult))
            step(tt(ca[:, 0, :, :, :], v[0], v[1], ALU.subtract))
            tt(v[0], w[0], c_[1], ALU.mult)
            step(tt(v[1], w[1], c_[0], ALU.mult))
            step(stt(ca[:, 1, :, :, :].rearrange("p g k c -> p (g k c)"), t1, -1.0, t2, ALU.mult, ALU.subtract))
            dve.memset(cum[:], 0.0).then_inc(s("s5_operators"), 1)
            await_bank(dve, ("b", GP - 1))
            dve.memset(kpad[:, :, 0:7, :], 0.0)
            dve.wait_ge(s("d_loaded"), 16)
            dve.wait_ge(s("constants"), 8)
            skip = t1[0:GC, 0:512].rearrange("c (g o) -> c g o", o=GC)
            step(tt(skip, ident[0:GC, 0:GC].unsqueeze(1).broadcast_to([GC, NG, GC]),
                    dsk[:].unsqueeze(2).broadcast_to([GC, NG, GC]), ALU.mult))
            dve.wait_ge(s("k_ready"), 8)
            tt(kpad[:, :, 7, :], kpad[:, :, 7, :], skip, ALU.add).then_inc(s("s5_operators"), 1)

            dve.wait_ge(s("s5_operators"), 4)
            step(dve.memset(mk[:, 0:MASK_AT[2]], 0.0))
            for i in range(2):
                e = MASK_AT[i] + keys(i)[1]
                step(dve.memset(mk[0:64, e - 64:e], HID))
            mask_step = {0: steps[0], 1: steps[0]}

            def add_scores(i):
                r = rows(i)
                for _, c0, n in score_keys(i):
                    o = mk[0:r, MASK_AT[i] + c0:MASK_AT[i] + c0 + n]
                    for h in range(NH):
                        m = score_no[i, c0, h]
                        w, x = iws[0:r, i, h:h + 1], rel[0:r, m % 4, 0:n]
                        dve.wait_ge(s("rel_ready"), m + 1)
                        if h == 0:
                            ins = ts(o, x, w, None, ALU.mult)
                        else:
                            dve.wait_ge(s("rel_used"), m)
                            ins = stt(o, x, w, o, ALU.mult, ALU.add)
                        ins.then_inc(s("rel_used"), 1)
                    if 2 < i < 7:
                        choose(0.8)
                dve.wait_ge(s("rel_used"), m + 1)
                if i < NT - 1:
                    e = MASK_AT[i] + keys(i)[1]
                    step(dve.memset(mk[0:64, e - 64:e], HID))

            at_round, owed = [0], [0.0]

            def choose(us):
                owed[0] += us
                while owed[0] > 0 and at_round[0] < len(CHOOSING) * TOPK // 8:
                    i, r_ = CHOOSING[at_round[0] // (TOPK // 8)], at_round[0] % (TOPK // 8)
                    r, n = rows(i), keys(i)[1]
                    sc = mk[0:r, MASK_AT[i]:MASK_AT[i] + n]
                    step(dve.max(best[0:r, :], sc))
                    step(dve.match_replace(sc, best[0:r, :], sc, TAKEN))
                    if r_ == TOPK // 8 - 1:
                        step(ts(sc, sc, TAKEN / 2, HID, ALU.is_gt, ALU.mult))
                        mask_step[i] = steps[0]
                    at_round[0] += 1
                    owed[0] -= 2 * (n / 960 + 0.07)

            CHOOSE_AFTER_SCORES, CHOOSE_GLU, CHOOSE_QKV, CHOOSE_GATES = 55, 8.6, 84, 7.3
            CHOOSE_ATTENTION = {5: 1, 6: 2.3, 7: 3.5}
            for i in CHOOSING:
                if i == NT - 1:
                    await_bank(dve, ("cik", 3))
                    dve.memset(zeros, 0.0).then_inc(s("zeros_ready"), 1)
                add_scores(i)
            choose(CHOOSE_AFTER_SCORES)

            m = 0
            for d in range(DK):
                for c, (t0, n) in enumerate(TOK_CHUNKS):
                    dve.wait_ge(s("sg_ready"), 2 * m + 2)
                    await_bank(dve, ("val", d, c))
                    v_ = sg[:, 2 * (m % 2), 0:n]
                    tt(v_, bank(("val", d, c))[:, 0:n], v_, ALU.mult).then_inc(s("val_used"), 1)
                    choose(CHOOSE_GLU if m < 3 * DK - 2 else 0)
                    m += 1
            choose(CHOOSE_QKV)

            maskings = [0]

            def mask(n):
                i, _ = ATT[n]
                r, p = rows(i), probs_at(n)
                dve.wait_ge(dve_step, mask_step[i])
                chunks = split(keys(i)[1], 512)
                for q, (c0, w) in enumerate(chunks):
                    for e in range(2):
                        key = ("l", n, c0, e)
                        await_bank(dve, key)
                        dve.tensor_tensor_reduce(out=p[0:r, e, c0:c0 + w], in0=bank(key)[0:r, 0:w],
                                                 in1=mk[0:r, MASK_AT[i] + c0:MASK_AT[i] + c0 + w], scale=1.0,
                                                 scalar=TAKEN, op0=ALU.add, op1=ALU.max,
                                                 accum_out=mx[0:r, n % 2, e, q:q + 1]).then_inc(s("masked"), 1)
                        maskings[0] += 1
                dve.wait_ge(s("masked"), maskings[0])
                top = mx[0:r, n % 2, :, 0]
                if len(chunks) > 1:
                    top = mx1[0:r, :]
                    step(dve.reduce_max(top, mx[0:r, n % 2, :, 0:len(chunks)], AX.X))
                ts(nbias[0:r, n % 2, :], top, -HD ** -0.5, None, ALU.mult).then_inc(s("nbias_ready"), 1)

            def take_values(m):
                i, hp_ = ATT[2 * m]
                if m == 0:
                    dve.wait_ge(s("slots_cleared"), 16 * DK)
                    dve.wait_ge(s("h_stored"), 64)
                    dve.wait_ge(s("k_stored0"), 16 * 5)
                    dve.wait_ge(s("k_stored1"), 16 * 4)
                await_bank(dve, ("o", m))
                v, o = quad(("o", m), rows(i)), aT[:, hp_:hp_ + 2, tok(i)]
                step(dve.tensor_copy(o, v[:, 2:4, :]))
                tt(o, v[:, 0:2, :], o, ALU.mult).then_inc(s("aT_ready"), 1)

            def attend(ns):
                mask(ns[0])
                mask(ns[1])
                for n in ns:
                    r = rows(ATT[n][0])
                    dve.wait_ge(s("probs"), 2 * n + 2)
                    dve.reciprocal(rinv[0:r, n % 4, :], rsum[0:r, n % 2, :]).then_inc(s("rinv_ready"), 1)
                    if n % 2 and n - 3 >= ns[0]:
                        take_values((n - 3) // 2)
                    if n + 2 in ns:
                        mask(n + 2)
                    if CHOOSE_ATTENTION.get(ATT[n][0]):
                        choose(CHOOSE_ATTENTION[ATT[n][0]])
                take_values(ns[-1] // 2)

            def attend_sample():
                mask(SAMPLE[0])
                for n in SAMPLE:
                    r = rows(NT - 1)
                    if n + 1 in SAMPLE:
                        mask(n + 1)
                    dve.wait_ge(s("probs"), 2 * n + 2)
                    dve.reciprocal(rinv[0:r, n % 4, :], rsum[0:r, n % 2, :]).then_inc(s("rinv_ready"), 1)
                    for q in range(2, len(key_groups(NT - 1))):
                        take_turned_probs(dve, dve.tensor_copy, n, q)
                for m in (-2, -1):
                    take_values(len(ATT) // 2 + m)

            def gate_attention(steps):
                for d, c in steps:
                    m, n = step_no[d, c], TOK_CHUNKS[c][1]
                    dve.wait_ge(s("sga_ready"), m + 1)
                    await_bank(dve, ("ao", d, c))
                    v_ = sga[:, m % 4, 0:n]
                    tt(v_, bank(("ao", d, c))[:, 0:n], v_, ALU.mult).then_inc(s("ao_used"), 1)
                    if c < 2:
                        choose(CHOOSE_GATES)

            attend(PROMPT)
            gate_attention(EARLY)
            choose(1e9)
            dve.wait_ge(s("mixed_ready"), len(EARLY))
            attend_sample()
            gate_attention(LATE)

            def statistics(x, r, n):
                if n > 0:
                    dve.wait_ge(s("normed"), n)
                for q_ in range(2):
                    last = dve.bn_stats(stats[0:r, q_, :], x[:, q_ * 512:(q_ + 1) * 512])
                step(last)
                step(dve.bn_aggr(mv[0:r, :], stats[0:r, :, :].rearrange("p a b -> p (a b)")))
                ts(lst[0:r, 0:1], mv[0:r, 1:2], EPS, None, ALU.add).then_inc(s("var_ready"), 1)
                dve.wait_ge(s("std_ready"), n + 1)
                step(dve.reciprocal(lst[0:r, 2:3], lst[0:r, 1:2]))
                stt(lst[0:r, 3:4], mv[0:r, 0:1], -1.0, lst[0:r, 2:3], ALU.mult,
                    ALU.mult).then_inc(s("rstd_ready"), 1)

            def residual(i):
                r = rows(i)
                dve.wait_ge(s(f"xre_loaded{i % 2}"), 16 * (i // 2 + 1))
                f0 = banks.at[("wo", i)][0]
                for j in range(2):
                    await_bank(dve, ("wo", i), j)
                x = xre[0:r, i % 2, :]
                stt(x, x, ALPHA, psum[0:r, f0:f0 + 2, :].rearrange("p b n -> p (b n)"), ALU.mult,
                    ALU.add).then_inc(s("res_ready"), 1)
                dve.wait_ge(s("res_ready"), i + 1)
                statistics(x, r, i)

            def expert_match(i):
                r = rows(i)
                step(tt(oh[0:r], iota64[0:r, 0:NE].unsqueeze(1).broadcast_to([r, MK, NE]),
                        idx[0:r, i, 0:MK].unsqueeze(2).broadcast_to([r, MK, NE]), ALU.is_equal))

            def route(i):
                r = rows(i)
                sc = rsc[0:r, i % 2, :]
                dve.wait_ge(s("rsc_ready"), i + 1)
                if i == 0:
                    dve.wait_ge(s("w_s_loaded"), 64)
                biased = sb64[0:r, :]
                step(tt(biased, sc, rbias[0:r, :], ALU.add))
                step(dve.max(v8[0:r, :], biased))
                step(dve.max_index(i8[0:r, :], v8[0:r, :], biased))
                step(dve.tensor_copy(idx[0:r, i, :], i8[0:r, :]))
                expert_match(i)
                step(tt(oh2[0:r], oh[0:r], sc.unsqueeze(1).broadcast_to([r, MK, NE]), ALU.mult))
                g = gate[0:r, i, 0:MK]
                step(dve.reduce_sum(g, oh2[0:r], AX.X))
                step(dve.reduce_sum(gsum[0:r, 0:1], g, AX.X))
                step(dve.reciprocal(gsum[0:r, 1:2], gsum[0:r, 0:1]))
                ts(g, g, gsum[0:r, 1:2], ROUTED_SCALE, ALU.mult, ALU.mult)
                dve.reduce_sum(sel[0:r, i % 2, :], oh[0:r].rearrange("p k e -> p e k"),
                               AX.X).then_inc(s("sel_ready"), 1)

            def gate_shared(i):
                r = rows(i)
                dve.wait_ge(s("silu_ready"), i + 1)
                await_bank(dve, ("sg", i))
                h = hsh[0:r, i % 2, :]
                tt(h, h, bank(("sg", i))[0:r, DE:2 * DE], ALU.mult).then_inc(s("hsh_ready"), 1)

            def count(i):
                r = rows(i)
                await_bank(dve, ("rk", i))
                dve.tensor_copy(rk[0:r, i, :], bank(("rk", i))[0:r, 0:NE]).then_inc(s("rk_ready"), 1)
                dve.wait_ge(s("sel_ready"), i + 1)
                if i > 0:
                    dve.wait_ge(s("cum_ready"), i)
                tt(cum[0:r, :], cum[0:r, :], sel[0:r, i % 2, :], ALU.add).then_inc(s("cum_ready"), 1)

            def add_shared(i):
                r = rows(i)
                f0 = banks.at[("sd", i)][0]
                for j in range(2):
                    await_bank(dve, ("sd", i), j)
                x = x1[0:r, i, :]
                stt(x, x, ALPHA, psum[0:r, f0:f0 + 2, :].rearrange("p b n -> p (b n)"), ALU.mult,
                    ALU.add).then_inc(s("base_ready"), 1)

            for i in range(NT + 2):
                if i < NT:
                    residual(i)
                if 0 <= i - 2 < NT:
                    count(i - 2)
                if 0 <= i - 1 < NT:
                    route(i - 1)

            await_bank(dve, "cnt")
            cn, nb_, bend, base_ = (cnt[:, q_, :] for q_ in range(4))
            dve.tensor_copy(cn, bank("cnt")[:, 0:NE]).then_inc(s("blocks_planned"), 1)
            dve.wait_ge(s("blocks_planned"), 1)
            step(ts(nb_, cn, 63.5, 1.0 / P, ALU.add, ALU.mult))
            step(ts(nb_, nb_, ROUND, None, ALU.add))
            step(ts(nb_, nb_, -ROUND, 1.0, ALU.add, ALU.max))
            step(dve.tensor_tensor_scan(bend, ones[:, 0:NE], nb_, 0.0, ALU.mult, ALU.add))
            step(tt(base_, bend, nb_, ALU.subtract))
            step(ts(base_, base_, float(P), None, ALU.mult))
            step(ts(npair[0:1, 0:1], bend[0:1, NE - 1:NE], 0.5, 0.5, ALU.add, ALU.mult))
            step(ts(npair[0:1, 1:2], npair[0:1, 0:1], ROUND, None, ALU.add))
            ts(npair_i[0:1, 0:1], npair[0:1, 1:2], -ROUND, None, ALU.add)
            ts(npair_i[0:1, 1:2], npair[0:1, 1:2], -ROUND, -1.0, ALU.add, ALU.add).then_inc(s("blocks_planned"), 1)
            step(ts(oh[:, 0, :], bend, bexp[:, 0:1], None, ALU.is_le))
            step(dve.reduce_sum(bexp[:, 1:2], oh[:, 0, :], AX.X))
            ts(bexp_i[:], bexp[:, 1:2], float(NE - 1), None, ALU.min).then_inc(s("blocks_planned"), 1)

            def slots(i):
                r = rows(i)
                step(tt(rk[0:r, i, :], rk[0:r, i, :], base_[0:r, :], ALU.add))
                expert_match(i)
                step(tt(oh2[0:r], oh[0:r], rk[0:r, i, :].unsqueeze(1).broadcast_to([r, MK, NE]), ALU.mult))
                step(dve.reduce_sum(slot[0:r, i, 0:MK], oh2[0:r], AX.X))

            def block_and_place():
                dve.tensor_copy(slot_i[:], slot[:])
                step(ts(sblk[:], slot[:], -63.5, 1.0 / P, ALU.add, ALU.mult))
                step(ts(sblk[:], sblk[:], ROUND, None, ALU.add))
                step(ts(sblk[:], sblk[:], -ROUND, None, ALU.add))
                stt(sin_[:], sblk[:], -float(P), slot[:], ALU.mult, ALU.add).then_inc(s("slots_ready"), 1)
                dve.wait_ge(s("slots_ready"), 1)

            def list_rows(u, column):
                ts(tid[u][:], column, 1.0, None, ALU.mult).then_inc(s("tid_ready"), 1)

            dve.wait_ge(s("x1_stored"), 16 * NT)
            for i in range(NT + 1):
                if i < NT:
                    gate_shared(i)
                if i == NT - 1:
                    await_bank(dve, "tab")
                    dve.tensor_copy(tab[:].rearrange("p a b -> p (a b)"), bank("tab")[:, 0:2 * NBP]
                                    ).then_inc(s("tab_ready"), 1)
                    dve.wait_ge(s("tab_ready"), 1)
                    list_rows(0, tab[:, 0, 0:1])
                    list_rows(1, tab[:, 0, 1:2])
                if i > 0:
                    add_shared(i - 1)
                if i < 3:
                    for j in range(3 * i, 3 * i + 3):
                        slots(j)
                if i == 2:
                    block_and_place()
                for m in planned_in(i):
                    r, k = rows(m // MK), m % MK
                    if m >= 12:
                        dve.wait_ge(s("onehot_used"), m - 11)
                    o = onehot[0:r, m % 12, :]
                    ts(o[:, 0:P], iota64[0:r, :], sin_[0:r, m // MK, k:k + 1], None, ALU.is_equal)
                    ts(o[:, P + NBP:], iota64[0:r, 0:NBP], sblk[0:r, m // MK, k:k + 1],
                       gate[0:r, m // MK, k:k + 1], ALU.is_equal, ALU.mult).then_inc(s("onehot_ready"), 1)
            dve.wait_ge(s("base_ready"), NT)

            last_pair = dve.value_load(npair_i[0:1, 1:2], min_val=NE // 2 - 1, max_val=NBP // 2 - 1)

            def half_rows(u, blocks):
                dve.wait_ge(s("xg_turned1"), blocks)
                dve.tensor_copy(xgT[u][:, 4:8, :], psum[:, 1, :].rearrange("p (q n) -> p q n", q=4)
                                ).then_inc(s("xgT_ready"), 1)

            def gate_up(u, blocks):
                dve.wait_ge(s("esilu_ready"), blocks)
                tt(eh[:, 2 + u, :], eh[:, u, :], psum[:, 2, DE:2 * DE], ALU.mult).then_inc(s("eh_ready"), 1)

            def half_y(u, n, blocks, stores):
                dve.wait_ge(s(f"y_stored{u}"), stores)
                ts(gcol[:, u:u + 1], tab[:, 1, bass.ds(n, 1)], 1.0, None, ALU.mult).then_inc(s("gcol_ready"), 1)
                dve.wait_ge(s("gcol_ready"), blocks)
                dve.wait_ge(s("edn_full1"), blocks)
                ts(yb[u][:, 512:1024], psum[:, 5 + 2 * u, :], gcol[:, u:u + 1], None,
                   ALU.mult).then_inc(s("y_half"), 1)

            half_rows(0, 1)
            list_rows(0, tab[:, 0, 2:3])
            gate_up(0, 1)
            half_rows(1, 2)
            with dve.Fori(0, last_pair) as ip:
                for u in range(2):
                    n = ip * 2 + u
                    list_rows(1 - u, tab[:, 0, bass.ds(n + 3, 1)])
                    gate_up(1 - u, n + 2)
                    half_rows(u, n + 3)
                    half_y(u, n, n + 1, ip * 16 + 16)
            gate_up(1, last_pair * 2 + 2)
            half_y(0, last_pair * 2, last_pair * 2 + 1, last_pair * 16 + 16)
            half_y(1, last_pair * 2 + 1, last_pair * 2 + 2, last_pair * 16 + 16)

            for i in range(NT):
                r = rows(i)
                x = x1[0:r, i, :]
                for k in range(MK):
                    m = i * MK + k
                    dve.wait_ge(s(f"part_loaded{m % 8}"), 16 * (m // 8 + 1))
                    tt(x, x, part[0:r, m % 8, :], ALU.add).then_inc(s("part_used"), 1)
                    dve.wait_ge(s("part_used"), m + 1)
                statistics(x, r, NT + i)


_INS = ["x_prompt", "x_sample", "cache_k", "cache_v", "cache_idx_k", "state_ssm_re", "state_ssm_im",
        "w_in", "ssm_a_re", "ssm_a_im", "ssm_log_dt", "ssm_b_re", "ssm_b_im", "ssm_c_re", "ssm_c_im", "ssm_d",
        "w_glu", "w_attn_proj", "w_out", "ln1_g", "ln1_b", "w_router", "router_bias",
        "w_exp_gu", "w_exp_down", "w_sh_gu", "w_sh_down", "ln2_g", "ln2_b"]
_OUTS = [("y_p", (1, SEQ, DM)), ("y_s", (1, DEC, DM)),
         ("k_p", (1, 1, SEQ, NKV, HD)), ("v_p", (1, 1, SEQ, NKV, HD)), ("ik_p", (1, 1, SEQ, HD)),
         ("hre_p", (1, 1, NG, NS)), ("him_p", (1, 1, NG, NS)),
         ("k_s", (1, 1, DEC, NKV, HD)), ("v_s", (1, 1, DEC, NKV, HD)), ("ik_s", (1, 1, DEC, HD)),
         ("hre_s", (1, 1, NG, NS)), ("him_s", (1, 1, NG, NS))]


def rope_table():
    pos = np.zeros(NT * P, np.float32)
    pos[:SEQ] = np.arange(SEQ)
    pos[SEQ:T] = PAST + np.arange(DEC)
    inv = np.float32(500000.0) ** (-np.arange(8, dtype=np.float32) * np.float32(2.0) / np.float32(16.0))
    ang = (pos[:, None] * inv.astype(np.float32)).astype(np.float32)
    return np.stack([np.cos(ang), np.sin(ang)], axis=1).astype(np.float32)


def kernel(**inputs):
    import concourse.bacc as _bacc
    from concourse.bass_utils import run_bass_kernel_spmd as _run

    nc = _bacc.Bacc("TRN2", target_bir_lowering=False, num_devices=1)
    arrays, a, out = {}, {}, {}
    for name in _INS:
        x = np.ascontiguousarray(inputs[name])
        arrays[f"in_{name}"] = x
        a[name] = nc.dram_tensor(f"in_{name}", x.shape, F32, kind="ExternalInput").ap()
    arrays["in_rope_table"] = rope_table()
    a["rope_table"] = nc.dram_tensor("in_rope_table", arrays["in_rope_table"].shape, F32, kind="ExternalInput").ap()
    for name, shape in _OUTS:
        out[name] = nc.dram_tensor(f"out_{name}", shape, F32, kind="ExternalOutput").ap()
    layer_program(nc, a, out)
    r = _run(nc, [arrays], core_ids=[0])
    return tuple(r.results[0][f"out_{name}"] for name, _ in _OUTS)
```
